# Optimizing a Trainium2 kernel written in Bass

```python
import jax, jax.numpy as jnp
from jax import lax
import numpy as np

D_MODEL = 1024
BATCH = 1
SEQ = 256
DEPTH = 1
DEC_BATCH = 1
DEC_SEQ = 1024
PAST_LEN = 512

GRID_W = 64
HEAD_DIM = 64
GLA_HEADS = 8
GLA_DK = 64
GLA_DV = 64
GLA_WIDTH = GLA_HEADS * GLA_DV
GATE_RANK = 16
GATE_TEMP = 16.0
GLA_CHUNK = 64
SWA_HEADS = 8
SWA_KV_HEADS = 2
SWA_GROUP = SWA_HEADS // SWA_KV_HEADS
SWA_WIDTH = SWA_HEADS * HEAD_DIM
WINDOW = 128
BLOCK = 128
MIX_WIDTH = GLA_WIDTH + SWA_WIDTH
D_FF = 4 * D_MODEL
ROPE_THETA = 10000.0
ROPE_AXIS_DIM = HEAD_DIM // 2
EPS = 1e-6
NEG_INF = -1e30
SPLIT_SIZES = (GLA_HEADS * GLA_DK, GLA_HEADS * GLA_DK, GLA_WIDTH, GLA_WIDTH, 2 * GATE_RANK,
               SWA_WIDTH, SWA_KV_HEADS * HEAD_DIM, SWA_KV_HEADS * HEAD_DIM)
D_IN = 2 * GLA_HEADS * GLA_DK + 2 * GLA_WIDTH + 2 * GATE_RANK + SWA_WIDTH + 2 * SWA_KV_HEADS * HEAD_DIM

kernel_name = "hybrid_gla_swa_prefix_diffusion_step"

def rmsnorm(x, gain):
    xf = x.astype(jnp.float32)
    xf = xf * lax.rsqrt(jnp.mean(xf * xf, axis=-1, keepdims=True) + EPS)
    return xf.astype(x.dtype) * gain

def modulation(cond, w_ada, b_ada):
    m = jax.nn.silu(cond) @ w_ada + b_ada
    return jnp.split(m[:, None, :], 6, axis=-1)

def adaln(x, gain, shift, scale):
    return rmsnorm(x, gain) * (1.0 + scale) + shift

def axial_rope(T):
    rows = T // GRID_W
    t = jnp.arange(rows * GRID_W)
    row = (t // GRID_W).astype(jnp.float32)
    col = (t % GRID_W).astype(jnp.float32)
    half = ROPE_AXIS_DIM // 2
    freqs = ROPE_THETA ** (-jnp.arange(half, dtype=jnp.float32) / half)
    ang_r = row[:, None] * freqs[None, :]
    ang_c = col[:, None] * freqs[None, :]
    return (jnp.cos(ang_r), jnp.sin(ang_r), jnp.cos(ang_c), jnp.sin(ang_c))

def _rotate(x, cos, sin):
    x1, x2 = jnp.split(x, 2, axis=-1)
    return jnp.concatenate([x1 * cos - x2 * sin, x2 * cos + x1 * sin], axis=-1)

def apply_rope(x, rope):
    cos_r, sin_r, cos_c, sin_c = rope
    xr, xc = x[..., :ROPE_AXIS_DIM], x[..., ROPE_AXIS_DIM:]
    out = jnp.concatenate([_rotate(xr, cos_r, sin_r), _rotate(xc, cos_c, sin_c)], axis=-1)
    return out.astype(x.dtype)

def project(h, w_in, w_gk_f, b_gk_f, w_gk_b, b_gk_b, q_norm, k_norm):
    B, T, _ = h.shape
    idx, acc = [], 0
    for s in SPLIT_SIZES[:-1]:
        acc += s
        idx.append(acc)
    gq, gk, gv, gg, glr, sq, sk, sv = jnp.split(h @ w_in, idx, axis=-1)

    def heads(t, n):
        return t.reshape(B, T, n, -1).transpose(0, 2, 1, 3)

    gq = heads(gq, GLA_HEADS) * (GLA_DK ** -0.5)
    gk = heads(gk, GLA_HEADS)
    gv = heads(gv, GLA_HEADS)
    lr_f, lr_b = jnp.split(glr, 2, axis=-1)
    g_f = heads(jax.nn.log_sigmoid(lr_f @ w_gk_f + b_gk_f) / GATE_TEMP, GLA_HEADS)
    g_b = heads(jax.nn.log_sigmoid(lr_b @ w_gk_b + b_gk_b) / GATE_TEMP, GLA_HEADS)
    sq = rmsnorm(heads(sq, SWA_HEADS), q_norm).reshape(B, SWA_KV_HEADS, SWA_GROUP, T, HEAD_DIM)
    sk = rmsnorm(heads(sk, SWA_KV_HEADS), k_norm)
    sv = heads(sv, SWA_KV_HEADS)
    return (gq, gk, gv, g_f, g_b), (sq, sk, sv), gg

def gla_scan(q, k, v, g, s0):
    B, H, T, DK = q.shape
    DV = v.shape[-1]
    n = T // GLA_CHUNK

    def chunks(t):
        return jnp.moveaxis(t.reshape(B, H, n, GLA_CHUNK, t.shape[-1]), 2, 0)

    causal = jnp.tril(jnp.ones((GLA_CHUNK, GLA_CHUNK), dtype=bool))[:, :, None]

    def step(S, inp):
        qc, kc, vc, gc = inp
        b = jnp.cumsum(gc.astype(jnp.float32), axis=2)
        rel = jnp.where(causal, b[:, :, :, None, :] - b[:, :, None, :, :], -jnp.inf)
        decay = jnp.exp(rel)
        A = jnp.einsum('bhid,bhjd,bhijd->bhij', qc, kc, decay)
        o = (jnp.einsum('bhid,bhde->bhie', qc * jnp.exp(b), S)
             + jnp.einsum('bhij,bhje->bhie', A, vc))
        b_last = b[:, :, -1:, :]
        S = (jnp.exp(b_last[:, :, 0, :])[..., None] * S
             + jnp.einsum('bhjd,bhje->bhde', kc * jnp.exp(b_last - b), vc))
        return S, o

    S, o = lax.scan(step, s0.astype(jnp.float32), (chunks(q), chunks(k), chunks(v), chunks(g)))
    o = jnp.moveaxis(o, 0, 2).reshape(B, H, T, DV)
    return o.astype(v.dtype), S

def gla_bidirectional(q, k, v, g_f, g_b, s0_f, s0_b):
    o_f, s_f = gla_scan(q, k, v, g_f, s0_f)
    flip = lambda t: jnp.flip(t, axis=2)
    o_b, s_b = gla_scan(flip(q), flip(k), flip(v), flip(g_b), s0_b)
    return o_f + flip(o_b), s_f, s_b

def softmax_with_sink(s, sink):
    sk = jnp.broadcast_to(sink.astype(jnp.float32).reshape(1, SWA_KV_HEADS, SWA_GROUP, 1, 1),
                          s.shape[:-1] + (1,))
    p = jax.nn.softmax(jnp.concatenate([s, sk], axis=-1), axis=-1)
    return p[..., :-1]

def context_attention(q, k, v, sink):
    B, KVH, G, Lc, D = q.shape
    scale = HEAD_DIM ** -0.5

    def blk(i):
        qb = lax.dynamic_slice_in_dim(q, i * BLOCK, BLOCK, axis=3)
        s = jnp.einsum('bkgqd,bksd->bkgqs', qb, k).astype(jnp.float32) * scale
        p = softmax_with_sink(s, sink).astype(v.dtype)
        return jnp.einsum('bkgqs,bksd->bkgqd', p, v)

    o = lax.map(blk, jnp.arange(Lc // BLOCK))
    return jnp.moveaxis(o, 0, 3).reshape(B, KVH, G, Lc, D)

def latent_attention(q, k, v, kc, vc, sink):
    B, KVH, G, T, D = q.shape
    scale = HEAD_DIM ** -0.5
    span = BLOCK + 2 * WINDOW
    pad = ((0, 0), (0, 0), (WINDOW, WINDOW), (0, 0))
    kp, vp = jnp.pad(k, pad), jnp.pad(v, pad)

    def blk(i):
        qb = lax.dynamic_slice_in_dim(q, i * BLOCK, BLOCK, axis=3)
        kb = lax.dynamic_slice_in_dim(kp, i * BLOCK, span, axis=2)
        vb = lax.dynamic_slice_in_dim(vp, i * BLOCK, span, axis=2)
        qpos = i * BLOCK + jnp.arange(BLOCK)
        kpos = i * BLOCK - WINDOW + jnp.arange(span)
        valid = ((jnp.abs(qpos[:, None] - kpos[None, :]) <= WINDOW)
                 & (kpos[None, :] >= 0) & (kpos[None, :] < T))
        s_loc = jnp.einsum('bkgqd,bksd->bkgqs', qb, kb).astype(jnp.float32) * scale
        s_loc = jnp.where(valid, s_loc, NEG_INF)
        s_ctx = jnp.einsum('bkgqd,bksd->bkgqs', qb, kc).astype(jnp.float32) * scale
        p = softmax_with_sink(jnp.concatenate([s_loc, s_ctx], axis=-1), sink).astype(v.dtype)
        return (jnp.einsum('bkgqs,bksd->bkgqd', p[..., :span], vb)
                + jnp.einsum('bkgqs,bksd->bkgqd', p[..., span:], vc))

    o = lax.map(blk, jnp.arange(T // BLOCK))
    return jnp.moveaxis(o, 0, 3).reshape(B, KVH, G, T, D)

def merge(o_gla, gg, gla_norm, o_swa, w_o):
    B, H, T, DV = o_gla.shape
    og = rmsnorm(o_gla.transpose(0, 2, 1, 3), gla_norm).reshape(B, T, GLA_WIDTH) * jax.nn.silu(gg)
    osw = o_swa.transpose(0, 3, 1, 2, 4).reshape(B, T, SWA_WIDTH)
    return jnp.concatenate([og, osw], axis=-1) @ w_o

def sq_relu_mlp(h, w1, w2):
    return jnp.square(jax.nn.relu(h @ w1)) @ w2

def setup_inputs(seed: int = 0) -> dict:
    key = jax.random.key(seed)
    ks = jax.random.split(key, 26)
    nrm = lambda k, shape, s: jax.random.normal(k, shape, jnp.float32) * s
    gain = lambda k, shape: 1.0 + nrm(k, shape, 0.02)
    L = DEPTH
    return {
        "x_prompt": nrm(ks[0], (BATCH, SEQ, D_MODEL), 1.0),
        "x_sample": nrm(ks[1], (DEC_BATCH, DEC_SEQ, D_MODEL), 1.0),
        "c": nrm(ks[2], (DEC_BATCH, D_MODEL), 1.0),
        "cache_k": nrm(ks[3], (DEC_BATCH, L, SWA_KV_HEADS, PAST_LEN, HEAD_DIM), 1.0),
        "cache_v": nrm(ks[4], (DEC_BATCH, L, SWA_KV_HEADS, PAST_LEN, HEAD_DIM), 1.0),
        "state_gla_fwd": nrm(ks[5], (DEC_BATCH, L, GLA_HEADS, GLA_DK, GLA_DV), 0.3),
        "state_gla_bwd": nrm(ks[6], (DEC_BATCH, L, GLA_HEADS, GLA_DK, GLA_DV), 0.3),
        "c_ctx": nrm(ks[7], (D_MODEL,), 1.0),
        "w_ada": nrm(ks[8], (L, D_MODEL, 6 * D_MODEL), 0.5 * D_MODEL ** -0.5),
        "b_ada": nrm(ks[9], (L, 6 * D_MODEL), 0.02),
        "norm_mix": gain(ks[10], (L, D_MODEL)),
        "norm_ff": gain(ks[11], (L, D_MODEL)),
        "w_in": nrm(ks[12], (L, D_MODEL, D_IN), D_MODEL ** -0.5),
        "w_gk_fwd": nrm(ks[13], (L, GATE_RANK, GLA_HEADS * GLA_DK), GATE_RANK ** -0.5),
        "b_gk_fwd": nrm(ks[14], (L, GLA_HEADS * GLA_DK), 0.1),
        "w_gk_bwd": nrm(ks[15], (L, GATE_RANK, GLA_HEADS * GLA_DK), GATE_RANK ** -0.5),
        "b_gk_bwd": nrm(ks[16], (L, GLA_HEADS * GLA_DK), 0.1),
        "gla_norm": gain(ks[17], (L, GLA_DV)),
        "q_norm": gain(ks[18], (L, HEAD_DIM)),
        "k_norm": gain(ks[19], (L, HEAD_DIM)),
        "sink": nrm(ks[20], (L, SWA_HEADS), 0.5),
        "w_o": nrm(ks[21], (L, MIX_WIDTH, D_MODEL), MIX_WIDTH ** -0.5),
        "w_ff1": nrm(ks[22], (L, D_MODEL, D_FF), D_MODEL ** -0.5),
        "w_ff2": nrm(ks[23], (L, D_FF, D_MODEL), D_FF ** -0.5),
    }

def reference(x_prompt, x_sample, c, cache_k, cache_v, state_gla_fwd, state_gla_bwd, c_ctx,
              w_ada, b_ada, norm_mix, norm_ff, w_in, w_gk_fwd, b_gk_fwd, w_gk_bwd, b_gk_bwd,
              gla_norm, q_norm, k_norm, sink, w_o, w_ff1, w_ff2):
    rope = axial_rope(x_sample.shape[1])
    xp, xs = x_prompt, x_sample
    new_k, new_v, new_sf, new_sb = [], [], [], []
    for l in range(DEPTH):
        proj_w = (w_in[l], w_gk_fwd[l], b_gk_fwd[l], w_gk_bwd[l], b_gk_bwd[l], q_norm[l], k_norm[l])

        sh1, sc1, g1, sh2, sc2, g2 = modulation(c_ctx[None, :], w_ada[l], b_ada[l])
        h = adaln(xp, norm_mix[l], sh1, sc1)
        (gq, gk, gv, gf, gb), (sq, sk, sv), gg = project(h, *proj_w)
        zeros = jnp.zeros((xp.shape[0], GLA_HEADS, GLA_DK, GLA_DV), jnp.float32)
        o_gla, s_f, s_b = gla_bidirectional(gq, gk, gv, gf, gb, zeros, zeros)
        o_swa = context_attention(sq, sk, sv, sink[l])
        xp = xp + g1 * merge(o_gla, gg, gla_norm[l], o_swa, w_o[l])
        h = adaln(xp, norm_ff[l], sh2, sc2)
        xp = xp + g2 * sq_relu_mlp(h, w_ff1[l], w_ff2[l])
        new_k.append(sk)
        new_v.append(sv)
        new_sf.append(s_f.astype(xp.dtype))
        new_sb.append(s_b.astype(xp.dtype))

        sh1, sc1, g1, sh2, sc2, g2 = modulation(c, w_ada[l], b_ada[l])
        h = adaln(xs, norm_mix[l], sh1, sc1)
        (gq, gk, gv, gf, gb), (sq, sk, sv), gg = project(h, *proj_w)
        sq = apply_rope(sq, rope)
        sk = apply_rope(sk, rope)
        o_gla, _, _ = gla_bidirectional(gq, gk, gv, gf, gb, state_gla_fwd[:, l], state_gla_bwd[:, l])
        o_swa = latent_attention(sq, sk, sv, cache_k[:, l], cache_v[:, l], sink[l])
        xs = xs + g1 * merge(o_gla, gg, gla_norm[l], o_swa, w_o[l])
        h = adaln(xs, norm_ff[l], sh2, sc2)
        xs = xs + g2 * sq_relu_mlp(h, w_ff1[l], w_ff2[l])

    return (xp, xs, jnp.stack(new_k, axis=1), jnp.stack(new_v, axis=1),
            jnp.stack(new_sf, axis=1), jnp.stack(new_sb, axis=1))


_drawn_inputs = setup_inputs


def setup_inputs(seed=0):
    import zlib

    import numpy as np

    out = dict(_drawn_inputs(seed))
    spreads = {}
    factors = {'cache_k': 6.114,
     'cache_v': 4.783,
     'state_gla_fwd': 8.0,
     'state_gla_bwd': 8.0,
     'norm_ff': 6.059,
     'gla_norm': 28.173,
     'q_norm': 8.0,
     'k_norm': 7.897,
     'sink': 8.0}
    for name, (base, spread) in spreads.items():
        noise = np.random.default_rng([zlib.crc32(name.encode()), seed]).standard_normal(out[name].shape)
        drawn = base * np.exp(spread * noise) if base else spread * noise
        out[name] = __import__('jax').numpy.asarray(drawn.astype(out[name].dtype))
    for name, factor in factors.items():
        out[name] = (out[name] * factor).astype(out[name].dtype)
    return out
```

```python
from contextlib import ExitStack

import numpy as np

import concourse.bass as bass
from concourse import mybir

F32 = mybir.dt.float32
F32R = mybir.dt.float32r
BF16 = mybir.dt.bfloat16
ALU = mybir.AluOpType
ACT = mybir.ActivationFunctionType
AX_X = mybir.AxisListType.X

P = 128
D = 1024
KD = D // P
TP, TS = 256, 1024
T = TP + TS
NT, NTP = T // P, TP // P
PAST = 512
H = 8
DH = 64
KV = 2
GW = H * DH
RANK = 16
DIN = 4 * GW + 2 * RANK + GW + 2 * KV * DH
C_GG, C_LR, C_SQ = 3 * GW, 4 * GW, 4 * GW + 2 * RANK
DFF = 4 * D
EPS = 1e-6
NEG = -1e30
GRID_W = 64
THETA = 10000.0
GATE_TEMP = 16.0
CLAMP = 42.0
HALF = 512


def constants():
    j = np.arange(P)[:, None]
    i = np.arange(P)[None, :]
    mid = P // 2
    cum_f = ((j <= i).astype(np.float32) - (j < mid)) / GATE_TEMP
    cum_b = ((j >= i).astype(np.float32) - (j >= mid)) / GATE_TEMP
    vec_f = np.zeros((P, 4), np.float32)
    vec_f[:mid, 0] = 1 / GATE_TEMP
    vec_f[:, 1] = 1 / GATE_TEMP
    vec_f[mid:, 2] = 1 / GATE_TEMP
    vec_b = vec_f.copy()
    vec_b[:, 0], vec_b[:, 2] = vec_f[:, 2], vec_f[:, 0]
    keep_f = (j <= i).astype(np.float32)
    keep_b = (j >= i).astype(np.float32)
    ident = np.eye(P, dtype=np.float32)
    mats = np.concatenate([ident, cum_f, cum_b, keep_f, keep_b, vec_f, vec_b], 1).astype(np.float32)
    tiles = TS // P
    left = np.where(i >= j, 0.0, NEG)
    right = np.where(i <= j, 0.0, NEG)
    none = np.full((P, P), NEG)
    left_all = np.concatenate([none] + [left] * (tiles - 1), 1)
    right_all = np.concatenate([right] * (tiles - 1) + [none], 1)
    window = np.concatenate([left_all, right_all], 1).astype(np.float32)
    half = DH // 4
    freqs = (THETA ** (-np.arange(half, dtype=np.float32) / half)).astype(np.float32)
    t = np.arange(TS)
    row = (t // GRID_W).astype(np.float32)[:, None] * freqs
    col = (t % GRID_W).astype(np.float32)[:, None] * freqs
    cos = np.concatenate([np.cos(row), np.cos(row), np.cos(col), np.cos(col)], 1)
    sin = np.concatenate([-np.sin(row), np.sin(row), -np.sin(col), np.sin(col)], 1)
    cos = np.concatenate([np.ones((TP, DH)), cos], 0).astype(np.float32)
    sin = np.concatenate([np.zeros((TP, DH)), sin], 0).astype(np.float32)
    rope = np.stack([cos, sin], 1)
    return mats, window, rope


class Space:

    def __init__(self, nc, ctx, prefix):
        self.nc, self.ctx, self.prefix, self.sems = nc, ctx, prefix, []
        ctx.callback(self.clear)

    def sb(self, name, shape, dt=F32):
        return self.ctx.enter_context(self.nc.sbuf_tensor(f"{self.prefix}_{name}", shape, dt))

    def ps(self, name, shape, dt=F32):
        return self.ctx.enter_context(self.nc.psum_tensor(f"{self.prefix}_{name}", shape, dt))

    def sem(self, name):
        self.sems.append(self.nc.alloc_semaphore(f"{self.prefix}_{name}"))
        return self.sems[-1]

    def clear(self):
        if self.sems:
            self.nc.clear_and_free_semaphores(self.sems)
            self.nc.all_engine_barrier()


def tile_rows(t):
    return bass.ds(t * P, P)


def modulation(nc, keep, a, scratch):
    COLS = HALF
    NCH = 6 * D // COLS
    with ExitStack() as ctx:
        s = Space(nc, ctx, "ada")
        w = s.sb("w", [P, 2, KD, COLS])
        cond = s.sb("cond", [P, 2, KD])
        e = s.sb("e", [P, 2, KD])
        e1 = s.sb("e1", [P, 2, KD])
        rec = s.sb("rec", [P, 2, KD])
        silu = s.sb("silu", [P, KD, 2])
        bias = s.sb("bias", [2, 6 * D])
        rows = s.sb("rows", [2, 6 * D])
        gain = s.sb("gain", [P, 2, KD])
        acc = s.ps("acc", [2, 2, COLS])
        cols = s.ps("cols", [P, 4, KD, 2])
        small_in = s.sem("small_in")
        w_in = [s.sem(f"w_in{j}") for j in range(2)]
        e_ready, e1_ready, rec_ready, silu_ready = (s.sem(n) for n in ("e_ready", "e1_ready", "rec_ready", "silu_ready"))
        acc_ready, rows_ready, cols_ready, mod_ready, scaled = (
            s.sem(n) for n in ("acc_ready", "rows_ready", "cols_ready", "mod_ready", "scaled"))
        rows_out = s.sem("rows_out")
        PARTS = (0, 1, 3, 4)
        with nc.Block() as block:

            @block.sync
            def _(sp):
                sp.dma_start(cond[:, 0, :], a["c_ctx"].rearrange("(k p) -> p k", p=P), allow_slow_non_contiguous=True).then_inc(small_in, 16)
                sp.dma_start(cond[:, 1, :], a["c"][0].rearrange("(k p) -> p k", p=P), allow_slow_non_contiguous=True).then_inc(small_in, 16)
                sp.dma_start(bias[:, :], a["b_ada"].broadcast_to([2, 6 * D])).then_inc(small_in, 16)
                sp.dma_start(gain[:, 0, :], a["norm_mix"][0].rearrange("(k p) -> p k", p=P), allow_slow_non_contiguous=True).then_inc(small_in, 16)
                sp.dma_start(gain[:, 1, :], a["norm_ff"][0].rearrange("(k p) -> p k", p=P), allow_slow_non_contiguous=True).then_inc(small_in, 16)
                sp.dma_start(keep["mats"][:, :], a["mats"]).then_inc(small_in, 16)
                wv = a["w_ada"][0].rearrange("(k p) n -> p k n", p=P)

                def load(i, j, first):
                    if not first:
                        sp.wait_ge(acc_ready, 2 * i + j - 1)
                    sp.dma_start(w[:, j], wv[:, :, bass.ds((2 * i + j) * COLS, COLS)]).then_inc(w_in[j], 16)

                for j in range(2):
                    load(0, j, True)
                with sp.Fori(1, NCH // 2) as i:
                    for j in range(2):
                        load(i, j, False)
                sp.wait_ge(rows_ready, NCH)
                sp.dma_start(scratch["mod"], rows[:, :]).then_inc(rows_out, 16)
                sp.wait_ge(rows_out, 16)

            @block.scalar
            def _(act):
                act.wait_ge(small_in, 6 * 16)
                act.activation(e[:, :, :], cond[:, :, :], ACT.Exp, scale=-1.0).then_inc(e_ready, 1)

            @block.vector
            def _(dve):
                dve.wait_ge(e_ready, 1)
                dve.tensor_scalar(e1[:, :, :], e[:, :, :], 1.0, None, ALU.add).then_inc(e1_ready, 1)
                dve.wait_ge(e1_ready, 1)
                dve.reciprocal(rec[:, :, :], e1[:, :, :]).then_inc(rec_ready, 1)
                dve.wait_ge(rec_ready, 1)
                dve.tensor_tensor(silu[:, :, :], cond[:, :, :].rearrange("p c k -> p k c"),
                                  rec[:, :, :].rearrange("p c k -> p k c"), ALU.mult).then_inc(silu_ready, 1)
                with dve.Fori(0, NCH // 2) as i:
                    for j in range(2):
                        dve.wait_ge(acc_ready, 2 * i + j + 1)
                        at = bass.ds((2 * i + j) * COLS, COLS)
                        dve.tensor_tensor(rows[:, at], acc[:, j], bias[:, at], ALU.add).then_inc(rows_ready, 1)
                dve.wait_ge(cols_ready, 1)
                for n in range(2):
                    dve.tensor_copy(keep["shift"][:, n], cols[:, 2 * n]).then_inc(mod_ready, 1)
                    dve.tensor_scalar(keep["scale"][:, n], cols[:, 2 * n + 1], 1.0, None, ALU.add).then_inc(mod_ready, 1)
                dve.wait_ge(mod_ready, 4)
                for n in range(2):
                    for c in range(2):
                        dve.tensor_tensor(keep["scale"][:, n, :, c], keep["scale"][:, n, :, c], gain[:, n, :],
                                          ALU.mult).then_inc(scaled, 1)

            @block.tensor
            def _(pe):
                pe.wait_ge(silu_ready, 1)

                def body(i, first):
                    for j in range(2):
                        pe.wait_ge(w_in[j], 16 * i + 16)
                        if not first:
                            pe.wait_ge(rows_ready, 2 * i + j - 1)
                        for k in range(KD):
                            mm = pe.matmul(acc[:, j], silu[:, k, :], w[:, j, k, :], start=(k == 0), stop=(k == KD - 1))
                        mm.then_inc(acc_ready, 1)
                body(0, True)
                with pe.Fori(1, NCH // 2) as i:
                    body(i, False)
                pe.wait_ge(rows_ready, NCH)
                for n, part in enumerate(PARTS):
                    for k in range(KD):
                        at = part * D + k * P
                        tr = pe.transpose(cols[:, n, k, :], rows[0:2, at:at + P], keep["ident"][0:2, 0:2])
                tr.then_inc(cols_ready, 1)


class NormStage:

    def __init__(self, s, keep, which, hi, lo, slots=2):
        self.slots = slots
        self.keep, self.which, self.hi, self.lo = keep, which, hi, lo
        self.x = s.sb("x", [P, 2, D])
        self.ssq = s.sb("ssq", [P, 2])
        self.ms = s.sb("ms", [P, 2])
        self.rstd = s.sb("rstd", [P, 2])
        self.xn = s.sb("xn", [P, 2, D])
        self.h = s.sb("h", [P, slots, KD, P])
        self.xT = s.ps("xT", [P, slots, KD, P])
        self.ssq_ready, self.ms_ready = s.sem("ssq_ready"), s.sem("ms_ready")
        self.rstd_ready, self.xn_ready = s.sem("rstd_ready"), s.sem("xn_ready")
        self.xT_ready, self.h_ready = s.sem("xT_ready"), s.sem("h_ready")
        self.hi_ready, self.lo_ready = s.sem("hi_ready"), s.sem("lo_ready")

    def act_square(self, act, i, j, ready, value, first):
        act.wait_ge(ready, value)
        if not first:
            act.wait_ge(self.xT_ready, 2 * i + j - 1)
        act.activation(self.xn[:, j], self.x[:, j], ACT.Square, accum_out=self.ssq[:, j:j + 1]).then_inc(self.ssq_ready, 1)

    def pool_rstd(self, pool, i, j):
        t = 2 * i + j
        pool.wait_ge(self.ssq_ready, t + 1)
        pool.tensor_tensor(self.ms[:, j:j + 1], self.ssq[:, j:j + 1], self.keep["eps_d"][:, 0:1], ALU.add).then_inc(self.ms_ready, 1)
        pool.wait_ge(self.ms_ready, t + 1)
        pool.tensor_tensor(self.rstd[:, j:j + 1], self.ms[:, j:j + 1], self.keep["minus_half"][:, 0:1], ALU.pow).then_inc(self.rstd_ready, 1)

    def dve_xn(self, dve, i, j, first):
        t = 2 * i + j
        dve.wait_ge(self.rstd_ready, t + 1)
        if not first:
            dve.wait_ge(self.xT_ready, t - 1)
        dve.tensor_scalar(self.xn[:, j], self.x[:, j], self.rstd[:, j:j + 1], D ** 0.5, ALU.mult, ALU.mult).then_inc(self.xn_ready, 1)

    def pe_transpose(self, pe, i, j, first):
        t = 2 * i + j
        m = j % self.slots
        pe.wait_ge(self.xn_ready, t + 1)
        if not (first and j < self.slots):
            pe.wait_ge(self.h_ready, t + 1 - self.slots)
        for k in range(KD):
            tr = pe.transpose(self.xT[:, m, k], self.xn[:, j, k * P:(k + 1) * P], self.keep["ident"])
        tr.then_inc(self.xT_ready, 1)

    def dve_modulate(self, dve, i, j, cond, first):
        t = 2 * i + j
        m = j % self.slots
        dve.wait_ge(self.xT_ready, t + 1)
        if not (first and j < self.slots):
            dve.wait_ge(self.lo_ready, t + 1 - self.slots)
        for k in range(KD):
            op = dve.tensor_scalar(self.h[:, m, k], self.xT[:, m, k], self.keep["scale"][:, self.which, k, cond:cond + 1],
                                   self.keep["shift"][:, self.which, k, cond:cond + 1], ALU.mult, ALU.add)
        op.then_inc(self.h_ready, 1)

    def act_hi(self, act, i, j):
        t = 2 * i + j
        act.wait_ge(self.h_ready, t + 1)
        act.activation(self.hi[:, :, tile_rows(t)], self.h[:, j % self.slots], ACT.Copy).then_inc(self.hi_ready, 1)

    def pool_lo(self, pool, i, j):
        t = 2 * i + j
        pool.wait_ge(self.hi_ready, t + 1)
        pool.tensor_tensor(self.lo[:, :, tile_rows(t)], self.h[:, j % self.slots], hi_view(self.hi)[:, :, tile_rows(t)],
                           ALU.subtract).then_inc(self.lo_ready, 1)


def hi_view(hi):
    return hi[:, :, :].bitcast(F32)


def pairs(engine, body):
    body(0, 0, True)
    with engine.Fori(1, NT // 2) as i:
        body(i, 1, False)


def norm_first(nc, keep, a, hi, lo):
    with ExitStack() as ctx:
        s = Space(nc, ctx, "n1")
        st = NormStage(s, keep, 0, hi, lo)
        x_in = [s.sem(f"x_in{j}") for j in range(2)]
        const_ready = s.sem("const_ready")
        with nc.Block() as block:

            @block.sync
            def _(sp):
                for j in range(2):
                    sp.dma_start(st.x[:, j], a["x_prompt"][0, j * P:(j + 1) * P, :]).then_inc(x_in[j], 16)
                with sp.Fori(1, NT // 2) as i:
                    for j in range(2):
                        sp.wait_ge(st.xn_ready, 2 * i + j - 1)
                        sp.dma_start(st.x[:, j], a["x_sample"][0, bass.ds((2 * i + j - NTP) * P, P), :]).then_inc(x_in[j], 16)

            @block.scalar
            def _(act):
                def body(i, cond, first):
                    for j in range(2):
                        st.act_square(act, i, j, x_in[j], 16 * i + 16, first)
                    for j in range(2):
                        st.act_hi(act, i, j)
                pairs(act, body)

            @block.gpsimd
            def _(pool):
                pool.memset(keep["minus_half"][:, :], -0.5).then_inc(const_ready, 1)
                pool.memset(keep["eps_d"][:, :], D * EPS).then_inc(const_ready, 1)
                pool.memset(keep["eps_h"][:, :], DH * EPS).then_inc(const_ready, 1)
                pool.wait_ge(const_ready, 3)

                def body(i, cond, first):
                    for j in range(2):
                        st.pool_rstd(pool, i, j)
                    for j in range(2):
                        st.pool_lo(pool, i, j)
                pairs(pool, body)

            @block.vector
            def _(dve):
                def body(i, cond, first):
                    for j in range(2):
                        st.dve_xn(dve, i, j, first)
                    for j in range(2):
                        st.dve_modulate(dve, i, j, cond, first)
                pairs(dve, body)

            @block.tensor
            def _(pe):
                def body(i, cond, first):
                    for j in range(2):
                        st.pe_transpose(pe, i, j, first)
                pairs(pe, body)


def project(nc, a, hi, lo, scratch):
    NG = 8
    COLS = DIN // NG
    RING = 4
    assert COLS * NG == DIN and COLS <= HALF and (2 * NT) % RING == 0
    with ExitStack() as ctx:
        s = Space(nc, ctx, "in")
        raw = s.sb("raw", [P, 2, KD, COLS])
        whi = [s.sb(f"whi{j}", [P, KD, COLS], F32R) for j in range(2)]
        wlo = [s.sb(f"wlo{j}", [P, KD, COLS], F32R) for j in range(2)]
        stage = s.sb("stage", [P, RING, COLS])
        acc = s.ps("acc", [P, RING, HALF])
        w_in = [s.sem(f"w_in{j}") for j in range(2)]
        whi_ready, wlo_ready, acc_ready = s.sem("whi_ready"), s.sem("wlo_ready"), s.sem("acc_ready")
        staged = [s.sem("staged_dve"), s.sem("staged_act")]
        stored = [s.sem(f"stored{b}") for b in range(RING)]
        wv = a["w_in"][0].rearrange("(k p) n -> p k n", p=P)
        with nc.Block() as block:

            @block.sync
            def _(sp):
                for j in range(2):
                    sp.dma_start(raw[:, j], wv[:, :, j * COLS:(j + 1) * COLS]).then_inc(w_in[j], 16)

                def body(i, last):
                    for j in range(2):
                        g = 2 * i + j
                        if not last:
                            sp.wait_ge(wlo_ready, g + 1)
                            sp.dma_start(raw[:, j], wv[:, :, bass.ds((g + 2) * COLS, COLS)]).then_inc(w_in[j], 16)
                        for t in range(NT):
                            n = NT * j + t
                            sp.wait_ge(staged[n % 2], NT * i + n // 2 + 1)
                            sp.dma_start(scratch["proj"][t * P:(t + 1) * P, bass.ds(g * COLS, COLS)],
                                         stage[:, n % RING]).then_inc(stored[n % RING], 16)
                with sp.Fori(0, NG // 2 - 1) as i:
                    body(i, False)
                body(NG // 2 - 1, True)
                for b in range(RING):
                    sp.wait_ge(stored[b], 16 * NG * NT // RING)

            def evacuate(eng, copy, parity, i, first):
                for n in range(parity, 2 * NT, 2):
                    eng.wait_ge(acc_ready, 2 * NT * i + n + 1)
                    if not (first and n < RING):
                        eng.wait_ge(stored[n % RING], 16 * (2 * NT // RING * i + n // RING))
                    copy(stage[:, n % RING], acc[:, n % RING, 0:COLS]).then_inc(staged[parity], 1)

            @block.scalar
            def _(act):
                def split(i, j, first):
                    g = 2 * i + j
                    act.wait_ge(w_in[j], 16 * i + 16)
                    if not first:
                        act.wait_ge(acc_ready, NT * (g - 1))
                    act.activation(whi[j][:, :, :], raw[:, j], ACT.Copy).then_inc(whi_ready, 1)

                def copy(out, in_):
                    return act.activation(out, in_, ACT.Copy)
                for j in range(2):
                    split(0, j, True)

                def body(i, first, last):
                    for j in range(2):
                        for n in range(NT * j + (1 - (NT * j) % 2), NT * (j + 1), 2):
                            act.wait_ge(acc_ready, 2 * NT * i + n + 1)
                            if not (first and n < RING):
                                act.wait_ge(stored[n % RING], 16 * (2 * NT // RING * i + n // RING))
                            copy(stage[:, n % RING], acc[:, n % RING, 0:COLS]).then_inc(staged[1], 1)
                        if not last:
                            split(i + 1, j, False)
                body(0, True, False)
                with act.Fori(1, NG // 2 - 1) as i:
                    body(i, False, False)
                body(NG // 2 - 1, False, True)

            @block.gpsimd
            def _(pool):
                with pool.Fori(0, NG // 2) as i:
                    for j in range(2):
                        g = 2 * i + j
                        pool.wait_ge(whi_ready, g + 1)
                        pool.tensor_tensor(wlo[j][:, :, :], raw[:, j], hi_view(whi[j]), ALU.subtract).then_inc(wlo_ready, 1)

            @block.vector
            def _(dve):
                evacuate(dve, dve.tensor_copy, 0, 0, True)
                with dve.Fori(1, NG // 2) as i:
                    evacuate(dve, dve.tensor_copy, 0, i, False)

            @block.tensor
            def _(pe):
                def body(i, first):
                    for j in range(2):
                        pe.wait_ge(wlo_ready, 2 * i + j + 1)
                        for t in range(NT):
                            n = NT * j + t
                            if not (first and n < RING):
                                pe.wait_ge(staged[n % 2], NT * i + n // 2 - 1)
                            for k in range(KD):
                                x_hi, x_lo = (x[:, k, t * P:(t + 1) * P] for x in (hi, lo))
                                pe.matmul(acc[:, n % RING, 0:COLS], x_hi, whi[j][:, k, :], start=(k == 0), stop=False)
                                pe.matmul(acc[:, n % RING, 0:COLS], x_hi, wlo[j][:, k, :], start=False, stop=False)
                                mm = pe.matmul(acc[:, n % RING, 0:COLS], x_lo, whi[j][:, k, :], start=False, stop=(k == KD - 1))
                            mm.then_inc(acc_ready, 1)
                body(0, True)
                with pe.Fori(1, NG // 2) as i:
                    body(i, False)


def gla(nc, keep, a, scratch, outs):
    with ExitStack() as ctx:
        s = Space(nc, ctx, "gla")
        qkv = s.sb("qkv", [P, NT, 3 * GW])
        glr = s.sb("glr", [P, NT, 2 * RANK])
        lrT = s.sb("lrT", [2 * RANK + 1, T])
        wgk = s.sb("wgk", [2 * RANK + 1, 2, GW])
        lr = [s.sb(f"lr{d}", [2 * RANK + 1, P]) for d in range(2)]
        mag = s.sb("mag", [P, 2, GW])
        ex = s.sb("ex", [P, 2, GW])
        ln = s.sb("ln", [P, 2, GW])
        g = s.sb("g", [P, 2, GW])
        bc = s.sb("bc", [P, 2, GW])
        up = s.sb("up", [P, 2, GW])
        down = s.sb("down", [P, 2, GW])
        qe = s.sb("qe", [P, 2, GW])
        ke = s.sb("ke", [P, 2, GW])
        qT = s.sb("qT", [P, 2, H // 2, P])
        kT = s.sb("kT", [P, 2, H // 2, P])
        at = s.sb("at", [P, 2, H, P])
        dec = s.sb("dec", [P, 2, H // 2, 4])
        state = [s.sb("state_p", [P, 2, H // 2, DH]), s.sb("state_s", [P, 2, H // 2, DH])]
        mid = s.sb("mid", [P, 2, H // 2, 2, DH])
        kept = s.sb("kept", [P, 2, H // 2, DH])
        new = s.sb("new", [P, 2, H // 2, DH])
        o = s.sb("o", [P, 2, NT, GW])
        ps = [s.ps(f"ps{d}", [P, 4, HALF]) for d in range(2)]
        (lr_ready, logit_ready, mag_ready, ex_ready, ln_ready, g_ready, bc_ready, clamp_ready, up_ready, down_ready,
         qe_ready, ke_ready, tr_ready, qT_ready, kT_ready, score_ready, at_ready, dec_ready, mid_ready, o_ready,
         o_kept, ds_ready, kept_ready, new_ready, state_ready) = (s.sem(n) for n in (
             "lr_ready", "logit_ready", "mag_ready", "ex_ready", "ln_ready", "g_ready", "bc_ready", "clamp_ready",
             "up_ready", "down_ready", "qe_ready", "ke_ready", "tr_ready", "qT_ready", "kT_ready", "score_ready",
             "at_ready", "dec_ready", "mid_ready", "o_ready", "o_kept", "ds_ready", "kept_ready", "new_ready",
             "state_ready"))
        loaded, zeroed, weights_in, lrT_ready, lrT_kept, stored = (s.sem(n) for n in (
            "loaded", "zeroed", "weights_in", "lrT_ready", "lrT_kept", "stored"))

        def steps(eng, body):
            body(0, 0, True)
            body(1, 0, False)
            with eng.Fori(2, NT) as i:
                body(i, 1, False)

        def tiles_of(eng, i, part):
            if part == 0:
                return i, NTP - 1 - i
            return eng.snap(i + 0), eng.snap(i * -1 + (NTP + NT - 1))

        with nc.Block() as block:

            @block.sync
            def _(sp):
                sp.dma_start(glr[:, :, :], scratch["proj"][:, C_LR:C_SQ].rearrange("(t p) n -> p t n", p=P)).then_inc(loaded, 16)
                for half in range(2):
                    t0 = half * NT // 2
                    sp.dma_start(qkv[:, t0:t0 + NT // 2, :],
                                 scratch["proj"][t0 * P:(t0 + NT // 2) * P, 0:3 * GW].rearrange("(t p) n -> p t n", p=P)
                                 ).then_inc(loaded, 16)
                sp.wait_ge(zeroed, 1)
                for d, (w, b) in enumerate((("w_gk_fwd", "b_gk_fwd"), ("w_gk_bwd", "b_gk_bwd"))):
                    sp.dma_start(wgk[d * RANK:(d + 1) * RANK, d, :], a[w][0]).then_inc(weights_in, 16)
                    sp.dma_start(wgk[2 * RANK:2 * RANK + 1, d, :], a[b]).then_inc(weights_in, 16)
                for d, name in enumerate(("state_gla_fwd", "state_gla_bwd")):
                    for half in range(2):
                        sp.dma_start(state[1][half * DH:(half + 1) * DH, d],
                                     a[name][0, 0].rearrange("(b c) k v -> c k b v", c=2)[half]).then_inc(loaded, 16)
                sp.wait_ge(state_ready, 2 * NTP)
                for d in range(2):
                    for half in range(2):
                        sp.dma_start(outs[4 + d][0, 0].rearrange("(b c) k v -> c k b v", c=2)[half],
                                     state[0][half * DH:(half + 1) * DH, d]).then_inc(stored, 16)
                sp.wait_ge(o_kept, 2 * NT)
                for d in range(2):
                    sp.dma_start(scratch["o"][d].rearrange("(t p) n -> p t n", p=P), o[:, d]).then_inc(stored, 16)
                sp.wait_ge(stored, 6 * 16)

            @block.gpsimd
            def _(pool):
                pool.wait_ge(lrT_kept, 3)
                pool.wait_ge(zeroed, 4)
                pool.wait_ge(loaded, 7 * 16)

                def body(i, part, first):
                    tile = tiles_of(pool, i, part)
                    for d in range(2):
                        u = 2 * i + d
                        if not first:
                            pool.wait_ge(logit_ready, u - 1)
                        pool.tensor_copy(lr[d][:, :], lrT[:, tile_rows(tile[d])]).then_inc(lr_ready, 1)
                    for d in range(2):
                        u = 2 * i + d
                        pool.wait_ge(down_ready, u + 1)
                        if not first:
                            pool.wait_ge(ds_ready, u - 1)
                        pool.tensor_tensor(ke[:, d], down[:, d], qkv[:, bass.ds(tile[d], 1), GW:2 * GW].rearrange("p t n -> p (t n)"),
                                           ALU.mult).then_inc(ke_ready, 1)
                steps(pool, body)

            @block.scalar
            def _(act):
                def body(i, part, first):
                    for d in range(2):
                        u = 2 * i + d
                        act.wait_ge(logit_ready, u + 1)
                        act.activation(mag[:, d], ps[d][:, 0], ACT.Abs).then_inc(mag_ready, 1)
                        act.wait_ge(mag_ready, u + 1)
                        act.activation(ex[:, d], mag[:, d], ACT.Exp, scale=-1.0).then_inc(ex_ready, 1)
                        act.wait_ge(ex_ready, u + 1)
                        if not first:
                            act.wait_ge(g_ready, u - 1)
                        act.activation(ln[:, d], ex[:, d], ACT.Ln, bias=1.0).then_inc(ln_ready, 1)
                    for d in range(2):
                        u = 2 * i + d
                        act.wait_ge(clamp_ready, u + 1)
                        if not first:
                            act.wait_ge(qe_ready, u - 1)
                            act.wait_ge(ke_ready, u - 1)
                        act.activation(up[:, d], bc[:, d], ACT.Exp).then_inc(up_ready, 1)
                        act.activation(down[:, d], bc[:, d], ACT.Exp, scale=-1.0).then_inc(down_ready, 1)
                        if not first:
                            act.wait_ge(state_ready, u - 1)
                        act.activation(dec[:, d], ps[d][:, 3, 0:2 * H].rearrange("p (b c) -> p b c", c=4), ACT.Exp).then_inc(dec_ready, 1)
                    for d in range(2):
                        u = 2 * i + d
                        act.wait_ge(tr_ready, u + 1)
                        act.activation(qT[:, d], ps[d][:, 1].rearrange("p (b c) -> p b c", c=P), ACT.Copy).then_inc(qT_ready, 1)
                steps(act, body)

            @block.vector
            def _(dve):
                dve.memset(wgk[:, :, :], 0.0).then_inc(zeroed, 1)
                dve.memset(lrT[2 * RANK:2 * RANK + 1, :], 1.0).then_inc(zeroed, 1)
                dve.memset(state[0][:, :, :, :], 0.0).then_inc(zeroed, 1)
                dve.memset(mid[:, :, :, :, :], 0.0).then_inc(zeroed, 1)
                for n in range(3):
                    w = min(4, NT - 4 * n) * P
                    dve.wait_ge(lrT_ready, 1)
                    dve.tensor_copy(lrT[0:2 * RANK, 4 * n * P:4 * n * P + w], ps[0][0:2 * RANK, n, 0:w]).then_inc(lrT_kept, 1)
                dve.wait_ge(loaded, 7 * 16)
                dve.wait_ge(zeroed, 4)

                def body(i, part, first):
                    tile = tiles_of(dve, i, part)
                    for d in range(2):
                        u = 2 * i + d
                        dve.wait_ge(ln_ready, u + 1)
                        dve.scalar_tensor_tensor(g[:, d], ps[d][:, 0], 0.0, ln[:, d], ALU.min, ALU.subtract).then_inc(g_ready, 1)
                    for d in range(2):
                        u = 2 * i + d
                        dve.wait_ge(bc_ready, u + 1)
                        if not first:
                            dve.wait_ge(down_ready, u - 1)
                        dve.tensor_scalar(bc[:, d], ps[d][:, 0], CLAMP, -CLAMP, ALU.min, ALU.max).then_inc(clamp_ready, 1)
                    for d in range(2):
                        u = 2 * i + d
                        dve.wait_ge(up_ready, u + 1)
                        if not first:
                            dve.wait_ge(tr_ready, u - 1)
                        dve.scalar_tensor_tensor(qe[:, d], up[:, d], DH ** -0.5,
                                                 qkv[:, bass.ds(tile[d], 1), 0:GW].rearrange("p t n -> p (t n)"),
                                                 ALU.mult, ALU.mult).then_inc(qe_ready, 1)
                        dve.wait_ge(dec_ready, u + 1)
                        if not first:
                            dve.wait_ge(state_ready, u - 1)
                            dve.wait_ge(o_ready, u - 1)
                        for half in range(2):
                            rows = slice(half * DH, (half + 1) * DH)
                            dve.tensor_tensor(mid[rows, d, :, half], state[part][rows, d],
                                              dec[rows, d, :, 0:1].broadcast_to([DH, H // 2, DH]), ALU.mult).then_inc(mid_ready, 1)
                    for d in range(2):
                        u = 2 * i + d
                        dve.wait_ge(tr_ready, u + 1)
                        dve.tensor_copy(kT[:, d], ps[d][:, 2].rearrange("p (b c) -> p b c", c=P)).then_inc(kT_ready, 1)
                    for d in range(2):
                        u = 2 * i + d
                        dve.wait_ge(score_ready, u + 1)
                        if not first:
                            dve.wait_ge(o_ready, u - 1)
                        dve.tensor_tensor(at[:, d], ps[d][:, 1:3].rearrange("p b (c n) -> p (b c) n", n=P),
                                          keep["causal"][d].unsqueeze(1).broadcast_to([P, H, P]), ALU.mult).then_inc(at_ready, 1)
                        dve.tensor_tensor(kept[:, d], state[part][:, d], dec[:, d, :, 1:2].broadcast_to([P, H // 2, DH]),
                                          ALU.mult).then_inc(kept_ready, 1)
                    for d in range(2):
                        u = 2 * i + d
                        dve.wait_ge(ds_ready, u + 1)
                        for half in range(2):
                            rows = slice(half * DH, (half + 1) * DH)
                            upd = ps[d][rows, 0].rearrange("p (b c) -> p b c", c=P)[:, :, half * DH:(half + 1) * DH]
                            dve.tensor_tensor(new[rows, d], upd, dec[rows, d, :, 2:3].broadcast_to([DH, H // 2, DH]),
                                              ALU.mult).then_inc(new_ready, 1)
                        dve.wait_ge(new_ready, 2 * u + 2)
                        dve.wait_ge(kept_ready, u + 1)
                        dve.wait_ge(mid_ready, 2 * u + 2)
                        dve.tensor_tensor(state[part][:, d], kept[:, d], new[:, d], ALU.add).then_inc(state_ready, 1)
                        dve.wait_ge(o_ready, u + 1)
                        dve.tensor_copy(o[:, d, bass.ds(tile[d], 1), :].rearrange("p t n -> p (t n)"),
                                        ps[d][:, 3]).then_inc(o_kept, 1)
                steps(dve, body)

            @block.tensor
            def _(pe):
                pe.wait_ge(loaded, 7 * 16)
                for t in range(NT):
                    tr = pe.transpose(ps[0][0:2 * RANK, t // 4, (t % 4) * P:(t % 4 + 1) * P], glr[:, t, :], keep["ident"])
                tr.then_inc(lrT_ready, 1)
                pe.wait_ge(weights_in, 4 * 16)
                pe.wait_ge(lrT_kept, 3)

                def body(i, part, first):
                    tile = tiles_of(pe, i, part)
                    for d in range(2):
                        u = 2 * i + d
                        pe.wait_ge(lr_ready, u + 1)
                        if not first:
                            pe.wait_ge(state_ready, u - 1)
                        pe.matmul(ps[d][:, 0], lr[d][:, :], wgk[:, d, :], start=True, stop=True).then_inc(logit_ready, 1)
                    for d in range(2):
                        u = 2 * i + d
                        pe.wait_ge(g_ready, u + 1)
                        pe.matmul(ps[d][:, 0], keep["cum"][d], g[:, d], start=True, stop=True)
                        if not first:
                            pe.wait_ge(o_kept, u - 1)
                        for b in range(H // 2):
                            mm = pe.matmul(ps[d][:, 3, 4 * b:4 * b + 4], g[:, d, b * P:(b + 1) * P], keep["vec"][d],
                                           start=True, stop=True)
                        mm.then_inc(bc_ready, 1)
                    for d in range(2):
                        u = 2 * i + d
                        pe.wait_ge(qe_ready, u + 1)
                        pe.wait_ge(ke_ready, u + 1)
                        if not first:
                            pe.wait_ge(at_ready, u - 1)
                        for bank, x in ((1, qe), (2, ke)):
                            for b in range(H // 2):
                                tr = pe.transpose(ps[d][:, bank, b * P:(b + 1) * P], x[:, d, b * P:(b + 1) * P], keep["ident"])
                        tr.then_inc(tr_ready, 1)
                    for d in range(2):
                        u = 2 * i + d
                        pe.wait_ge(qT_ready, u + 1)
                        pe.wait_ge(kT_ready, u + 1)
                        for h in range(H):
                            rows = slice((h % 2) * DH, (h % 2 + 1) * DH)
                            mm = pe.matmul(ps[d][:, 1 + h % 2, (h // 2) * P:(h // 2 + 1) * P], kT[rows, d, h // 2], qT[rows, d, h // 2],
                                           start=True, stop=True)
                        mm.then_inc(score_ready, 1)
                        for b in range(H // 2):
                            mm = pe.matmul(ps[d][:, 0, b * P:(b + 1) * P], ke[:, d, b * P:(b + 1) * P],
                                           qkv[:, bass.ds(tile[d], 1), 2 * GW + b * P:2 * GW + (b + 1) * P].rearrange("p t n -> p (t n)"),
                                           start=True, stop=True)
                        mm.then_inc(ds_ready, 1)
                    for d in range(2):
                        u = 2 * i + d
                        pe.wait_ge(at_ready, u + 1)
                        pe.wait_ge(mid_ready, 2 * u + 2)
                        for b in range(H // 2):
                            pe.matmul(ps[d][:, 3, b * P:(b + 1) * P], qT[:, d, b], mid[:, d, b].rearrange("p c n -> p (c n)"),
                                      start=True, stop=False)
                            for half in range(2):
                                c = b * P + half * DH
                                mm = pe.matmul(ps[d][:, 3, c:c + DH], at[:, d, half * (H // 2) + b],
                                               qkv[:, bass.ds(tile[d], 1), 2 * GW + c:2 * GW + c + DH].rearrange("p t n -> p (t n)"),
                                               start=False, stop=(half == 1))
                        mm.then_inc(o_ready, 1)
                steps(pe, body)


def gla_output(nc, keep, a, scratch):
    with ExitStack() as ctx:
        s = Space(nc, ctx, "glo")
        of, ob, gg, o, sq, ex, e1, rec, si, on, og, out = (s.sb(n, [P, 2, GW]) for n in (
            "of", "ob", "gg", "o", "sq", "ex", "e1", "rec", "si", "on", "og", "out"))
        gain = s.sb("gain", [P, DH])
        ssq, ms, rstd = (s.sb(n, [P, 2, H]) for n in ("ssq", "ms", "rstd"))
        (o_ready, sq_ready, ssq_ready, ms_ready, rstd_ready, ex_ready, e1_ready, rec_ready, si_ready, on_ready, og_ready,
         out_ready, gain_in) = (s.sem(n) for n in (
             "o_ready", "sq_ready", "ssq_ready", "ms_ready", "rstd_ready", "ex_ready", "e1_ready", "rec_ready", "si_ready",
             "on_ready", "og_ready", "out_ready", "gain_in"))
        loaded = [s.sem(f"loaded{j}") for j in range(2)]
        stored = [s.sem(f"stored{j}") for j in range(2)]

        def loop(eng, body):
            body(0, True)
            with eng.Fori(1, NT // 2) as i:
                body(i, False)

        def heads(x):
            return x.rearrange("p (h d) -> p h d", d=DH)

        with nc.Block() as block:

            @block.sync
            def _(sp):
                sp.dma_start(gain[:, :], a["gla_norm"].broadcast_to([P, DH])).then_inc(gain_in, 16)

                def load(i, j, first):
                    t = 2 * i + j
                    if not first:
                        sp.wait_ge(out_ready, t - 1)
                    sp.dma_start(of[:, j], scratch["o"][0, tile_rows(t), :]).then_inc(loaded[j], 16)
                    sp.dma_start(ob[:, j], scratch["o"][1, tile_rows(t), :]).then_inc(loaded[j], 16)
                    sp.dma_start(gg[:, j], scratch["proj"][tile_rows(t), C_GG:C_LR]).then_inc(loaded[j], 16)

                def store(i, j):
                    t = 2 * i + j
                    sp.wait_ge(out_ready, t + 1)
                    sp.dma_start(scratch["mix"][tile_rows(t), 0:GW], out[:, j]).then_inc(stored[j], 16)
                for j in range(2):
                    load(0, j, True)
                with sp.Fori(1, NT // 2) as i:
                    for j in range(2):
                        load(i, j, False)
                        store(i - 1, j)
                for j in range(2):
                    store(NT // 2 - 1, j)
                for j in range(2):
                    sp.wait_ge(stored[j], 16 * NT // 2)

            @block.gpsimd
            def _(pool):
                def body(i, first):
                    for j in range(2):
                        t = 2 * i + j
                        pool.wait_ge(loaded[j], 48 * i + 48)
                        if not first:
                            pool.wait_ge(on_ready, t - 1)
                        pool.tensor_tensor(o[:, j], of[:, j], ob[:, j], ALU.add).then_inc(o_ready, 1)
                        pool.wait_ge(o_ready, t + 1)
                        if not first:
                            pool.wait_ge(ssq_ready, t - 1)
                        pool.tensor_tensor(sq[:, j], o[:, j], o[:, j], ALU.mult).then_inc(sq_ready, 1)
                    for j in range(2):
                        t = 2 * i + j
                        pool.wait_ge(ssq_ready, t + 1)
                        pool.tensor_tensor(ms[:, j], ssq[:, j], keep["eps_h"][:, 0:H], ALU.add).then_inc(ms_ready, 1)
                        pool.wait_ge(ms_ready, t + 1)
                        if not first:
                            pool.wait_ge(on_ready, t - 1)
                        pool.tensor_tensor(rstd[:, j], ms[:, j], keep["minus_half"][:, 0:H], ALU.pow).then_inc(rstd_ready, 1)
                loop(pool, body)

            @block.scalar
            def _(act):
                def body(i, first):
                    for j in range(2):
                        act.wait_ge(loaded[j], 48 * i + 48)
                        if not first:
                            act.wait_ge(e1_ready, 2 * i + j - 1)
                        act.activation(ex[:, j], gg[:, j], ACT.Exp, scale=-1.0).then_inc(ex_ready, 1)
                loop(act, body)

            @block.vector
            def _(dve):
                dve.wait_ge(gain_in, 16)

                def body(i, first):
                    for j in range(2):
                        t = 2 * i + j
                        dve.wait_ge(ex_ready, t + 1)
                        dve.tensor_scalar(e1[:, j], ex[:, j], 1.0, None, ALU.add).then_inc(e1_ready, 1)
                        dve.wait_ge(e1_ready, t + 1)
                        dve.reciprocal(rec[:, j], e1[:, j]).then_inc(rec_ready, 1)
                        dve.wait_ge(rec_ready, t + 1)
                        dve.tensor_tensor(si[:, j], gg[:, j], rec[:, j], ALU.mult).then_inc(si_ready, 1)
                        dve.wait_ge(sq_ready, t + 1)
                        dve.tensor_reduce(ssq[:, j], heads(sq[:, j]), AX_X, ALU.add).then_inc(ssq_ready, 1)
                    for j in range(2):
                        t = 2 * i + j
                        dve.wait_ge(rstd_ready, t + 1)
                        dve.scalar_tensor_tensor(heads(on[:, j]), heads(o[:, j]), DH ** 0.5,
                                                 rstd[:, j].unsqueeze(2).broadcast_to([P, H, DH]),
                                                 ALU.mult, ALU.mult).then_inc(on_ready, 1)
                        dve.wait_ge(on_ready, t + 1)
                        dve.tensor_tensor(heads(og[:, j]), heads(on[:, j]), gain[:, :].unsqueeze(1).broadcast_to([P, H, DH]),
                                          ALU.mult).then_inc(og_ready, 1)
                        dve.wait_ge(og_ready, t + 1)
                        dve.wait_ge(si_ready, t + 1)
                        if not first:
                            dve.wait_ge(stored[j], 16 * i)
                        dve.tensor_tensor(out[:, j], og[:, j], si[:, j], ALU.mult).then_inc(out_ready, 1)
                loop(dve, body)


def attention(nc, keep, a, scratch, outs):
    NL, NC = 3, PAST // P
    NX = H + KV
    WX = NX * DH
    PAD = NTP
    SLOTS = NT + 2
    with ExitStack() as ctx:
        s = Space(nc, ctx, "att")
        qT = s.sb("qT", [P, H // 2, T])
        kT = s.sb("kT", [P, KV, SLOTS * P])
        kcT = s.sb("kcT", [P, KV, PAST])
        v = s.sb("v", [P, SLOTS, KV * DH])
        vc = s.sb("vc", [P, NC, KV, DH])
        sink = s.sb("sink", [P, H])
        nsink = s.sb("nsink", [P, H])
        win = s.sb("win", [P, 2 * TS], BF16)
        identb = s.sb("identb", [P, P], BF16)

        with ExitStack() as inner:
            s1 = Space(nc, inner, "prep")
            x = s1.sb("x", [P, 2, WX + KV * DH])
            sq = s1.sb("sq", [P, 2, WX])
            ssq, ms, rstd = (s1.sb(n, [P, 2, NX]) for n in ("ssq", "ms", "rstd"))
            xn = s1.sb("xn", [P, 2, WX])
            xg = s1.sb("xg", [P, 2, WX])
            xc = s1.sb("xc", [P, 2, WX])
            xs = s1.sb("xs", [P, 2, WX])
            xr = s1.sb("xr", [P, 2, GW + 2 * KV * DH])
            gain = s1.sb("gain", [P, NX, DH])
            rope = s1.sb("rope", [P, NT, 2 * DH])
            winf = s1.sb("winf", [P, 2 * TS])
            kc = s1.sb("kc", [P, NC, KV, 2, DH])
            tr = s1.ps("tr", [P, 2, 2, HALF])
            trc = s1.ps("trc", [P, 2, HALF])
            const_in, x_const, padded, tables, ctx_ready = (s1.sem(n) for n in ("const_in", "x_const", "padded", "tables", "ctx_ready"))
            x_in = [s1.sem(f"x_in{j}") for j in range(2)]
            kv_out = s1.sem("kv_out")
            (sq_ready, ssq_ready, ms_ready, rstd_ready, xn_ready, xg_ready, xc_ready, xs_ready, xr_ready, v_ready, tr_ready,
             T_ready) = (s1.sem(n) for n in (
                 "sq_ready", "ssq_ready", "ms_ready", "rstd_ready", "xn_ready", "xg_ready", "xc_ready", "xs_ready", "xr_ready",
                 "v_ready", "tr_ready", "T_ready"))
            CONSTS = NX + 3 + 3 * KV

            def heads(y):
                return y.rearrange("p (h d) -> p h d", d=DH)

            def axes(y):
                return y.rearrange("p (h a b f) -> p h a b f", a=2, b=2, f=DH // 4)

            with nc.Block() as block:

                @block.sync
                def _(sp):
                    for h in range(NX):
                        sp.dma_start(gain[:, h], a["q_norm" if h < H else "k_norm"].broadcast_to([P, DH])).then_inc(const_in, 16)
                    sp.dma_start(rope[:, :, :], a["rope"].rearrange("(t p) c d -> p t (c d)", p=P)).then_inc(const_in, 16)

                    def load(i, j, first):
                        t = 2 * i + j
                        if not first:
                            sp.wait_ge(xn_ready, t - 1)
                            sp.wait_ge(sq_ready, t - 1)
                            sp.wait_ge(v_ready, t - 1)
                        sp.dma_start(x[:, j], scratch["proj"][tile_rows(t), C_SQ:DIN]).then_inc(x_in[j], 16)
                    for j in range(2):
                        load(0, j, True)
                    sp.dma_start(winf[:, :], a["window"]).then_inc(const_in, 16)
                    sp.dma_start(sink[:, :], a["sink"].broadcast_to([P, H])).then_inc(const_in, 16)
                    for dup in range(2):
                        for kv in range(KV):
                            sp.dma_start(kc[:, :, kv, dup, :], a["cache_k"][0, 0, kv].rearrange("(b p) d -> p b d", p=P)).then_inc(const_in, 16)
                    for kv in range(KV):
                        sp.dma_start(vc[:, :, kv, :], a["cache_v"][0, 0, kv].rearrange("(b p) d -> p b d", p=P)).then_inc(const_in, 16)
                    for j in range(NTP):
                        sp.wait_ge(xg_ready, j + 1)
                        for kv in range(KV):
                            sp.dma_start(outs[2][0, 0, kv, j * P:(j + 1) * P, :], xg[:, j, GW + kv * DH:GW + (kv + 1) * DH]).then_inc(kv_out, 16)
                            sp.dma_start(outs[3][0, 0, kv, j * P:(j + 1) * P, :], x[:, j, WX + kv * DH:WX + (kv + 1) * DH]).then_inc(kv_out, 16)
                    sp.wait_ge(kv_out, 16 * 2 * KV * NTP)
                    with sp.Fori(1, NT // 2) as i:
                        for j in range(2):
                            load(i, j, False)

                @block.gpsimd
                def _(pool):
                    pool.wait_ge(const_in, 16 * (NX + 1))

                    def body(i, cond, first):
                        for j in range(2):
                            t = 2 * i + j
                            pool.wait_ge(x_in[j], 16 * i + 16)
                            if not first:
                                pool.wait_ge(ssq_ready, t - 1)
                            pool.tensor_tensor(sq[:, j], x[:, j, 0:WX], x[:, j, 0:WX], ALU.mult).then_inc(sq_ready, 1)
                        for j in range(2):
                            t = 2 * i + j
                            pool.wait_ge(ssq_ready, t + 1)
                            pool.tensor_tensor(ms[:, j], ssq[:, j], keep["eps_h"][:, 0:NX], ALU.add).then_inc(ms_ready, 1)
                            pool.wait_ge(ms_ready, t + 1)
                            pool.tensor_tensor(rstd[:, j], ms[:, j], keep["minus_half"][:, 0:NX], ALU.pow).then_inc(rstd_ready, 1)
                        for j in range(2):
                            t = 2 * i + j
                            pool.wait_ge(xn_ready, t + 1)
                            if not first:
                                pool.wait_ge(kv_out, 16 * 2 * KV * NTP)
                                pool.wait_ge(xc_ready, t - 1)
                            pool.tensor_tensor(xg[:, j], xn[:, j], gain[:, :, :].rearrange("p h d -> p (h d)"), ALU.mult).then_inc(xg_ready, 1)
                            pool.wait_ge(xg_ready, t + 1)
                            if not first:
                                pool.wait_ge(xr_ready, 2 * t - 2)
                            sin = axes(rope[:, bass.ds(t, 1), DH:2 * DH].rearrange("p t d -> p (t d)"))
                            for b in range(2):
                                pool.tensor_tensor(axes(xs[:, j])[:, :, :, b], axes(xg[:, j])[:, :, :, 1 - b],
                                                   sin[:, :, :, b].broadcast_to([P, NX, 2, DH // 4]), ALU.mult).then_inc(xs_ready, 1)
                    pairs(pool, body)

                @block.vector
                def _(dve):
                    dve.memset(kT[:, :, PAD * P:(PAD + 1) * P], 0.0).then_inc(padded, 1)
                    dve.memset(kT[:, :, (SLOTS - 1) * P:SLOTS * P], 0.0).then_inc(padded, 1)
                    dve.memset(v[:, PAD], 0.0).then_inc(padded, 1)
                    dve.memset(v[:, SLOTS - 1], 0.0).then_inc(padded, 1)
                    dve.tensor_copy(identb[:, :], keep["ident"]).then_inc(tables, 1)
                    dve.wait_ge(const_in, 16 * CONSTS)
                    dve.tensor_scalar(nsink[:, :], sink[:, :], -1.0, None, ALU.mult).then_inc(tables, 1)
                    dve.tensor_copy(win[:, :], winf[:, :]).then_inc(tables, 1)
                    dve.wait_ge(x_const, 1)
                    dve.tensor_copy(kcT[:, :, :], trc[:, :, :]).then_inc(ctx_ready, 1)

                    def body(i, cond, first):
                        for j in range(2):
                            t = 2 * i + j
                            dve.wait_ge(sq_ready, t + 1)
                            if not first:
                                dve.wait_ge(ms_ready, t - 1)
                            dve.tensor_reduce(ssq[:, j], heads(sq[:, j]), AX_X, ALU.add).then_inc(ssq_ready, 1)
                            if not first:
                                dve.wait_ge(tr_ready, t - 1)
                            dve.tensor_copy(v[:, bass.ds(t + cond, 1), :].rearrange("p t d -> p (t d)"), x[:, j, WX:WX + KV * DH]).then_inc(v_ready, 1)
                        for j in range(2):
                            t = 2 * i + j
                            dve.wait_ge(rstd_ready, t + 1)
                            if not first:
                                dve.wait_ge(xg_ready, t - 1)
                            dve.scalar_tensor_tensor(heads(xn[:, j]), heads(x[:, j, 0:WX]), DH ** 0.5,
                                                     rstd[:, j].unsqueeze(2).broadcast_to([P, NX, DH]), ALU.mult, ALU.mult).then_inc(xn_ready, 1)
                        for j in range(2):
                            t = 2 * i + j
                            dve.wait_ge(xg_ready, t + 1)
                            if not first:
                                dve.wait_ge(xr_ready, 2 * t - 2)
                            dve.tensor_tensor(heads(xc[:, j]), heads(xg[:, j]),
                                              rope[:, bass.ds(t, 1), 0:DH].broadcast_to([P, NX, DH]), ALU.mult).then_inc(xc_ready, 1)
                            dve.wait_ge(xc_ready, t + 1)
                            dve.wait_ge(xs_ready, 2 * t + 2)
                            if not first:
                                dve.wait_ge(tr_ready, t - 1)
                            dve.tensor_tensor(xr[:, j, 0:GW], xc[:, j, 0:GW], xs[:, j, 0:GW], ALU.add).then_inc(xr_ready, 1)
                            dve.tensor_tensor(xr[:, j, GW:].rearrange("p (k c d) -> p k c d", k=KV, c=2),
                                              heads(xc[:, j, GW:WX]).unsqueeze(2).broadcast_to([P, KV, 2, DH]),
                                              heads(xs[:, j, GW:WX]).unsqueeze(2).broadcast_to([P, KV, 2, DH]), ALU.add).then_inc(xr_ready, 1)
                    pairs(dve, body)
                    dve.wait_ge(T_ready, 2 * NT)

                @block.scalar
                def _(act):
                    def body(i, cond, first):
                        for j in range(2):
                            t = 2 * i + j
                            act.wait_ge(tr_ready, t + 1)
                            act.activation(qT[:, :, tile_rows(t)], tr[:, j, 0].rearrange("p (b c) -> p b c", c=P), ACT.Copy).then_inc(T_ready, 1)
                            act.activation(kT[:, :, bass.ds((t + cond) * P, P)], tr[:, j, 1, 0:KV * P].rearrange("p (b c) -> p b c", c=P),
                                           ACT.Copy).then_inc(T_ready, 1)
                    pairs(act, body)

                @block.tensor
                def _(pe):
                    pe.wait_ge(const_in, 16 * CONSTS)
                    for kv in range(KV):
                        for b in range(NC):
                            mm = pe.transpose(trc[:, kv, b * P:(b + 1) * P], kc[:, b, kv].rearrange("p c d -> p (c d)"), keep["ident"])
                    mm.then_inc(x_const, 1)

                    def body(i, cond, first):
                        for j in range(2):
                            t = 2 * i + j
                            pe.wait_ge(xr_ready, 2 * t + 2)
                            if not first:
                                pe.wait_ge(T_ready, 2 * t - 2)
                            for b in range(H // 2 + KV):
                                mm = pe.transpose(tr[:, j, b // 4, (b % 4) * P:(b % 4 + 1) * P], xr[:, j, b * P:(b + 1) * P], keep["ident"])
                            mm.then_inc(tr_ready, 1)
                    pairs(pe, body)

        with ExitStack() as inner:
            s2 = Space(nc, inner, "soft")
            q = [s2.sb(f"q{j}", [P, H // 2, P]) for j in range(2)]
            kw = [s2.sb(f"kw{j}", [P, KV, NL * P]) for j in range(2)]
            prob = s2.sb("prob", [P, 2, (NC + NL) * P])
            pT = s2.sb("pT", [P, 2, 8, P])
            top = s2.sb("top", [P, 2, H])
            bias = s2.sb("bias", [P, 2, H])
            total = s2.sb("total", [P, 2, H])
            sb_in, sb_out, den, inv = (s2.sb(n, [P, 2, H]) for n in ("sb_in", "sb_out", "den", "inv"))
            o = s2.sb("o", [P, 2, GW])
            score = s2.ps("score", [P, 2, 2 * HALF])
            pTp = s2.ps("pTp", [P, 8, P])
            op = s2.ps("op", [P, 2, HALF])
            (q_ready, kw_ready, s_ready, top_ready, bias_ready, p_ready, pTp_ready, pTa_ready, pTd_ready, pv_ready, sin_ready, sout_ready,
             den_ready, inv_ready, o_ready) = (s2.sem(n) for n in (
                 "q_ready", "kw_ready", "s_ready", "top_ready", "bias_ready", "p_ready", "pTp_ready", "pTa_ready", "pTd_ready", "pv_ready",
                 "sin_ready", "sout_ready", "den_ready", "inv_ready", "o_ready"))
            stored = [s2.sem(f"stored{j}") for j in range(2)]
            UNITS = 2 * H

            def tile_pairs(eng, body):
                body(0, 0, False)
                with eng.Fori(0, TS // P // 2) as i:
                    body(i + 1, i, True)

            def softmax_span(sample):
                return slice(0, (NC + NL) * P) if sample else slice(HALF, HALF + NTP * P)

            def blocks(sample):
                if sample:
                    return [(b * P, b) for b in range(NC + NL)]
                return [(HALF, 0), (HALF + P, NC)]

            def evac_slots(sample, engine):
                if sample:
                    return (slice(0, NC), slice(NC, NC + NL))[engine]
                return (slice(0, 1), slice(NC, NC + 1))[engine]

            with nc.Block() as block:

                @block.sync
                def _(sp):
                    def body(i, si, sample):
                        for j in range(2):
                            sp.wait_ge(o_ready, 2 * i + j + 1)
                            sp.dma_start(scratch["mix"][bass.ds((2 * i + j) * P, P), GW:2 * GW], o[:, j]).then_inc(stored[j], 16)
                    tile_pairs(sp, body)
                    for j in range(2):
                        sp.wait_ge(stored[j], 16 * NT // 2)

                @block.gpsimd
                def _(pool):
                    def body(i, si, sample):
                        for j in range(2):
                            if sample:
                                pool.wait_ge(s_ready, UNITS * i - UNITS + H * j + H)
                            pool.tensor_copy(q[j][:, :, :], qT[:, :, bass.ds((2 * i + j) * P, P)]).then_inc(q_ready, 1)
                            if sample:
                                pool.tensor_copy(kw[j][:, :, :], kT[:, :, bass.ds((PAD + 2 * si + j) * P, NL * P)]).then_inc(kw_ready, 1)
                    tile_pairs(pool, body)

                @block.tensor
                def _(pe):
                    def body(i, si, sample):
                        def scores(n):
                            j, h = n // H, n % H
                            rows = slice((h % 2) * DH, (h % 2 + 1) * DH)
                            kv = h // (H // KV)
                            if h == 0:
                                pe.wait_ge(q_ready, 2 * i + j + 1)
                                if sample:
                                    pe.wait_ge(kw_ready, 2 * si + j + 1)
                            if sample or n >= 2:
                                pe.wait_ge(p_ready, UNITS * i + n - 1)
                            if sample:
                                st = 2 * si + j
                                pe.matmul(score[:, n % 2, 0:PAST], q[j][rows, h // 2], kcT[rows, kv], start=True, stop=True)
                                loc = score[:, n % 2, HALF:HALF + NL * P]
                                pe.matmul(loc, q[j][rows, h // 2], kw[j][rows, kv], start=True, stop=False)
                                pe.matmul(loc[:, 0:P], identb[:, :], win[:, bass.ds(st * P, P)], start=False, stop=False)
                                mm = pe.matmul(loc[:, 2 * P:3 * P], identb[:, :], win[:, bass.ds(TS + st * P, P)], start=False, stop=True)
                            else:
                                mm = pe.matmul(score[:, n % 2, HALF:HALF + TP], q[j][rows, h // 2], kT[rows, kv, 0:TP], start=True, stop=True)
                            mm.then_inc(s_ready, 1)

                        def turn(n):
                            pe.wait_ge(p_ready, UNITS * i + n + 1)
                            if sample or n >= 1:
                                pe.wait_ge(pTa_ready, UNITS * i + n)
                                pe.wait_ge(pTd_ready, UNITS * i + n)
                            for col, slot in blocks(sample):
                                mm = pe.transpose(pTp[:, slot], prob[:, n % 2, col:col + P] if sample else prob[:, n % 2, col - HALF:col - HALF + P],
                                                  keep["ident"])
                            mm.then_inc(pTp_ready, 1)

                        def values(n):
                            j, h = n // H, n % H
                            kv = h // (H // KV)
                            if h == 0 and sample:
                                pe.wait_ge(o_ready, 2 * i + j - 1)
                            pe.wait_ge(pTa_ready, UNITS * i + n + 1)
                            pe.wait_ge(pTd_ready, UNITS * i + n + 1)
                            every = blocks(sample)
                            for m, (col, slot) in enumerate(every):
                                if sample and slot < NC:
                                    rhs = vc[:, slot, kv]
                                else:
                                    first = PAD + 2 * si + j if sample else 0
                                    off = slot - NC if sample else m
                                    rhs = v[:, bass.ds(first + off, 1), kv * DH:(kv + 1) * DH].rearrange("p t d -> p (t d)")
                                mm = pe.matmul(op[:, j, h * DH:(h + 1) * DH], pT[:, n % 2, slot], rhs,
                                               start=(m == 0), stop=(m == len(every) - 1))
                            mm.then_inc(pv_ready, 1)

                        scores(0)
                        for n in range(UNITS):
                            if n + 1 < UNITS:
                                scores(n + 1)
                            turn(n)
                            if n:
                                values(n - 1)
                        values(UNITS - 1)
                    tile_pairs(pe, body)

                @block.scalar
                def _(act):
                    def body(i, si, sample):
                        span = softmax_span(sample)

                        def evac(n):
                            act.wait_ge(pTp_ready, UNITS * i + n + 1)
                            if sample or n >= 2:
                                act.wait_ge(pv_ready, UNITS * i + n - 1)
                            sl = evac_slots(sample, 0)
                            act.activation(pT[:, n % 2, sl], pTp[:, sl], ACT.Copy).then_inc(pTa_ready, 1)

                        def sink_term(j):
                            act.wait_ge(sin_ready, 2 * i + j + 1)
                            act.activation(sb_out[:, j], sb_in[:, j], ACT.Exp).then_inc(sout_ready, 1)

                        for n in range(UNITS):
                            j, h = n // H, n % H
                            act.wait_ge(bias_ready, UNITS * i + n + 1)
                            if sample or n >= 2:
                                act.wait_ge(pTp_ready, UNITS * i + n - 1)
                            if h == 0 and sample:
                                act.wait_ge(den_ready, 2 * i + j - 1)
                            act.activation(prob[:, n % 2, 0:span.stop - span.start], score[:, n % 2, span], ACT.Exp,
                                           bias=bias[:, j, h:h + 1], scale=DH ** -0.5, accum_out=total[:, j, h:h + 1]).then_inc(p_ready, 1)
                            if n:
                                evac(n - 1)
                            if n == H + 1:
                                sink_term(0)
                        evac(UNITS - 1)
                        sink_term(1)
                    tile_pairs(act, body)

                @block.vector
                def _(dve):
                    def body(i, si, sample):
                        span = softmax_span(sample)

                        def evac(n):
                            dve.wait_ge(pTp_ready, UNITS * i + n + 1)
                            if sample or n >= 2:
                                dve.wait_ge(pv_ready, UNITS * i + n - 1)
                            sl = evac_slots(sample, 1)
                            dve.tensor_copy(pT[:, n % 2, sl], pTp[:, sl]).then_inc(pTd_ready, 1)

                        def sink_in(j):
                            dve.wait_ge(bias_ready, UNITS * i + H * j + H)
                            dve.tensor_tensor(sb_in[:, j], sink[:, :], bias[:, j], ALU.add).then_inc(sin_ready, 1)

                        def finish(j):
                            dve.wait_ge(sout_ready, 2 * i + j + 1)
                            dve.wait_ge(p_ready, UNITS * i + H * j + H)
                            dve.tensor_tensor(den[:, j], sb_out[:, j], total[:, j], ALU.add).then_inc(den_ready, 1)
                            dve.wait_ge(den_ready, 2 * i + j + 1)
                            dve.reciprocal(inv[:, j], den[:, j]).then_inc(inv_ready, 1)
                            dve.wait_ge(inv_ready, 2 * i + j + 1)
                            dve.wait_ge(pv_ready, UNITS * i + H * j + H)
                            if sample:
                                dve.wait_ge(stored[j], 16 * i)
                            dve.tensor_tensor(o[:, j].rearrange("p (h d) -> p h d", d=DH), op[:, j].rearrange("p (h d) -> p h d", d=DH),
                                              inv[:, j].unsqueeze(2).broadcast_to([P, H, DH]), ALU.mult).then_inc(o_ready, 1)

                        for n in range(UNITS):
                            j, h = n // H, n % H
                            dve.wait_ge(s_ready, UNITS * i + n + 1)
                            dve.tensor_reduce(top[:, j, h:h + 1], score[:, n % 2, span], AX_X, ALU.max).then_inc(top_ready, 1)
                            dve.wait_ge(top_ready, UNITS * i + n + 1)
                            if h == 0 and sample:
                                dve.wait_ge(sin_ready, 2 * i + j - 1)
                            dve.tensor_scalar(bias[:, j, h:h + 1], top[:, j, h:h + 1], -DH ** -0.5, nsink[:, h:h + 1], ALU.mult, ALU.min).then_inc(bias_ready, 1)
                            if n:
                                evac(n - 1)
                            if n == H:
                                sink_in(0)
                            if n == H + 2:
                                finish(0)
                        evac(UNITS - 1)
                        sink_in(1)
                        finish(1)
                    tile_pairs(dve, body)


def merge(nc, keep, a, scratch, hi, lo):
    WC = P
    NW = D // WC
    with ExitStack() as ctx:
        s = Space(nc, ctx, "mrg")
        st = NormStage(s, keep, 1, hi, lo, slots=1)
        raw = s.sb("raw", [P, 2, KD, WC])
        whi = s.sb("whi", [P, KD, D], F32R)
        wlo = s.sb("wlo", [P, KD, D], F32R)
        mix = s.sb("mix", [P, 2, D])
        mhi = s.sb("mhi", [P, KD, P], F32R)
        mlo = s.sb("mlo", [P, KD, P], F32R)
        gate = s.sb("gate", [P, 2, D])
        mT = s.ps("mT", [P, KD, P])
        acc = s.ps("acc", [P, 2, HALF])
        w_in = [s.sem(f"w_in{j}") for j in range(2)]
        x_in = [s.sem(f"x_in{j}") for j in range(2)]
        mix_in = [s.sem(f"mix_in{j}") for j in range(2)]
        x1_out = [s.sem(f"x1_out{j}") for j in range(2)]
        (gate_in, whi_ready, wlo_ready, mT_ready, mhi_ready, mlo_ready, acc_ready, gated, x1_ready) = (s.sem(n) for n in (
            "gate_in", "whi_ready", "wlo_ready", "mT_ready", "mhi_ready", "mlo_ready", "acc_ready", "gated", "x1_ready"))
        wv = a["w_o"][0].rearrange("(k p) n -> p k n", p=P)
        with nc.Block() as block:

            @block.sync
            def _(sp):
                def load(i, j, cond, first):
                    t = 2 * i + j
                    if not first:
                        sp.wait_ge(mT_ready, t - 1)
                        sp.wait_ge(st.xn_ready, t - 1)
                    sp.dma_start(mix[:, j], scratch["mix"][tile_rows(t), :]).then_inc(mix_in[j], 16)
                    if not first:
                        sp.wait_ge(x1_out[j], 16 * i)
                    src = a["x_prompt"][0, tile_rows(t), :] if cond == 0 else a["x_sample"][0, bass.ds((t - NTP) * P, P), :]
                    sp.dma_start(st.x[:, j], src).then_inc(x_in[j], 16)

                def store(i, j):
                    t = 2 * i + j
                    sp.wait_ge(x1_ready, t + 1)
                    sp.dma_start(scratch["x1"][tile_rows(t), :], st.x[:, j]).then_inc(x1_out[j], 16)
                for n in range(2):
                    sp.dma_start(raw[:, n], wv[:, :, n * WC:(n + 1) * WC]).then_inc(w_in[n], 16)
                for j in range(2):
                    load(0, j, 0, True)
                for c in range(2):
                    sp.dma_start(gate[:, c], scratch["mod"][c:c + 1, 2 * D:3 * D].broadcast_to([P, D])).then_inc(gate_in, 16)
                for n in range(2, NW):
                    sp.wait_ge(wlo_ready, n - 1)
                    sp.dma_start(raw[:, n % 2], wv[:, :, n * WC:(n + 1) * WC]).then_inc(w_in[n % 2], 16)
                for j in range(2):
                    store(0, j)
                with sp.Fori(1, NT // 2) as i:
                    for j in range(2):
                        load(i, j, 1, False)
                    for j in range(2):
                        store(i, j)
                for j in range(2):
                    sp.wait_ge(x1_out[j], 16 * NT // 2)

            @block.scalar
            def _(act):
                for n in range(NW):
                    act.wait_ge(w_in[n % 2], 16 * (n // 2 + 1))
                    act.activation(whi[:, :, n * WC:(n + 1) * WC], raw[:, n % 2], ACT.Copy).then_inc(whi_ready, 1)

                def body(i, cond, first):
                    for j in range(2):
                        t = 2 * i + j
                        act.wait_ge(mT_ready, t + 1)
                        if not (first and j == 0):
                            act.wait_ge(acc_ready, t)
                        act.activation(mhi[:, :, :], mT[:, :, :], ACT.Copy).then_inc(mhi_ready, 1)
                    for j in range(2):
                        st.act_square(act, i, j, x1_ready, 2 * i + j + 1, first)
                    for j in range(2):
                        st.act_hi(act, i, j)
                pairs(act, body)

            @block.gpsimd
            def _(pool):
                for n in range(NW):
                    pool.wait_ge(whi_ready, n + 1)
                    at = slice(n * WC, (n + 1) * WC)
                    pool.tensor_tensor(wlo[:, :, at], raw[:, n % 2], hi_view(whi)[:, :, at], ALU.subtract).then_inc(wlo_ready, 1)

                def body(i, cond, first):
                    for j in range(2):
                        st.pool_rstd(pool, i, j)
                    for j in range(2):
                        st.pool_lo(pool, i, j)
                pairs(pool, body)

            @block.vector
            def _(dve):
                dve.wait_ge(gate_in, 32)

                def body(i, cond, first):
                    for j in range(2):
                        t = 2 * i + j
                        dve.wait_ge(mhi_ready, t + 1)
                        if not (first and j == 0):
                            dve.wait_ge(acc_ready, t)
                        dve.tensor_tensor(mlo[:, :, :], mT[:, :, :], hi_view(mhi), ALU.subtract).then_inc(mlo_ready, 1)
                        dve.wait_ge(acc_ready, t + 1)
                        if not first:
                            dve.wait_ge(st.xT_ready, t - 1)
                        dve.tensor_tensor(st.xn[:, j], acc[:, :, :].rearrange("p a b -> p (a b)"), gate[:, cond], ALU.mult).then_inc(gated, 1)
                        dve.wait_ge(gated, t + 1)
                        dve.wait_ge(x_in[j], 16 * i + 16)
                        dve.tensor_tensor(st.x[:, j], st.x[:, j], st.xn[:, j], ALU.add).then_inc(x1_ready, 1)
                    for j in range(2):
                        st.dve_xn(dve, i, j, first)
                    for j in range(2):
                        st.dve_modulate(dve, i, j, cond, first)
                pairs(dve, body)

            @block.tensor
            def _(pe):
                def body(i, cond, first):
                    for j in range(2):
                        t = 2 * i + j
                        pe.wait_ge(mix_in[j], 16 * i + 16)
                        if not (first and j == 0):
                            pe.wait_ge(mlo_ready, t)
                        for k in range(KD):
                            mm = pe.transpose(mT[:, k], mix[:, j, k * P:(k + 1) * P], keep["ident"])
                        mm.then_inc(mT_ready, 1)
                        pe.wait_ge(mlo_ready, t + 1)
                        if first and j == 0:
                            pe.wait_ge(wlo_ready, NW)
                        else:
                            pe.wait_ge(gated, t)
                        for half in range(2):
                            at = slice(half * HALF, (half + 1) * HALF)
                            for k in range(KD):
                                pe.matmul(acc[:, half], mhi[:, k], whi[:, k, at], start=(k == 0), stop=False)
                                pe.matmul(acc[:, half], mhi[:, k], wlo[:, k, at], start=False, stop=False)
                                mm = pe.matmul(acc[:, half], mlo[:, k], whi[:, k, at], start=False, stop=(k == KD - 1))
                        mm.then_inc(acc_ready, 1)
                    for j in range(2):
                        st.pe_transpose(pe, i, j, first)
                pairs(pe, body)


def feed_forward(nc, a, scratch, hi, lo, outs):
    NF = DFF // P
    BLOCKS = ((0, HALF), (HALF, 2 * HALF), (2 * HALF, T))
    NB = len(BLOCKS)
    RING = 5
    with ExitStack() as ctx:
        s = Space(nc, ctx, "ff")
        acc = s.sb("acc", [P, NT, D])
        raw1 = s.sb("raw1", [P, 2, KD, P])
        raw2 = s.sb("raw2", [P, 2, D])
        w1hi, w1lo = ([s.sb(f"w1{n}{j}", [P, KD, P], F32R) for j in range(2)] for n in ("hi", "lo"))
        w2hi, w2lo = ([s.sb(f"w2{n}{j}", [P, D], F32R) for j in range(2)] for n in ("hi", "lo"))
        uhi, ulo = ([s.sb(f"u{n}{j}", [P, T], F32R) for j in range(2)] for n in ("hi", "lo"))
        relu = s.sb("relu", [P, 2, HALF])
        sq = s.sb("sq", [P, 2, HALF])
        up = s.ps("up", [P, NB, HALF])
        down = s.ps("down", [P, RING, HALF])
        w1_in = [s.sem(f"w1_in{j}") for j in range(2)]
        w2_in = [s.sem(f"w2_in{j}") for j in range(2)]
        (zeroed, w1hi_ready, w1lo_ready, w2hi_ready, w2lo_ready, up_ready, relu_ready, sq_ready, uhi_ready, ulo_ready,
         down_ready, added, gate_in, x1_in, gated, out_ready, stored) = (s.sem(n) for n in (
             "zeroed", "w1hi_ready", "w1lo_ready", "w2hi_ready", "w2lo_ready", "up_ready", "relu_ready", "sq_ready",
             "uhi_ready", "ulo_ready", "down_ready", "added", "gate_in", "x1_in", "gated", "out_ready", "stored"))
        w1v = a["w_ff1"][0].rearrange("(k p) n -> p k n", p=P)
        PER = 2 * NT
        gate = [relu[:, :, :].rearrange("p a b -> p (a b)"), sq[:, :, :].rearrange("p a b -> p (a b)")]
        x1 = [raw1[:, 0].rearrange("p k n -> p (k n)"), raw1[:, 1].rearrange("p k n -> p (k n)"), raw2[:, 0], raw2[:, 1]]

        def chunks(eng, body):
            with eng.Fori(0, NF // 2) as i:
                for j in range(2):
                    body(i, j)

        def store_tile(sp, t):
            sp.wait_ge(out_ready, t + 1)
            out = outs[0][0, t * P:(t + 1) * P, :] if t < NTP else outs[1][0, (t - NTP) * P:(t - NTP + 1) * P, :]
            sp.dma_start(out, acc[:, t]).then_inc(stored, 16)

        with nc.Block() as block:

            @block.sync
            def _(sp):
                def load(i, j):
                    c = 2 * i + j
                    sp.dma_start(raw1[:, j], w1v[:, :, bass.ds(c * P, P)]).then_inc(w1_in[j], 16)
                    sp.dma_start(raw2[:, j], a["w_ff2"][0, bass.ds(c * P, P), :]).then_inc(w2_in[j], 16)
                for j in range(2):
                    load(0, j)
                with sp.Fori(1, NF // 2) as i:
                    for j in range(2):
                        sp.wait_ge(w1lo_ready, 2 * i + j - 1)
                        sp.wait_ge(w2lo_ready, 2 * i + j - 1)
                        load(i, j)
                sp.wait_ge(ulo_ready, NB * NF)
                for cond in range(2):
                    sp.dma_start(gate[cond], scratch["mod"][cond:cond + 1, 5 * D:6 * D].broadcast_to([P, D])).then_inc(gate_in, 16)
                sp.wait_ge(w2lo_ready, NF)
                for t in range(NT):
                    if t >= len(x1):
                        sp.wait_ge(out_ready, t - len(x1) + 1)
                    sp.dma_start(x1[t % len(x1)], scratch["x1"][t * P:(t + 1) * P, :]).then_inc(x1_in, 16)
                    sp.wait_ge(x1_in, 16 * (t + 1))
                    if t >= 2:
                        store_tile(sp, t - 2)
                for t in range(NT - 2, NT):
                    store_tile(sp, t)
                sp.wait_ge(stored, 16 * NT)

            @block.scalar
            def _(act):
                def split(i, j, first):
                    c = 2 * i + j
                    act.wait_ge(w1_in[j], 16 * i + 16)
                    if not first:
                        act.wait_ge(up_ready, NB * (c - 1))
                    act.activation(w1hi[j][:, :, :], raw1[:, j], ACT.Copy).then_inc(w1hi_ready, 1)
                    act.wait_ge(w2_in[j], 16 * i + 16)
                    if not first:
                        act.wait_ge(down_ready, PER * (c - 1))
                    act.activation(w2hi[j][:, :], raw2[:, j], ACT.Copy).then_inc(w2hi_ready, 1)

                def hidden(i, j, first):
                    c = 2 * i + j
                    for b, (t0, t1) in enumerate(BLOCKS):
                        n = NB * c + b
                        m = (NB * j + b) % 2
                        w = t1 - t0
                        act.wait_ge(up_ready, n + 1)
                        if not (first and NB * j + b < 2):
                            act.wait_ge(sq_ready, n - 1)
                        act.activation(relu[:, m, 0:w], up[:, b, 0:w], ACT.Relu).then_inc(relu_ready, 1)
                        act.wait_ge(sq_ready, n + 1)
                        if not first:
                            act.wait_ge(down_ready, PER * (c - 1))
                        act.activation(uhi[j][:, t0:t1], sq[:, m, 0:w], ACT.Copy).then_inc(uhi_ready, 1)
                def body(i, first):
                    hidden(i, 1, first)
                    split(i + 1, 0, False)
                    hidden(i + 1, 0, False)
                    split(i + 1, 1, False)
                for j in range(2):
                    split(0, j, True)
                hidden(0, 0, True)
                body(0, True)
                with act.Fori(1, NF // 2 - 1) as i:
                    body(i, False)
                hidden(NF // 2 - 1, 1, False)

            @block.gpsimd
            def _(pool):
                def split(i, j):
                    c = 2 * i + j
                    pool.wait_ge(w1hi_ready, c + 1)
                    pool.tensor_tensor(w1lo[j][:, :, :], raw1[:, j], hi_view(w1hi[j]), ALU.subtract).then_inc(w1lo_ready, 1)
                    pool.wait_ge(w2hi_ready, c + 1)
                    pool.tensor_tensor(w2lo[j][:, :], raw2[:, j], w2hi[j][:, :].bitcast(F32), ALU.subtract).then_inc(w2lo_ready, 1)

                def hidden(i, j):
                    c = 2 * i + j
                    for b, (t0, t1) in enumerate(BLOCKS):
                        pool.wait_ge(uhi_ready, NB * c + b + 1)
                        pool.tensor_tensor(ulo[j][:, t0:t1], sq[:, (NB * j + b) % 2, 0:t1 - t0], uhi[j][:, t0:t1].bitcast(F32),
                                           ALU.subtract).then_inc(ulo_ready, 1)
                for j in range(2):
                    split(0, j)
                hidden(0, 0)
                with pool.Fori(0, NF // 2 - 1) as i:
                    hidden(i, 1)
                    split(i + 1, 0)
                    hidden(i + 1, 0)
                    split(i + 1, 1)
                hidden(NF // 2 - 1, 1)
                pool.wait_ge(gate_in, 32)
                for t in range(NT):
                    pool.wait_ge(x1_in, 16 * (t + 1))
                    pool.wait_ge(gated, 2 * (t + 1))
                    pool.tensor_tensor(acc[:, t], acc[:, t], x1[t % len(x1)], ALU.add).then_inc(out_ready, 1)

            @block.vector
            def _(dve):
                for t in range(NT):
                    dve.memset(acc[:, t], 0.0).then_inc(zeroed, 1)

                def square(c, b, j, first):
                    t0, t1 = BLOCKS[b]
                    n = NB * c + b
                    m = (NB * j + b) % 2
                    w = t1 - t0
                    dve.wait_ge(relu_ready, n + 1)
                    if not (first and NB * j + b < 2):
                        dve.wait_ge(ulo_ready, n - 1)
                    dve.tensor_tensor(sq[:, m, 0:w], relu[:, m, 0:w], relu[:, m, 0:w], ALU.mult).then_inc(sq_ready, 1)

                def add(c, t, half, first):
                    n = 2 * t + half
                    dve.wait_ge(down_ready, PER * c + n + 1)
                    at = slice(half * HALF, (half + 1) * HALF)
                    if not first:
                        dve.wait_ge(added, PER * (c - 1) + n + 1)
                    dve.tensor_tensor(acc[:, t, at], acc[:, t, at], down[:, n % RING], ALU.add).then_inc(added, 1)

                def body(i, j, first):
                    c = 2 * i + j
                    for t in range(NT):
                        for half in range(2):
                            if t in (0, 2, 4) and half == 0:
                                square(c + 1, t // 2, 1 - j, first and j == 0)
                            add(c, t, half, first and j == 0)
                for b in range(NB):
                    square(0, b, 0, True)
                dve.wait_ge(zeroed, NT)
                for j in range(2):
                    body(0, j, True)
                with dve.Fori(1, NF // 2 - 1) as i:
                    for j in range(2):
                        body(i, j, False)
                body(NF // 2 - 1, 0, False)
                c = NF - 1
                dve.wait_ge(gate_in, 32)
                for t in range(NT):
                    for half in range(2):
                        add(c, t, half, False)
                        at = slice(half * HALF, (half + 1) * HALF)
                        dve.wait_ge(added, PER * c + 2 * t + half + 1)
                        dve.tensor_tensor(acc[:, t, at], acc[:, t, at], gate[0 if t < NTP else 1][:, at], ALU.mult).then_inc(gated, 1)

            @block.tensor
            def _(pe):
                def first_product(c, i, j, first):
                    pe.wait_ge(w1lo_ready, c + 1)
                    for b, (t0, t1) in enumerate(BLOCKS):
                        if not first:
                            pe.wait_ge(relu_ready, NB * (c - 1) + b + 1)
                        out = up[:, b, 0:t1 - t0]
                        for k in range(KD):
                            pe.matmul(out, w1hi[j][:, k, :], hi[:, k, t0:t1], start=(k == 0), stop=False)
                            pe.matmul(out, w1hi[j][:, k, :], lo[:, k, t0:t1], start=False, stop=False)
                            mm = pe.matmul(out, w1lo[j][:, k, :], hi[:, k, t0:t1], start=False, stop=(k == KD - 1))
                        mm.then_inc(up_ready, 1)

                def second_product(c, j, first):
                    pe.wait_ge(w2lo_ready, c + 1)
                    for t in range(NT):
                        if t in (0, 4, 8):
                            pe.wait_ge(ulo_ready, NB * c + t // 4 + 1)
                        for half in range(2):
                            n = 2 * t + half
                            at = slice(half * HALF, (half + 1) * HALF)
                            if not (first and n < RING):
                                pe.wait_ge(added, PER * c + n - RING + 1)
                            out = down[:, n % RING]
                            x_hi, x_lo = (x[j][:, t * P:(t + 1) * P] for x in (uhi, ulo))
                            pe.matmul(out, x_hi, w2hi[j][:, at], start=True, stop=False)
                            pe.matmul(out, x_hi, w2lo[j][:, at], start=False, stop=False)
                            pe.matmul(out, x_lo, w2hi[j][:, at], start=False, stop=True).then_inc(down_ready, 1)

                first_product(0, 0, 0, True)
                first_product(1, 0, 1, False)
                second_product(0, 0, True)
                first_product(2, 1, 0, False)
                second_product(1, 1, False)
                with pe.Fori(1, NF // 2 - 1) as i:
                    first_product(2 * i + 1, i, 1, False)
                    second_product(2 * i, 0, False)
                    first_product(2 * i + 2, i + 1, 0, False)
                    second_product(2 * i + 1, 1, False)
                first_product(NF - 1, NF // 2 - 1, 1, False)
                second_product(NF - 2, 0, False)
                second_product(NF - 1, 1, False)




def build(nc, a, outs):
    scratch = {
        "mod": nc.dram_tensor("mod_rows", (2, 6 * D), F32, kind="Internal").ap(),
        "proj": nc.dram_tensor("proj", (T, DIN), F32, kind="Internal").ap(),
        "o": nc.dram_tensor("gla_out", (2, T, GW), F32, kind="Internal").ap(),
        "mix": nc.dram_tensor("mix", (T, D), F32, kind="Internal").ap(),
        "x1": nc.dram_tensor("x1", (T, D), F32, kind="Internal").ap(),
    }
    with ExitStack() as ctx:
        s = Space(nc, ctx, "keep")
        mats = s.sb("mats", [P, 5 * P + 8])
        keep = {
            "mats": mats,
            "ident": mats[:, 0:P],
            "cum": [mats[:, P * (1 + d):P * (2 + d)] for d in range(2)],
            "causal": [mats[:, P * (3 + d):P * (4 + d)] for d in range(2)],
            "vec": [mats[:, 5 * P + 4 * d:5 * P + 4 * d + 4] for d in range(2)],
            "minus_half": s.sb("minus_half", [P, 16]),
            "eps_d": s.sb("eps_d", [P, 16]),
            "eps_h": s.sb("eps_h", [P, 16]),
            "shift": s.sb("shift", [P, 2, KD, 2]),
            "scale": s.sb("scale", [P, 2, KD, 2]),
        }
        modulation(nc, keep, a, scratch)
        with ExitStack() as inner:
            s1 = Space(nc, inner, "h1")
            hi = s1.sb("hi", [P, KD, T], F32R)
            lo = s1.sb("lo", [P, KD, T], F32R)
            norm_first(nc, keep, a, hi, lo)
            project(nc, a, hi, lo, scratch)
        gla(nc, keep, a, scratch, outs)
        gla_output(nc, keep, a, scratch)
        attention(nc, keep, a, scratch, outs)
        with ExitStack() as inner:
            s2 = Space(nc, inner, "h2")
            hi = s2.sb("hi", [P, KD, T], F32R)
            lo = s2.sb("lo", [P, KD, T], F32R)
            merge(nc, keep, a, scratch, hi, lo)
            feed_forward(nc, a, scratch, hi, lo, outs)


INPUTS = ("x_prompt", "x_sample", "c", "cache_k", "cache_v", "state_gla_fwd", "state_gla_bwd", "c_ctx", "w_ada", "b_ada",
          "norm_mix", "norm_ff", "w_in", "w_gk_fwd", "b_gk_fwd", "w_gk_bwd", "b_gk_bwd", "gla_norm", "q_norm", "k_norm",
          "sink", "w_o", "w_ff1", "w_ff2")
OUTPUTS = ((1, TP, D), (1, TS, D), (1, 1, KV, TP, DH), (1, 1, KV, TP, DH), (1, 1, H, DH, DH), (1, 1, H, DH, DH))


def kernel(**inputs):
    import concourse.bacc as bacc
    from concourse.bass_utils import run_bass_kernel_spmd

    nc = bacc.Bacc("TRN2", target_bir_lowering=False, num_devices=1)
    arrays = {name: np.ascontiguousarray(inputs[name]) for name in INPUTS}
    arrays["mats"], arrays["window"], arrays["rope"] = constants()
    args = {n: nc.dram_tensor(f"in_{n}", x.shape, mybir.dt.from_np(x.dtype), kind="ExternalInput").ap()
            for n, x in arrays.items()}
    outs = [nc.dram_tensor(f"out_{i}", shape, F32, kind="ExternalOutput").ap() for i, shape in enumerate(OUTPUTS)]
    build(nc, args, outs)
    r = run_bass_kernel_spmd(nc, [{f"in_{n}": x for n, x in arrays.items()}], core_ids=[0])
    return tuple(r.results[0][f"out_{i}"] for i in range(len(OUTPUTS)))
```

```python
from contextlib import ExitStack

import numpy as np

import concourse.bass as bass
from concourse import mybir

F32 = mybir.dt.float32
F32R = mybir.dt.float32r
BF16 = mybir.dt.bfloat16
ALU = mybir.AluOpType
ACT = mybir.ActivationFunctionType
AX_X = mybir.AxisListType.X

P = 128
D = 1024
KD = D // P
TP, TS = 256, 1024
T = TP + TS
NT, NTP = T // P, TP // P
PAST = 512
H = 8
DH = 64
KV = 2
GW = H * DH
RANK = 16
DIN = 4 * GW + 2 * RANK + GW + 2 * KV * DH
C_GG, C_LR, C_SQ = 3 * GW, 4 * GW, 4 * GW + 2 * RANK
DFF = 4 * D
EPS = 1e-6
NEG = -1e30
GRID_W = 64
THETA = 10000.0
GATE_TEMP = 16.0
CLAMP = 42.0
HALF = 512


def constants():
    j = np.arange(P)[:, None]
    i = np.arange(P)[None, :]
    mid = P // 2
    cum_f = ((j <= i).astype(np.float32) - (j < mid)) / GATE_TEMP
    cum_b = ((j >= i).astype(np.float32) - (j >= mid)) / GATE_TEMP
    vec_f = np.zeros((P, 4), np.float32)
    vec_f[:mid, 0] = 1 / GATE_TEMP
    vec_f[:, 1] = 1 / GATE_TEMP
    vec_f[mid:, 2] = 1 / GATE_TEMP
    vec_b = vec_f.copy()
    vec_b[:, 0], vec_b[:, 2] = vec_f[:, 2], vec_f[:, 0]
    keep_f = (j <= i).astype(np.float32)
    keep_b = (j >= i).astype(np.float32)
    ident = np.eye(P, dtype=np.float32)
    mats = np.concatenate([ident, cum_f, cum_b, keep_f, keep_b, vec_f, vec_b], 1).astype(np.float32)
    tiles = TS // P
    left = np.where(i >= j, 0.0, NEG)
    right = np.where(i <= j, 0.0, NEG)
    none = np.full((P, P), NEG)
    left_all = np.concatenate([none] + [left] * (tiles - 1), 1)
    right_all = np.concatenate([right] * (tiles - 1) + [none], 1)
    window = np.concatenate([left_all, right_all], 1).astype(np.float32)
    half = DH // 4
    freqs = (THETA ** (-np.arange(half, dtype=np.float32) / half)).astype(np.float32)
    t = np.arange(TS)
    row = (t // GRID_W).astype(np.float32)[:, None] * freqs
    col = (t % GRID_W).astype(np.float32)[:, None] * freqs
    cos = np.concatenate([np.cos(row), np.cos(row), np.cos(col), np.cos(col)], 1)
    sin = np.concatenate([-np.sin(row), np.sin(row), -np.sin(col), np.sin(col)], 1)
    cos = np.concatenate([np.ones((TP, DH)), cos], 0).astype(np.float32)
    sin = np.concatenate([np.zeros((TP, DH)), sin], 0).astype(np.float32)
    rope = np.stack([cos, sin], 1)
    return mats, window, rope


class Space:

    def __init__(self, nc, ctx, prefix):
        self.nc, self.ctx, self.prefix, self.sems = nc, ctx, prefix, []
        ctx.callback(self.clear)

    def sb(self, name, shape, dt=F32):
        return self.ctx.enter_context(self.nc.sbuf_tensor(f"{self.prefix}_{name}", shape, dt))

    def ps(self, name, shape, dt=F32):
        return self.ctx.enter_context(self.nc.psum_tensor(f"{self.prefix}_{name}", shape, dt))

    def sem(self, name):
        self.sems.append(self.nc.alloc_semaphore(f"{self.prefix}_{name}"))
        return self.sems[-1]

    def clear(self):
        if self.sems:
            self.nc.clear_and_free_semaphores(self.sems)
            self.nc.all_engine_barrier()


def tile_rows(t):
    return bass.ds(t * P, P)


def modulation(nc, keep, a, scratch):
    COLS = HALF
    NCH = 6 * D // COLS
    with ExitStack() as ctx:
        s = Space(nc, ctx, "ada")
        w = s.sb("w", [P, 2, KD, COLS])
        cond = s.sb("cond", [P, 2, KD])
        e = s.sb("e", [P, 2, KD])
        e1 = s.sb("e1", [P, 2, KD])
        rec = s.sb("rec", [P, 2, KD])
        silu = s.sb("silu", [P, KD, 2])
        bias = s.sb("bias", [2, 6 * D])
        rows = s.sb("rows", [2, 6 * D])
        gain = s.sb("gain", [P, 2, KD])
        acc = s.ps("acc", [2, 2, COLS])
        cols = s.ps("cols", [P, 4, KD, 2])
        small_in = s.sem("small_in")
        w_in = [s.sem(f"w_in{j}") for j in range(2)]
        e_ready, e1_ready, rec_ready, silu_ready = (s.sem(n) for n in ("e_ready", "e1_ready", "rec_ready", "silu_ready"))
        acc_ready, rows_ready, cols_ready, mod_ready, scaled = (
            s.sem(n) for n in ("acc_ready", "rows_ready", "cols_ready", "mod_ready", "scaled"))
        rows_out = s.sem("rows_out")
        PARTS = (0, 1, 3, 4)
        with nc.Block() as block:

            @block.sync
            def _(sp):
                sp.dma_start(cond[:, 0, :], a["c_ctx"].rearrange("(k p) -> p k", p=P), allow_slow_non_contiguous=True).then_inc(small_in, 16)
                sp.dma_start(cond[:, 1, :], a["c"][0].rearrange("(k p) -> p k", p=P), allow_slow_non_contiguous=True).then_inc(small_in, 16)
                sp.dma_start(bias[:, :], a["b_ada"].broadcast_to([2, 6 * D])).then_inc(small_in, 16)
                sp.dma_start(gain[:, 0, :], a["norm_mix"][0].rearrange("(k p) -> p k", p=P), allow_slow_non_contiguous=True).then_inc(small_in, 16)
                sp.dma_start(gain[:, 1, :], a["norm_ff"][0].rearrange("(k p) -> p k", p=P), allow_slow_non_contiguous=True).then_inc(small_in, 16)
                sp.dma_start(keep["mats"][:, :], a["mats"]).then_inc(small_in, 16)
                wv = a["w_ada"][0].rearrange("(k p) n -> p k n", p=P)

                def load(i, j, first):
                    if not first:
                        sp.wait_ge(acc_ready, 2 * i + j - 1)
                    sp.dma_start(w[:, j], wv[:, :, bass.ds((2 * i + j) * COLS, COLS)]).then_inc(w_in[j], 16)

                for j in range(2):
                    load(0, j, True)
                with sp.Fori(1, NCH // 2) as i:
                    for j in range(2):
                        load(i, j, False)
                sp.wait_ge(rows_ready, NCH)
                sp.dma_start(scratch["mod"], rows[:, :]).then_inc(rows_out, 16)
                sp.wait_ge(rows_out, 16)

            @block.scalar
            def _(act):
                act.wait_ge(small_in, 6 * 16)
                act.activation(e[:, :, :], cond[:, :, :], ACT.Exp, scale=-1.0).then_inc(e_ready, 1)

            @block.vector
            def _(dve):
                dve.wait_ge(e_ready, 1)
                dve.tensor_scalar(e1[:, :, :], e[:, :, :], 1.0, None, ALU.add).then_inc(e1_ready, 1)
                dve.wait_ge(e1_ready, 1)
                dve.reciprocal(rec[:, :, :], e1[:, :, :]).then_inc(rec_ready, 1)
                dve.wait_ge(rec_ready, 1)
                dve.tensor_tensor(silu[:, :, :], cond[:, :, :].rearrange("p c k -> p k c"),
                                  rec[:, :, :].rearrange("p c k -> p k c"), ALU.mult).then_inc(silu_ready, 1)
                with dve.Fori(0, NCH // 2) as i:
                    for j in range(2):
                        dve.wait_ge(acc_ready, 2 * i + j + 1)
                        at = bass.ds((2 * i + j) * COLS, COLS)
                        dve.tensor_tensor(rows[:, at], acc[:, j], bias[:, at], ALU.add).then_inc(rows_ready, 1)
                dve.wait_ge(cols_ready, 1)
                for n in range(2):
                    dve.tensor_copy(keep["shift"][:, n], cols[:, 2 * n]).then_inc(mod_ready, 1)
                    dve.tensor_scalar(keep["scale"][:, n], cols[:, 2 * n + 1], 1.0, None, ALU.add).then_inc(mod_ready, 1)
                dve.wait_ge(mod_ready, 4)
                for n in range(2):
                    for c in range(2):
                        dve.tensor_tensor(keep["scale"][:, n, :, c], keep["scale"][:, n, :, c], gain[:, n, :],
                                          ALU.mult).then_inc(scaled, 1)

            @block.tensor
            def _(pe):
                pe.wait_ge(silu_ready, 1)

                def body(i, first):
                    for j in range(2):
                        pe.wait_ge(w_in[j], 16 * i + 16)
                        if not first:
                            pe.wait_ge(rows_ready, 2 * i + j - 1)
                        for k in range(KD):
                            mm = pe.matmul(acc[:, j], silu[:, k, :], w[:, j, k, :], start=(k == 0), stop=(k == KD - 1))
                        mm.then_inc(acc_ready, 1)
                body(0, True)
                with pe.Fori(1, NCH // 2) as i:
                    body(i, False)
                pe.wait_ge(rows_ready, NCH)
                for n, part in enumerate(PARTS):
                    for k in range(KD):
                        at = part * D + k * P
                        tr = pe.transpose(cols[:, n, k, :], rows[0:2, at:at + P], keep["ident"][0:2, 0:2])
                tr.then_inc(cols_ready, 1)


class NormStage:

    def __init__(self, s, keep, which, hi, lo, slots=2):
        self.slots = slots
        self.keep, self.which, self.hi, self.lo = keep, which, hi, lo
        self.x = s.sb("x", [P, 2, D])
        self.ssq = s.sb("ssq", [P, 2])
        self.ms = s.sb("ms", [P, 2])
        self.rstd = s.sb("rstd", [P, 2])
        self.xn = s.sb("xn", [P, 2, D])
        self.h = s.sb("h", [P, slots, KD, P])
        self.xT = s.ps("xT", [P, slots, KD, P])
        self.ssq_ready, self.ms_ready = s.sem("ssq_ready"), s.sem("ms_ready")
        self.rstd_ready, self.xn_ready = s.sem("rstd_ready"), s.sem("xn_ready")
        self.xT_ready, self.h_ready = s.sem("xT_ready"), s.sem("h_ready")
        self.hi_ready, self.lo_ready = s.sem("hi_ready"), s.sem("lo_ready")

    def act_square(self, act, i, j, ready, value, first):
        act.wait_ge(ready, value)
        if not first:
            act.wait_ge(self.xT_ready, 2 * i + j - 1)
        act.activation(self.xn[:, j], self.x[:, j], ACT.Square, accum_out=self.ssq[:, j:j + 1]).then_inc(self.ssq_ready, 1)

    def pool_rstd(self, pool, i, j):
        t = 2 * i + j
        pool.wait_ge(self.ssq_ready, t + 1)
        pool.tensor_tensor(self.ms[:, j:j + 1], self.ssq[:, j:j + 1], self.keep["eps_d"][:, 0:1], ALU.add).then_inc(self.ms_ready, 1)
        pool.wait_ge(self.ms_ready, t + 1)
        pool.tensor_tensor(self.rstd[:, j:j + 1], self.ms[:, j:j + 1], self.keep["minus_half"][:, 0:1], ALU.pow).then_inc(self.rstd_ready, 1)

    def dve_xn(self, dve, i, j, first):
        t = 2 * i + j
        dve.wait_ge(self.rstd_ready, t + 1)
        if not first:
            dve.wait_ge(self.xT_ready, t - 1)
        dve.tensor_scalar(self.xn[:, j], self.x[:, j], self.rstd[:, j:j + 1], D ** 0.5, ALU.mult, ALU.mult).then_inc(self.xn_ready, 1)

    def pe_transpose(self, pe, i, j, first):
        t = 2 * i + j
        m = j % self.slots
        pe.wait_ge(self.xn_ready, t + 1)
        if not (first and j < self.slots):
            pe.wait_ge(self.h_ready, t + 1 - self.slots)
        for k in range(KD):
            tr = pe.transpose(self.xT[:, m, k], self.xn[:, j, k * P:(k + 1) * P], self.keep["ident"])
        tr.then_inc(self.xT_ready, 1)

    def dve_modulate(self, dve, i, j, cond, first):
        t = 2 * i + j
        m = j % self.slots
        dve.wait_ge(self.xT_ready, t + 1)
        if not (first and j < self.slots):
            dve.wait_ge(self.lo_ready, t + 1 - self.slots)
        for k in range(KD):
            op = dve.tensor_scalar(self.h[:, m, k], self.xT[:, m, k], self.keep["scale"][:, self.which, k, cond:cond + 1],
                                   self.keep["shift"][:, self.which, k, cond:cond + 1], ALU.mult, ALU.add)
        op.then_inc(self.h_ready, 1)

    def act_hi(self, act, i, j):
        t = 2 * i + j
        act.wait_ge(self.h_ready, t + 1)
        act.activation(self.hi[:, :, tile_rows(t)], self.h[:, j % self.slots], ACT.Copy).then_inc(self.hi_ready, 1)

    def pool_lo(self, pool, i, j):
        t = 2 * i + j
        pool.wait_ge(self.hi_ready, t + 1)
        pool.tensor_tensor(self.lo[:, :, tile_rows(t)], self.h[:, j % self.slots], hi_view(self.hi)[:, :, tile_rows(t)],
                           ALU.subtract).then_inc(self.lo_ready, 1)


def hi_view(hi):
    return hi[:, :, :].bitcast(F32)


def pairs(engine, body):
    body(0, 0, True)
    with engine.Fori(1, NT // 2) as i:
        body(i, 1, False)


def norm_first(nc, keep, a, hi, lo):
    with ExitStack() as ctx:
        s = Space(nc, ctx, "n1")
        st = NormStage(s, keep, 0, hi, lo)
        x_in = [s.sem(f"x_in{j}") for j in range(2)]
        const_ready = s.sem("const_ready")
        with nc.Block() as block:

            @block.sync
            def _(sp):
                for j in range(2):
                    sp.dma_start(st.x[:, j], a["x_prompt"][0, j * P:(j + 1) * P, :]).then_inc(x_in[j], 16)
                with sp.Fori(1, NT // 2) as i:
                    for j in range(2):
                        sp.wait_ge(st.xn_ready, 2 * i + j - 1)
                        sp.dma_start(st.x[:, j], a["x_sample"][0, bass.ds((2 * i + j - NTP) * P, P), :]).then_inc(x_in[j], 16)

            @block.scalar
            def _(act):
                def body(i, cond, first):
                    for j in range(2):
                        st.act_square(act, i, j, x_in[j], 16 * i + 16, first)
                    for j in range(2):
                        st.act_hi(act, i, j)
                pairs(act, body)

            @block.gpsimd
            def _(pool):
                pool.memset(keep["minus_half"][:, :], -0.5).then_inc(const_ready, 1)
                pool.memset(keep["eps_d"][:, :], D * EPS).then_inc(const_ready, 1)
                pool.memset(keep["eps_h"][:, :], DH * EPS).then_inc(const_ready, 1)
                pool.wait_ge(const_ready, 3)

                def body(i, cond, first):
                    for j in range(2):
                        st.pool_rstd(pool, i, j)
                    for j in range(2):
                        st.pool_lo(pool, i, j)
                pairs(pool, body)

            @block.vector
            def _(dve):
                def body(i, cond, first):
                    for j in range(2):
                        st.dve_xn(dve, i, j, first)
                    for j in range(2):
                        st.dve_modulate(dve, i, j, cond, first)
                pairs(dve, body)

            @block.tensor
            def _(pe):
                def body(i, cond, first):
                    for j in range(2):
                        st.pe_transpose(pe, i, j, first)
                pairs(pe, body)


def project(nc, a, hi, lo, scratch):
    NG = 8
    COLS = DIN // NG
    RING = 4
    assert COLS * NG == DIN and COLS <= HALF and (2 * NT) % RING == 0
    with ExitStack() as ctx:
        s = Space(nc, ctx, "in")
        raw = s.sb("raw", [P, 2, KD, COLS])
        whi = [s.sb(f"whi{j}", [P, KD, COLS], F32R) for j in range(2)]
        wlo = [s.sb(f"wlo{j}", [P, KD, COLS], F32R) for j in range(2)]
        stage = s.sb("stage", [P, RING, COLS])
        acc = s.ps("acc", [P, RING, HALF])
        w_in = [s.sem(f"w_in{j}") for j in range(2)]
        whi_ready, wlo_ready, acc_ready = s.sem("whi_ready"), s.sem("wlo_ready"), s.sem("acc_ready")
        staged = [s.sem("staged_dve"), s.sem("staged_act")]
        stored = [s.sem(f"stored{b}") for b in range(RING)]
        wv = a["w_in"][0].rearrange("(k p) n -> p k n", p=P)
        with nc.Block() as block:

            @block.sync
            def _(sp):
                for j in range(2):
                    sp.dma_start(raw[:, j], wv[:, :, j * COLS:(j + 1) * COLS]).then_inc(w_in[j], 16)

                def body(i, last):
                    for j in range(2):
                        g = 2 * i + j
                        if not last:
                            sp.wait_ge(wlo_ready, g + 1)
                            sp.dma_start(raw[:, j], wv[:, :, bass.ds((g + 2) * COLS, COLS)]).then_inc(w_in[j], 16)
                        for t in range(NT):
                            n = NT * j + t
                            sp.wait_ge(staged[n % 2], NT * i + n // 2 + 1)
                            sp.dma_start(scratch["proj"][t * P:(t + 1) * P, bass.ds(g * COLS, COLS)],
                                         stage[:, n % RING]).then_inc(stored[n % RING], 16)
                with sp.Fori(0, NG // 2 - 1) as i:
                    body(i, False)
                body(NG // 2 - 1, True)
                for b in range(RING):
                    sp.wait_ge(stored[b], 16 * NG * NT // RING)

            def evacuate(eng, copy, parity, i, first):
                for n in range(parity, 2 * NT, 2):
                    eng.wait_ge(acc_ready, 2 * NT * i + n + 1)
                    if not (first and n < RING):
                        eng.wait_ge(stored[n % RING], 16 * (2 * NT // RING * i + n // RING))
                    copy(stage[:, n % RING], acc[:, n % RING, 0:COLS]).then_inc(staged[parity], 1)

            @block.scalar
            def _(act):
                def split(i, j, first):
                    g = 2 * i + j
                    act.wait_ge(w_in[j], 16 * i + 16)
                    if not first:
                        act.wait_ge(acc_ready, NT * (g - 1))
                    act.activation(whi[j][:, :, :], raw[:, j], ACT.Copy).then_inc(whi_ready, 1)

                def copy(out, in_):
                    return act.activation(out, in_, ACT.Copy)
                for j in range(2):
                    split(0, j, True)

                def body(i, first, last):
                    for j in range(2):
                        for n in range(NT * j + (1 - (NT * j) % 2), NT * (j + 1), 2):
                            act.wait_ge(acc_ready, 2 * NT * i + n + 1)
                            if not (first and n < RING):
                                act.wait_ge(stored[n % RING], 16 * (2 * NT // RING * i + n // RING))
                            copy(stage[:, n % RING], acc[:, n % RING, 0:COLS]).then_inc(staged[1], 1)
                        if not last:
                            split(i + 1, j, False)
                body(0, True, False)
                with act.Fori(1, NG // 2 - 1) as i:
                    body(i, False, False)
                body(NG // 2 - 1, False, True)

            @block.gpsimd
            def _(pool):
                with pool.Fori(0, NG // 2) as i:
                    for j in range(2):
                        g = 2 * i + j
                        pool.wait_ge(whi_ready, g + 1)
                        pool.tensor_tensor(wlo[j][:, :, :], raw[:, j], hi_view(whi[j]), ALU.subtract).then_inc(wlo_ready, 1)

            @block.vector
            def _(dve):
                evacuate(dve, dve.tensor_copy, 0, 0, True)
                with dve.Fori(1, NG // 2) as i:
                    evacuate(dve, dve.tensor_copy, 0, i, False)

            @block.tensor
            def _(pe):
                def body(i, first):
                    for j in range(2):
                        pe.wait_ge(wlo_ready, 2 * i + j + 1)
                        for t in range(NT):
                            n = NT * j + t
                            if not (first and n < RING):
                                pe.wait_ge(staged[n % 2], NT * i + n // 2 - 1)
                            for k in range(KD):
                                x_hi, x_lo = (x[:, k, t * P:(t + 1) * P] for x in (hi, lo))
                                pe.matmul(acc[:, n % RING, 0:COLS], x_hi, whi[j][:, k, :], start=(k == 0), stop=False)
                                pe.matmul(acc[:, n % RING, 0:COLS], x_hi, wlo[j][:, k, :], start=False, stop=False)
                                mm = pe.matmul(acc[:, n % RING, 0:COLS], x_lo, whi[j][:, k, :], start=False, stop=(k == KD - 1))
                            mm.then_inc(acc_ready, 1)
                body(0, True)
                with pe.Fori(1, NG // 2) as i:
                    body(i, False)


def gla(nc, keep, a, scratch, outs):
    with ExitStack() as ctx:
        s = Space(nc, ctx, "gla")
        qkv = s.sb("qkv", [P, NT, 3 * GW])
        glr = s.sb("glr", [P, NT, 2 * RANK])
        lrT = s.sb("lrT", [2 * RANK + 1, T])
        wgk = s.sb("wgk", [2 * RANK + 1, 2, GW])
        lr = [s.sb(f"lr{d}", [2 * RANK + 1, P]) for d in range(2)]
        mag = s.sb("mag", [P, 2, GW])
        ex = s.sb("ex", [P, 2, GW])
        ln = s.sb("ln", [P, 2, GW])
        g = s.sb("g", [P, 2, GW])
        bc = s.sb("bc", [P, 2, GW])
        up = s.sb("up", [P, 2, GW])
        down = s.sb("down", [P, 2, GW])
        qe = s.sb("qe", [P, 2, GW])
        ke = s.sb("ke", [P, 2, GW])
        qT = s.sb("qT", [P, 2, H // 2, P])
        kT = s.sb("kT", [P, 2, H // 2, P])
        at = s.sb("at", [P, 2, H, P])
        dec = s.sb("dec", [P, 2, H // 2, 4])
        state = [s.sb("state_p", [P, 2, H // 2, DH]), s.sb("state_s", [P, 2, H // 2, DH])]
        mid = s.sb("mid", [P, 2, H // 2, 2, DH])
        kept = s.sb("kept", [P, 2, H // 2, DH])
        new = s.sb("new", [P, 2, H // 2, DH])
        o = s.sb("o", [P, 2, NT, GW])
        ps = [s.ps(f"ps{d}", [P, 4, HALF]) for d in range(2)]
        (lr_ready, logit_ready, mag_ready, ex_ready, ln_ready, g_ready, bc_ready, clamp_ready, up_ready, down_ready,
         qe_ready, ke_ready, tr_ready, qT_ready, kT_ready, score_ready, at_ready, dec_ready, mid_ready, o_ready,
         o_kept, ds_ready, kept_ready, new_ready, state_ready) = (s.sem(n) for n in (
             "lr_ready", "logit_ready", "mag_ready", "ex_ready", "ln_ready", "g_ready", "bc_ready", "clamp_ready",
             "up_ready", "down_ready", "qe_ready", "ke_ready", "tr_ready", "qT_ready", "kT_ready", "score_ready",
             "at_ready", "dec_ready", "mid_ready", "o_ready", "o_kept", "ds_ready", "kept_ready", "new_ready",
             "state_ready"))
        loaded, zeroed, weights_in, lrT_ready, lrT_kept, stored = (s.sem(n) for n in (
            "loaded", "zeroed", "weights_in", "lrT_ready", "lrT_kept", "stored"))

        def steps(eng, body):
            body(0, 0, True)
            body(1, 0, False)
            with eng.Fori(2, NT) as i:
                body(i, 1, False)

        def tiles_of(eng, i, part):
            if part == 0:
                return i, NTP - 1 - i
            return eng.snap(i + 0), eng.snap(i * -1 + (NTP + NT - 1))

        with nc.Block() as block:

            @block.sync
            def _(sp):
                sp.dma_start(glr[:, :, :], scratch["proj"][:, C_LR:C_SQ].rearrange("(t p) n -> p t n", p=P)).then_inc(loaded, 16)
                for half in range(2):
                    t0 = half * NT // 2
                    sp.dma_start(qkv[:, t0:t0 + NT // 2, :],
                                 scratch["proj"][t0 * P:(t0 + NT // 2) * P, 0:3 * GW].rearrange("(t p) n -> p t n", p=P)
                                 ).then_inc(loaded, 16)
                sp.wait_ge(zeroed, 1)
                for d, (w, b) in enumerate((("w_gk_fwd", "b_gk_fwd"), ("w_gk_bwd", "b_gk_bwd"))):
                    sp.dma_start(wgk[d * RANK:(d + 1) * RANK, d, :], a[w][0]).then_inc(weights_in, 16)
                    sp.dma_start(wgk[2 * RANK:2 * RANK + 1, d, :], a[b]).then_inc(weights_in, 16)
                for d, name in enumerate(("state_gla_fwd", "state_gla_bwd")):
                    for half in range(2):
                        sp.dma_start(state[1][half * DH:(half + 1) * DH, d],
                                     a[name][0, 0].rearrange("(b c) k v -> c k b v", c=2)[half]).then_inc(loaded, 16)
                sp.wait_ge(state_ready, 2 * NTP)
                for d in range(2):
                    for half in range(2):
                        sp.dma_start(outs[4 + d][0, 0].rearrange("(b c) k v -> c k b v", c=2)[half],
                                     state[0][half * DH:(half + 1) * DH, d]).then_inc(stored, 16)
                sp.wait_ge(o_kept, 2 * NT)
                for d in range(2):
                    sp.dma_start(scratch["o"][d].rearrange("(t p) n -> p t n", p=P), o[:, d]).then_inc(stored, 16)
                sp.wait_ge(stored, 6 * 16)

            @block.gpsimd
            def _(pool):
                pool.wait_ge(lrT_kept, 3)
                pool.wait_ge(zeroed, 4)
                pool.wait_ge(loaded, 7 * 16)

                def body(i, part, first):
                    tile = tiles_of(pool, i, part)
                    for d in range(2):
                        u = 2 * i + d
                        if not first:
                            pool.wait_ge(logit_ready, u - 1)
                        pool.tensor_copy(lr[d][:, :], lrT[:, tile_rows(tile[d])]).then_inc(lr_ready, 1)
                    for d in range(2):
                        u = 2 * i + d
                        pool.wait_ge(down_ready, u + 1)
                        if not first:
                            pool.wait_ge(ds_ready, u - 1)
                        pool.tensor_tensor(ke[:, d], down[:, d], qkv[:, bass.ds(tile[d], 1), GW:2 * GW].rearrange("p t n -> p (t n)"),
                                           ALU.mult).then_inc(ke_ready, 1)
                steps(pool, body)

            @block.scalar
            def _(act):
                def body(i, part, first):
                    for d in range(2):
                        u = 2 * i + d
                        act.wait_ge(logit_ready, u + 1)
                        act.activation(mag[:, d], ps[d][:, 0], ACT.Abs).then_inc(mag_ready, 1)
                        act.wait_ge(mag_ready, u + 1)
                        act.activation(ex[:, d], mag[:, d], ACT.Exp, scale=-1.0).then_inc(ex_ready, 1)
                        act.wait_ge(ex_ready, u + 1)
                        if not first:
                            act.wait_ge(g_ready, u - 1)
                        act.activation(ln[:, d], ex[:, d], ACT.Ln, bias=1.0).then_inc(ln_ready, 1)
                    for d in range(2):
                        u = 2 * i + d
                        act.wait_ge(clamp_ready, u + 1)
                        if not first:
                            act.wait_ge(qe_ready, u - 1)
                            act.wait_ge(ke_ready, u - 1)
                        act.activation(up[:, d], bc[:, d], ACT.Exp).then_inc(up_ready, 1)
                        act.activation(down[:, d], bc[:, d], ACT.Exp, scale=-1.0).then_inc(down_ready, 1)
                        if not first:
                            act.wait_ge(state_ready, u - 1)
                        act.activation(dec[:, d], ps[d][:, 3, 0:2 * H].rearrange("p (b c) -> p b c", c=4), ACT.Exp).then_inc(dec_ready, 1)
                    for d in range(2):
                        u = 2 * i + d
                        act.wait_ge(tr_ready, u + 1)
                        act.activation(qT[:, d], ps[d][:, 1].rearrange("p (b c) -> p b c", c=P), ACT.Copy).then_inc(qT_ready, 1)
                steps(act, body)

            @block.vector
            def _(dve):
                dve.memset(wgk[:, :, :], 0.0).then_inc(zeroed, 1)
                dve.memset(lrT[2 * RANK:2 * RANK + 1, :], 1.0).then_inc(zeroed, 1)
                dve.memset(state[0][:, :, :, :], 0.0).then_inc(zeroed, 1)
                dve.memset(mid[:, :, :, :, :], 0.0).then_inc(zeroed, 1)
                for n in range(3):
                    w = min(4, NT - 4 * n) * P
                    dve.wait_ge(lrT_ready, 1)
                    dve.tensor_copy(lrT[0:2 * RANK, 4 * n * P:4 * n * P + w], ps[0][0:2 * RANK, n, 0:w]).then_inc(lrT_kept, 1)
                dve.wait_ge(loaded, 7 * 16)
                dve.wait_ge(zeroed, 4)

                def body(i, part, first):
                    tile = tiles_of(dve, i, part)
                    for d in range(2):
                        u = 2 * i + d
                        dve.wait_ge(ln_ready, u + 1)
                        dve.scalar_tensor_tensor(g[:, d], ps[d][:, 0], 0.0, ln[:, d], ALU.min, ALU.subtract).then_inc(g_ready, 1)
                    for d in range(2):
                        u = 2 * i + d
                        dve.wait_ge(bc_ready, u + 1)
                        if not first:
                            dve.wait_ge(down_ready, u - 1)
                        dve.tensor_scalar(bc[:, d], ps[d][:, 0], CLAMP, -CLAMP, ALU.min, ALU.max).then_inc(clamp_ready, 1)
                    for d in range(2):
                        u = 2 * i + d
                        dve.wait_ge(up_ready, u + 1)
                        if not first:
                            dve.wait_ge(tr_ready, u - 1)
                        dve.scalar_tensor_tensor(qe[:, d], up[:, d], DH ** -0.5,
                                                 qkv[:, bass.ds(tile[d], 1), 0:GW].rearrange("p t n -> p (t n)"),
                                                 ALU.mult, ALU.mult).then_inc(qe_ready, 1)
                        dve.wait_ge(dec_ready, u + 1)
                        if not first:
                            dve.wait_ge(state_ready, u - 1)
                            dve.wait_ge(o_ready, u - 1)
                        for half in range(2):
                            rows = slice(half * DH, (half + 1) * DH)
                            dve.tensor_tensor(mid[rows, d, :, half], state[part][rows, d],
                                              dec[rows, d, :, 0:1].broadcast_to([DH, H // 2, DH]), ALU.mult).then_inc(mid_ready, 1)
                    for d in range(2):
                        u = 2 * i + d
                        dve.wait_ge(tr_ready, u + 1)
                        dve.tensor_copy(kT[:, d], ps[d][:, 2].rearrange("p (b c) -> p b c", c=P)).then_inc(kT_ready, 1)
                    for d in range(2):
                        u = 2 * i + d
                        dve.wait_ge(score_ready, u + 1)
                        if not first:
                            dve.wait_ge(o_ready, u - 1)
                        dve.tensor_tensor(at[:, d], ps[d][:, 1:3].rearrange("p b (c n) -> p (b c) n", n=P),
                                          keep["causal"][d].unsqueeze(1).broadcast_to([P, H, P]), ALU.mult).then_inc(at_ready, 1)
                        dve.tensor_tensor(kept[:, d], state[part][:, d], dec[:, d, :, 1:2].broadcast_to([P, H // 2, DH]),
                                          ALU.mult).then_inc(kept_ready, 1)
                    for d in range(2):
                        u = 2 * i + d
                        dve.wait_ge(ds_ready, u + 1)
                        for half in range(2):
                            rows = slice(half * DH, (half + 1) * DH)
                            upd = ps[d][rows, 0].rearrange("p (b c) -> p b c", c=P)[:, :, half * DH:(half + 1) * DH]
                            dve.tensor_tensor(new[rows, d], upd, dec[rows, d, :, 2:3].broadcast_to([DH, H // 2, DH]),
                                              ALU.mult).then_inc(new_ready, 1)
                        dve.wait_ge(new_ready, 2 * u + 2)
                        dve.wait_ge(kept_ready, u + 1)
                        dve.wait_ge(mid_ready, 2 * u + 2)
                        dve.tensor_tensor(state[part][:, d], kept[:, d], new[:, d], ALU.add).then_inc(state_ready, 1)
                        dve.wait_ge(o_ready, u + 1)
                        dve.tensor_copy(o[:, d, bass.ds(tile[d], 1), :].rearrange("p t n -> p (t n)"),
                                        ps[d][:, 3]).then_inc(o_kept, 1)
                steps(dve, body)

            @block.tensor
            def _(pe):
                pe.wait_ge(loaded, 7 * 16)
                for t in range(NT):
                    tr = pe.transpose(ps[0][0:2 * RANK, t // 4, (t % 4) * P:(t % 4 + 1) * P], glr[:, t, :], keep["ident"])
                tr.then_inc(lrT_ready, 1)
                pe.wait_ge(weights_in, 4 * 16)
                pe.wait_ge(lrT_kept, 3)

                def body(i, part, first):
                    tile = tiles_of(pe, i, part)
                    for d in range(2):
                        u = 2 * i + d
                        pe.wait_ge(lr_ready, u + 1)
                        if not first:
                            pe.wait_ge(state_ready, u - 1)
                        pe.matmul(ps[d][:, 0], lr[d][:, :], wgk[:, d, :], start=True, stop=True).then_inc(logit_ready, 1)
                    for d in range(2):
                        u = 2 * i + d
                        pe.wait_ge(g_ready, u + 1)
                        pe.matmul(ps[d][:, 0], keep["cum"][d], g[:, d], start=True, stop=True)
                        if not first:
                            pe.wait_ge(o_kept, u - 1)
                        for b in range(H // 2):
                            mm = pe.matmul(ps[d][:, 3, 4 * b:4 * b + 4], g[:, d, b * P:(b + 1) * P], keep["vec"][d],
                                           start=True, stop=True)
                        mm.then_inc(bc_ready, 1)
                    for d in range(2):
                        u = 2 * i + d
                        pe.wait_ge(qe_ready, u + 1)
                        pe.wait_ge(ke_ready, u + 1)
                        if not first:
                            pe.wait_ge(at_ready, u - 1)
                        for bank, x in ((1, qe), (2, ke)):
                            for b in range(H // 2):
                                tr = pe.transpose(ps[d][:, bank, b * P:(b + 1) * P], x[:, d, b * P:(b + 1) * P], keep["ident"])
                        tr.then_inc(tr_ready, 1)
                    for d in range(2):
                        u = 2 * i + d
                        pe.wait_ge(qT_ready, u + 1)
                        pe.wait_ge(kT_ready, u + 1)
                        for h in range(H):
                            rows = slice((h % 2) * DH, (h % 2 + 1) * DH)
                            mm = pe.matmul(ps[d][:, 1 + h % 2, (h // 2) * P:(h // 2 + 1) * P], kT[rows, d, h // 2], qT[rows, d, h // 2],
                                           start=True, stop=True)
                        mm.then_inc(score_ready, 1)
                        for b in range(H // 2):
                            mm = pe.matmul(ps[d][:, 0, b * P:(b + 1) * P], ke[:, d, b * P:(b + 1) * P],
                                           qkv[:, bass.ds(tile[d], 1), 2 * GW + b * P:2 * GW + (b + 1) * P].rearrange("p t n -> p (t n)"),
                                           start=True, stop=True)
                        mm.then_inc(ds_ready, 1)
                    for d in range(2):
                        u = 2 * i + d
                        pe.wait_ge(at_ready, u + 1)
                        pe.wait_ge(mid_ready, 2 * u + 2)
                        for b in range(H // 2):
                            pe.matmul(ps[d][:, 3, b * P:(b + 1) * P], qT[:, d, b], mid[:, d, b].rearrange("p c n -> p (c n)"),
                                      start=True, stop=False)
                            for half in range(2):
                                c = b * P + half * DH
                                mm = pe.matmul(ps[d][:, 3, c:c + DH], at[:, d, half * (H // 2) + b],
                                               qkv[:, bass.ds(tile[d], 1), 2 * GW + c:2 * GW + c + DH].rearrange("p t n -> p (t n)"),
                                               start=False, stop=(half == 1))
                        mm.then_inc(o_ready, 1)
                steps(pe, body)


class GlaOutput:
    def __init__(self, s, keep, a, scratch, out, stored):
        self.out, self.stored = out, stored
        self.keep, self.a, self.scratch = keep, a, scratch
        self.of, self.ob, self.gg, self.o, self.sq, self.tanh, self.factor, self.si, self.on, self.og = (
            s.sb("glo_" + n, [P, 2, GW]) for n in ("of", "ob", "gg", "o", "sq", "tanh", "factor", "si", "on", "og"))
        self.norm = s.sb("glo_norm", [P, DH])
        self.root = s.sb("glo_root", [P, DH])
        self.one = s.sb("glo_one", [P, GW])
        self.gain = s.sb("glo_gain", [P, DH])
        self.ssq, self.ms, self.rstd = (s.sb("glo_" + n, [P, 2, H]) for n in ("ssq", "ms", "rstd"))
        (self.o_ready, self.sq_ready, self.ssq_ready, self.ms_ready, self.rstd_ready, self.tanh_ready, self.factor_ready,
         self.si_ready, self.on_ready, self.og_ready, self.out_ready, self.norm_in, self.root_ready,
         self.gain_ready) = (s.sem("glo_" + n) for n in (
             "o_ready", "sq_ready", "ssq_ready", "ms_ready", "rstd_ready", "tanh_ready", "factor_ready", "si_ready",
             "on_ready", "og_ready", "out_ready", "norm_in", "root_ready", "gain_ready"))
        self.loaded = [s.sem(f"glo_loaded{j}") for j in range(2)]

    def sp_gain(self, sp):
        sp.dma_start(self.norm[:, :], self.a["gla_norm"].broadcast_to([P, DH])).then_inc(self.norm_in, 16)

    def sp_load(self, sp, t, j):
        sp.dma_start(self.of[:, j], self.scratch["o"][0, tile_rows(t), :]).then_inc(self.loaded[j], 16)
        sp.dma_start(self.ob[:, j], self.scratch["o"][1, tile_rows(t), :]).then_inc(self.loaded[j], 16)
        sp.dma_start(self.gg[:, j], self.scratch["proj"][tile_rows(t), C_GG:C_LR]).then_inc(self.loaded[j], 16)

    def pool_gain(self, pool):
        pool.memset(self.root[:, :], DH ** 0.5 / 2).then_inc(self.root_ready, 1)
        pool.memset(self.one[:, :], 1.0).then_inc(self.root_ready, 1)
        pool.wait_ge(self.root_ready, 2)
        pool.wait_ge(self.norm_in, 16)
        pool.tensor_tensor(self.gain[:, :], self.norm[:, :], self.root[:, :], ALU.mult).then_inc(self.gain_ready, 1)
        pool.wait_ge(self.gain_ready, 1)

    def pool(self, pool, i, j, first):
        t = 2 * i + j

        def heads(x):
            return x.rearrange("p (h d) -> p h d", d=DH)
        pool.wait_ge(self.loaded[j], 48 * i + 48)
        pool.tensor_tensor(self.o[:, j], self.of[:, j], self.ob[:, j], ALU.add).then_inc(self.o_ready, 1)
        pool.wait_ge(self.o_ready, t + 1)
        pool.tensor_tensor(self.sq[:, j], self.o[:, j], self.o[:, j], ALU.mult).then_inc(self.sq_ready, 1)
        pool.wait_ge(self.ssq_ready, t + 1)
        pool.tensor_tensor(self.ms[:, j], self.ssq[:, j], self.keep["eps_h"][:, 0:H], ALU.add).then_inc(self.ms_ready, 1)
        pool.wait_ge(self.ms_ready, t + 1)
        pool.tensor_tensor(self.rstd[:, j], self.ms[:, j], self.keep["minus_half"][:, 0:H], ALU.pow).then_inc(self.rstd_ready, 1)
        pool.wait_ge(self.rstd_ready, t + 1)
        pool.tensor_tensor(heads(self.on[:, j]), heads(self.o[:, j]), self.rstd[:, j].unsqueeze(2).broadcast_to([P, H, DH]),
                           ALU.mult).then_inc(self.on_ready, 1)
        pool.wait_ge(self.on_ready, t + 1)
        pool.tensor_tensor(heads(self.og[:, j]), heads(self.on[:, j]), self.gain[:, :].unsqueeze(1).broadcast_to([P, H, DH]),
                           ALU.mult).then_inc(self.og_ready, 1)
        pool.wait_ge(self.tanh_ready, t + 1)
        pool.tensor_tensor(self.factor[:, j], self.tanh[:, j], self.one[:, :], ALU.add).then_inc(self.factor_ready, 1)
        pool.wait_ge(self.factor_ready, t + 1)
        pool.tensor_tensor(self.si[:, j], self.gg[:, j], self.factor[:, j], ALU.mult).then_inc(self.si_ready, 1)
        pool.wait_ge(self.si_ready, t + 1)
        pool.wait_ge(self.og_ready, t + 1)
        if not first:
            pool.wait_ge(self.stored[j], 16 * i)
        pool.tensor_tensor(self.out[:, j], self.og[:, j], self.si[:, j], ALU.mult).then_inc(self.out_ready, 1)

    def act(self, act, i, j, first):
        act.wait_ge(self.loaded[j], 48 * i + 48)
        if not first:
            act.wait_ge(self.factor_ready, 2 * i + j - 1)
        act.activation(self.tanh[:, j], self.gg[:, j], ACT.Tanh, scale=0.5).then_inc(self.tanh_ready, 1)

    def dve(self, dve, i, j, first):
        t = 2 * i + j
        dve.wait_ge(self.sq_ready, t + 1)
        if not first:
            dve.wait_ge(self.ms_ready, t - 1)
        dve.tensor_reduce(self.ssq[:, j], self.sq[:, j].rearrange("p (h d) -> p h d", d=DH), AX_X, ALU.add).then_inc(self.ssq_ready, 1)


def attention(nc, keep, a, scratch, outs):
    NL, NC = 3, PAST // P
    NX = H + KV
    WX = NX * DH
    PAD = NTP
    SLOTS = NT + 2
    with ExitStack() as ctx:
        s = Space(nc, ctx, "att")
        qhi, qlo = (s.sb(n, [P, H, T], F32R) for n in ("qhi", "qlo"))
        kT = s.sb("kT", [P, KV, SLOTS * P], F32R)
        kcT = s.sb("kcT", [P, KV, PAST], F32R)
        v = s.sb("v", [P, SLOTS, KV * DH])
        vc = s.sb("vc", [P, NC, KV, DH])
        sink = s.sb("sink", [P, H])
        nsink = s.sb("nsink", [P, H])
        win = s.sb("win", [P, 2 * TS], BF16)
        identb = s.sb("identb", [P, P], BF16)

        with ExitStack() as inner:
            s1 = Space(nc, inner, "prep")
            x = s1.sb("x", [P, 2, WX + KV * DH])
            sq = s1.sb("sq", [P, 2, WX])
            ssq, ms, rstd = (s1.sb(n, [P, 2, NX]) for n in ("ssq", "ms", "rstd"))
            xn = s1.sb("xn", [P, 2, WX])
            xg = s1.sb("xg", [P, 2, WX])
            xc = s1.sb("xc", [P, 2, WX])
            xs = s1.sb("xs", [P, 2, WX])
            xr = s1.sb("xr", [P, 2, NX, 2, DH])
            khi = s1.sb("khi", [P, 2, KV, P], F32R)
            kchi = s1.sb("kchi", [P, KV, PAST], F32R)
            gain = s1.sb("gain", [P, NX, DH])
            rope = s1.sb("rope", [P, NT, 2 * DH])
            winf = s1.sb("winf", [P, 2 * TS])
            kc = s1.sb("kc", [P, NC, KV, 2, DH])
            tr = s1.ps("tr", [P, 2, 3, HALF])
            trc = s1.ps("trc", [P, 2, HALF])
            const_in, x_const, padded, tables, ctx_ready = (s1.sem(n) for n in ("const_in", "x_const", "padded", "tables", "ctx_ready"))
            ctx_hi_ready = s1.sem("ctx_hi_ready")
            x_in = [s1.sem(f"x_in{j}") for j in range(2)]
            kv_out = s1.sem("kv_out")
            (sq_ready, ssq_ready, ms_ready, rstd_ready, xn_ready, xg_ready, xc_ready, xs_ready, xr_ready, v_ready, tr_ready,
             hi_ready, lo_ready) = (s1.sem(n) for n in (
                 "sq_ready", "ssq_ready", "ms_ready", "rstd_ready", "xn_ready", "xg_ready", "xc_ready", "xs_ready", "xr_ready",
                 "v_ready", "tr_ready", "hi_ready", "lo_ready"))
            CONSTS = NX + 3 + 3 * KV

            def heads(y):
                return y.rearrange("p (h d) -> p h d", d=DH)

            def heads_of(y):
                return y.rearrange("p b (h n) -> p (b h) n", n=P)

            def keys_of(y):
                return y[:, 0:KV * P].rearrange("p (b c) -> p b c", c=P)

            def axes(y):
                return y.rearrange("p (h a b f) -> p h a b f", a=2, b=2, f=DH // 4)

            with nc.Block() as block:

                @block.sync
                def _(sp):
                    for h in range(NX):
                        sp.dma_start(gain[:, h], a["q_norm" if h < H else "k_norm"].broadcast_to([P, DH])).then_inc(const_in, 16)
                    sp.dma_start(rope[:, :, :], a["rope"].rearrange("(t p) c d -> p t (c d)", p=P)).then_inc(const_in, 16)

                    def load(i, j, first):
                        t = 2 * i + j
                        if not first:
                            sp.wait_ge(xn_ready, t - 1)
                            sp.wait_ge(sq_ready, t - 1)
                            sp.wait_ge(v_ready, t - 1)
                        sp.dma_start(x[:, j], scratch["proj"][tile_rows(t), C_SQ:DIN]).then_inc(x_in[j], 16)
                    for j in range(2):
                        load(0, j, True)
                    sp.dma_start(winf[:, :], a["window"]).then_inc(const_in, 16)
                    sp.dma_start(sink[:, :], a["sink"].broadcast_to([P, H])).then_inc(const_in, 16)
                    for dup in range(2):
                        for kv in range(KV):
                            sp.dma_start(kc[:, :, kv, dup, :], a["cache_k"][0, 0, kv].rearrange("(b p) d -> p b d", p=P)).then_inc(const_in, 16)
                    for kv in range(KV):
                        sp.dma_start(vc[:, :, kv, :], a["cache_v"][0, 0, kv].rearrange("(b p) d -> p b d", p=P)).then_inc(const_in, 16)
                    for j in range(NTP):
                        sp.wait_ge(xg_ready, j + 1)
                        for kv in range(KV):
                            sp.dma_start(outs[2][0, 0, kv, j * P:(j + 1) * P, :], xg[:, j, GW + kv * DH:GW + (kv + 1) * DH]).then_inc(kv_out, 16)
                            sp.dma_start(outs[3][0, 0, kv, j * P:(j + 1) * P, :], x[:, j, WX + kv * DH:WX + (kv + 1) * DH]).then_inc(kv_out, 16)
                    sp.wait_ge(kv_out, 16 * 2 * KV * NTP)
                    with sp.Fori(1, NT // 2) as i:
                        for j in range(2):
                            load(i, j, False)

                @block.gpsimd
                def _(pool):
                    pool.wait_ge(const_in, 16 * (NX + 1))

                    def body(i, cond, first):
                        for j in range(2):
                            t = 2 * i + j
                            pool.wait_ge(x_in[j], 16 * i + 16)
                            if not first:
                                pool.wait_ge(ssq_ready, t - 1)
                            pool.tensor_tensor(sq[:, j], x[:, j, 0:WX], x[:, j, 0:WX], ALU.mult).then_inc(sq_ready, 1)
                        for j in range(2):
                            t = 2 * i + j
                            pool.wait_ge(ssq_ready, t + 1)
                            pool.tensor_tensor(ms[:, j], ssq[:, j], keep["eps_h"][:, 0:NX], ALU.add).then_inc(ms_ready, 1)
                            pool.wait_ge(ms_ready, t + 1)
                            pool.tensor_tensor(rstd[:, j], ms[:, j], keep["minus_half"][:, 0:NX], ALU.pow).then_inc(rstd_ready, 1)
                        for j in range(2):
                            t = 2 * i + j
                            pool.wait_ge(xn_ready, t + 1)
                            if not first:
                                pool.wait_ge(kv_out, 16 * 2 * KV * NTP)
                                pool.wait_ge(xc_ready, t - 1)
                            pool.tensor_tensor(xg[:, j], xn[:, j], gain[:, :, :].rearrange("p h d -> p (h d)"), ALU.mult).then_inc(xg_ready, 1)
                            pool.wait_ge(xg_ready, t + 1)
                            if not first:
                                pool.wait_ge(xr_ready, t - 1)
                            sin = axes(rope[:, bass.ds(t, 1), DH:2 * DH].rearrange("p t d -> p (t d)"))
                            for b in range(2):
                                pool.tensor_tensor(axes(xs[:, j])[:, :, :, b], axes(xg[:, j])[:, :, :, 1 - b],
                                                   sin[:, :, :, b].broadcast_to([P, NX, 2, DH // 4]), ALU.mult).then_inc(xs_ready, 1)
                    pairs(pool, body)

                @block.vector
                def _(dve):
                    dve.tensor_scalar(kT[:, :, PAD * P:(PAD + 1) * P], keep["ident"].unsqueeze(1).broadcast_to([P, KV, P]), 0.0, None, ALU.mult).then_inc(padded, 1)
                    dve.tensor_scalar(kT[:, :, (SLOTS - 1) * P:SLOTS * P], keep["ident"].unsqueeze(1).broadcast_to([P, KV, P]), 0.0, None, ALU.mult).then_inc(padded, 1)
                    dve.memset(v[:, PAD], 0.0).then_inc(padded, 1)
                    dve.memset(v[:, SLOTS - 1], 0.0).then_inc(padded, 1)
                    dve.tensor_copy(identb[:, :], keep["ident"]).then_inc(tables, 1)
                    dve.wait_ge(const_in, 16 * CONSTS)
                    dve.tensor_scalar(nsink[:, :], sink[:, :], -1.0, None, ALU.mult).then_inc(tables, 1)
                    dve.tensor_copy(win[:, :], winf[:, :]).then_inc(tables, 1)
                    dve.wait_ge(ctx_hi_ready, 2)
                    dve.tensor_tensor(kcT[DH:P], trc[DH:P], kchi[DH:P].bitcast(F32), ALU.subtract).then_inc(ctx_ready, 1)

                    def body(i, cond, first):
                        for j in range(2):
                            t = 2 * i + j
                            dve.wait_ge(sq_ready, t + 1)
                            if not first:
                                dve.wait_ge(ms_ready, t - 1)
                            dve.tensor_reduce(ssq[:, j], heads(sq[:, j]), AX_X, ALU.add).then_inc(ssq_ready, 1)
                            if not first:
                                dve.wait_ge(tr_ready, t - 1)
                            dve.tensor_copy(v[:, bass.ds(t + cond, 1), :].rearrange("p t d -> p (t d)"), x[:, j, WX:WX + KV * DH]).then_inc(v_ready, 1)
                        for j in range(2):
                            t = 2 * i + j
                            dve.wait_ge(rstd_ready, t + 1)
                            if not first:
                                dve.wait_ge(xg_ready, t - 1)
                            dve.scalar_tensor_tensor(heads(xn[:, j]), heads(x[:, j, 0:WX]), DH ** 0.5,
                                                     rstd[:, j].unsqueeze(2).broadcast_to([P, NX, DH]), ALU.mult, ALU.mult).then_inc(xn_ready, 1)
                        for j in range(2):
                            t = 2 * i + j
                            dve.wait_ge(xg_ready, t + 1)
                            if not first:
                                dve.wait_ge(xr_ready, t - 1)
                            dve.tensor_tensor(heads(xc[:, j]), heads(xg[:, j]),
                                              rope[:, bass.ds(t, 1), 0:DH].broadcast_to([P, NX, DH]), ALU.mult).then_inc(xc_ready, 1)
                            dve.wait_ge(xc_ready, t + 1)
                            dve.wait_ge(xs_ready, 2 * t + 2)
                            if not first:
                                dve.wait_ge(tr_ready, t - 1)
                            dve.tensor_tensor(xr[:, j], heads(xc[:, j]).unsqueeze(2).broadcast_to([P, NX, 2, DH]),
                                              heads(xs[:, j]).unsqueeze(2).broadcast_to([P, NX, 2, DH]), ALU.add).then_inc(xr_ready, 1)
                        for j in range(2):
                            t = 2 * i + j
                            dve.wait_ge(hi_ready, 3 * t + 3)
                            dve.tensor_tensor(qlo[:, :, tile_rows(t)], heads_of(tr[:, j, 0:2]), qhi[:, :, tile_rows(t)].bitcast(F32),
                                              ALU.subtract).then_inc(lo_ready, 1)
                            dve.tensor_tensor(kT[DH:P, :, bass.ds((t + cond) * P, P)], keys_of(tr[DH:P, j, 2]), khi[DH:P, j].bitcast(F32),
                                              ALU.subtract).then_inc(lo_ready, 1)
                    pairs(dve, body)
                    dve.wait_ge(lo_ready, 2 * NT)

                @block.scalar
                def _(act):
                    act.wait_ge(x_const, 1)
                    act.activation(kcT[0:DH], trc[0:DH], ACT.Copy).then_inc(ctx_hi_ready, 1)
                    act.activation(kchi[DH:P], trc[DH:P], ACT.Copy).then_inc(ctx_hi_ready, 1)

                    def body(i, cond, first):
                        for j in range(2):
                            t = 2 * i + j
                            act.wait_ge(tr_ready, t + 1)
                            act.activation(qhi[:, :, tile_rows(t)], heads_of(tr[:, j, 0:2]), ACT.Copy).then_inc(hi_ready, 1)
                            act.activation(kT[0:DH, :, bass.ds((t + cond) * P, P)], keys_of(tr[0:DH, j, 2]), ACT.Copy).then_inc(hi_ready, 1)
                            if not first:
                                act.wait_ge(lo_ready, 2 * t - 2)
                            act.activation(khi[DH:P, j], keys_of(tr[DH:P, j, 2]), ACT.Copy).then_inc(hi_ready, 1)
                    pairs(act, body)

                @block.tensor
                def _(pe):
                    pe.wait_ge(const_in, 16 * CONSTS)
                    for kv in range(KV):
                        for b in range(NC):
                            mm = pe.transpose(trc[:, kv, b * P:(b + 1) * P], kc[:, b, kv].rearrange("p c d -> p (c d)"), keep["ident"])
                    mm.then_inc(x_const, 1)

                    def body(i, cond, first):
                        for j in range(2):
                            t = 2 * i + j
                            pe.wait_ge(xr_ready, t + 1)
                            if not first:
                                pe.wait_ge(lo_ready, 2 * t - 2)
                            for b in range(NX):
                                mm = pe.transpose(tr[:, j, b // 4, (b % 4) * P:(b % 4 + 1) * P], xr[:, j, b].rearrange("p c d -> p (c d)"), keep["ident"])
                            mm.then_inc(tr_ready, 1)
                    pairs(pe, body)

        with ExitStack() as inner:
            s2 = Space(nc, inner, "soft")
            qh, ql = ([s2.sb(f"{n}{j}", [P, H, P], F32R) for j in range(2)] for n in ("qh", "ql"))
            prob = s2.sb("prob", [P, 2, (NC + NL) * P])
            pT = s2.sb("pT", [P, 2, 8, P])
            top = s2.sb("top", [P, 2, H])
            bias = s2.sb("bias", [P, 2, H])
            total = s2.sb("total", [P, 2, H])
            sb_in, sb_out, den, inv = (s2.sb(n, [P, 2, H]) for n in ("sb_in", "sb_out", "den", "inv"))
            mix = s2.sb("mix", [P, 2, 2 * GW])
            score = s2.ps("score", [P, 2, 2 * HALF])
            pTp = s2.ps("pTp", [P, 8, P])
            op = s2.ps("op", [P, 2, HALF])
            (q_ready, s_ready, top_ready, bias_ready, p_ready, pTp_ready, pTa_ready, pTd_ready, pv_ready, sin_ready, sout_ready,
             den_ready, inv_ready, o_ready) = (s2.sem(n) for n in (
                 "q_ready", "s_ready", "top_ready", "bias_ready", "p_ready", "pTp_ready", "pTa_ready", "pTd_ready", "pv_ready",
                 "sin_ready", "sout_ready", "den_ready", "inv_ready", "o_ready"))
            stored = [s2.sem(f"stored{j}") for j in range(2)]
            glo = GlaOutput(s2, keep, a, scratch, mix[:, :, 0:GW], stored)
            UNITS = 2 * H

            def tile_pairs(eng, body):
                body(0, 0, False)
                with eng.Fori(0, TS // P // 2) as i:
                    body(i + 1, i, True)

            def softmax_span(sample):
                return slice(0, (NC + NL) * P) if sample else slice(HALF, HALF + NTP * P)

            def blocks(sample):
                if sample:
                    return [(b * P, b) for b in range(NC + NL)]
                return [(HALF, 0), (HALF + P, NC)]

            def evac_slots(sample, engine):
                if sample:
                    return (slice(0, NC), slice(NC, NC + NL))[engine]
                return (slice(0, 1), slice(NC, NC + 1))[engine]

            with nc.Block() as block:

                @block.sync
                def _(sp):
                    glo.sp_gain(sp)
                    for j in range(2):
                        glo.sp_load(sp, j, j)

                    def body(i, last):
                        for j in range(2):
                            t = 2 * i + j
                            sp.wait_ge(glo.out_ready, t + 1)
                            sp.wait_ge(o_ready, t + 1)
                            sp.dma_start(scratch["mix"][tile_rows(t), :], mix[:, j]).then_inc(stored[j], 16)
                            if not last:
                                glo.sp_load(sp, t + 2, j)
                    with sp.Fori(0, NT // 2 - 1) as i:
                        body(i, False)
                    body(NT // 2 - 1, True)
                    for j in range(2):
                        sp.wait_ge(stored[j], 16 * NT // 2)

                @block.gpsimd
                def _(pool):
                    glo.pool_gain(pool)

                    def body(i, si, sample):
                        for j in range(2):
                            if sample:
                                pool.wait_ge(s_ready, UNITS * i - UNITS + H * j + H)
                            at = bass.ds((2 * i + j) * P, P)
                            pool.tensor_copy(qh[j][:, :, :], qhi[:, :, at]).then_inc(q_ready, 1)
                            pool.tensor_copy(ql[j][:, :, :], qlo[:, :, at]).then_inc(q_ready, 1)
                            glo.pool(pool, i, j, not sample)
                    tile_pairs(pool, body)

                @block.tensor
                def _(pe):
                    def body(i, si, sample):
                        def scores(n):
                            j, h = n // H, n % H
                            kv = h // (H // KV)
                            if h == 0:
                                pe.wait_ge(q_ready, 2 * (2 * i + j) + 2)
                            if sample or n >= 2:
                                pe.wait_ge(p_ready, UNITS * i + n - 1)
                            if sample:
                                st = 2 * si + j
                                keys = kT[:, kv, bass.ds((PAD + st) * P, NL * P)]
                                loc = score[:, n % 2, HALF:HALF + NL * P]
                                for part, q in enumerate((qh[j], ql[j])):
                                    pe.matmul(score[:, n % 2, 0:PAST], q[:, h], kcT[:, kv], start=(part == 0), stop=(part == 1))
                                    pe.matmul(loc, q[:, h], keys, start=(part == 0), stop=False)
                                pe.matmul(loc[:, 0:P], identb[:, :], win[:, bass.ds(st * P, P)], start=False, stop=False)
                                mm = pe.matmul(loc[:, 2 * P:3 * P], identb[:, :], win[:, bass.ds(TS + st * P, P)], start=False, stop=True)
                            else:
                                for part, q in enumerate((qh[j], ql[j])):
                                    mm = pe.matmul(score[:, n % 2, HALF:HALF + TP], q[:, h], kT[:, kv, 0:TP],
                                                   start=(part == 0), stop=(part == 1))
                            mm.then_inc(s_ready, 1)

                        def turn(n):
                            pe.wait_ge(p_ready, UNITS * i + n + 1)
                            if sample or n >= 1:
                                pe.wait_ge(pTa_ready, UNITS * i + n)
                                pe.wait_ge(pTd_ready, UNITS * i + n)
                            for col, slot in blocks(sample):
                                mm = pe.transpose(pTp[:, slot], prob[:, n % 2, col:col + P] if sample else prob[:, n % 2, col - HALF:col - HALF + P],
                                                  keep["ident"])
                            mm.then_inc(pTp_ready, 1)

                        def values(n):
                            j, h = n // H, n % H
                            kv = h // (H // KV)
                            if h == 0 and sample:
                                pe.wait_ge(o_ready, 2 * i + j - 1)
                            pe.wait_ge(pTa_ready, UNITS * i + n + 1)
                            pe.wait_ge(pTd_ready, UNITS * i + n + 1)
                            every = blocks(sample)
                            for m, (col, slot) in enumerate(every):
                                if sample and slot < NC:
                                    rhs = vc[:, slot, kv]
                                else:
                                    first = PAD + 2 * si + j if sample else 0
                                    off = slot - NC if sample else m
                                    rhs = v[:, bass.ds(first + off, 1), kv * DH:(kv + 1) * DH].rearrange("p t d -> p (t d)")
                                mm = pe.matmul(op[:, j, h * DH:(h + 1) * DH], pT[:, n % 2, slot], rhs,
                                               start=(m == 0), stop=(m == len(every) - 1))
                            mm.then_inc(pv_ready, 1)

                        scores(0)
                        for n in range(UNITS):
                            if n + 1 < UNITS:
                                scores(n + 1)
                            turn(n)
                            if n:
                                values(n - 1)
                        values(UNITS - 1)
                    tile_pairs(pe, body)

                @block.scalar
                def _(act):
                    def body(i, si, sample):
                        span = softmax_span(sample)

                        def evac(n):
                            act.wait_ge(pTp_ready, UNITS * i + n + 1)
                            if sample or n >= 2:
                                act.wait_ge(pv_ready, UNITS * i + n - 1)
                            sl = evac_slots(sample, 0)
                            act.activation(pT[:, n % 2, sl], pTp[:, sl], ACT.Copy).then_inc(pTa_ready, 1)

                        def sink_term(j):
                            act.wait_ge(sin_ready, 2 * i + j + 1)
                            act.activation(sb_out[:, j], sb_in[:, j], ACT.Exp).then_inc(sout_ready, 1)

                        for n in range(UNITS):
                            j, h = n // H, n % H
                            act.wait_ge(bias_ready, UNITS * i + n + 1)
                            if sample or n >= 2:
                                act.wait_ge(pTp_ready, UNITS * i + n - 1)
                            if h == 0 and sample:
                                act.wait_ge(den_ready, 2 * i + j - 1)
                            act.activation(prob[:, n % 2, 0:span.stop - span.start], score[:, n % 2, span], ACT.Exp,
                                           bias=bias[:, j, h:h + 1], scale=DH ** -0.5, accum_out=total[:, j, h:h + 1]).then_inc(p_ready, 1)
                            if n:
                                evac(n - 1)
                            if h == 0:
                                glo.act(act, i, j, not sample)
                            if n == H + 1:
                                sink_term(0)
                        evac(UNITS - 1)
                        sink_term(1)
                    tile_pairs(act, body)

                @block.vector
                def _(dve):
                    def body(i, si, sample):
                        span = softmax_span(sample)

                        def evac(n):
                            dve.wait_ge(pTp_ready, UNITS * i + n + 1)
                            if sample or n >= 2:
                                dve.wait_ge(pv_ready, UNITS * i + n - 1)
                            sl = evac_slots(sample, 1)
                            dve.tensor_copy(pT[:, n % 2, sl], pTp[:, sl]).then_inc(pTd_ready, 1)

                        def sink_in(j):
                            dve.wait_ge(bias_ready, UNITS * i + H * j + H)
                            dve.tensor_tensor(sb_in[:, j], sink[:, :], bias[:, j], ALU.add).then_inc(sin_ready, 1)

                        def finish(j):
                            dve.wait_ge(sout_ready, 2 * i + j + 1)
                            dve.wait_ge(p_ready, UNITS * i + H * j + H)
                            dve.tensor_tensor(den[:, j], sb_out[:, j], total[:, j], ALU.add).then_inc(den_ready, 1)
                            dve.wait_ge(den_ready, 2 * i + j + 1)
                            dve.reciprocal(inv[:, j], den[:, j]).then_inc(inv_ready, 1)
                            dve.wait_ge(inv_ready, 2 * i + j + 1)
                            dve.wait_ge(pv_ready, UNITS * i + H * j + H)
                            if sample:
                                dve.wait_ge(stored[j], 16 * i)
                            dve.tensor_tensor(mix[:, j, GW:2 * GW].rearrange("p (h d) -> p h d", d=DH), op[:, j].rearrange("p (h d) -> p h d", d=DH),
                                              inv[:, j].unsqueeze(2).broadcast_to([P, H, DH]), ALU.mult).then_inc(o_ready, 1)

                        for n in range(UNITS):
                            j, h = n // H, n % H
                            dve.wait_ge(s_ready, UNITS * i + n + 1)
                            dve.tensor_reduce(top[:, j, h:h + 1], score[:, n % 2, span], AX_X, ALU.max).then_inc(top_ready, 1)
                            dve.wait_ge(top_ready, UNITS * i + n + 1)
                            if h == 0 and sample:
                                dve.wait_ge(sin_ready, 2 * i + j - 1)
                            dve.tensor_scalar(bias[:, j, h:h + 1], top[:, j, h:h + 1], -DH ** -0.5, nsink[:, h:h + 1], ALU.mult, ALU.min).then_inc(bias_ready, 1)
                            if n:
                                evac(n - 1)
                            if h == 3:
                                glo.dve(dve, i, j, not sample)
                            if n == H:
                                sink_in(0)
                            if n == H + 2:
                                finish(0)
                        evac(UNITS - 1)
                        sink_in(1)
                        finish(1)
                    tile_pairs(dve, body)


def merge(nc, keep, a, scratch, hi, lo):
    WC = P // 2
    NW = D // WC
    with ExitStack() as ctx:
        s = Space(nc, ctx, "mrg")
        st = NormStage(s, keep, 1, hi, lo, slots=1)
        raw = s.sb("raw", [P, 2, KD, WC])
        whi = s.sb("whi", [P, KD, D], F32R)
        wlo = s.sb("wlo", [P, KD, D], F32R)
        mix = s.sb("mix", [P, 2, D])
        mhi = [s.sb(f"mhi{j}", [P, KD, P], F32R) for j in range(2)]
        mlo = [s.sb(f"mlo{j}", [P, KD, P], F32R) for j in range(2)]
        gate = s.sb("gate", [P, 2, D])
        mT = s.ps("mT", [P, KD, P])
        acc = s.ps("acc", [P, 2, 2, HALF])
        w_in = [s.sem(f"w_in{j}") for j in range(2)]
        x_in = [s.sem(f"x_in{j}") for j in range(2)]
        mix_in = [s.sem(f"mix_in{j}") for j in range(2)]
        x1_out = [s.sem(f"x1_out{j}") for j in range(2)]
        (gate_in, whi_ready, wlo_ready, mT_ready, mhi_ready, mlo_ready, acc_ready, gated, x1_ready) = (s.sem(n) for n in (
            "gate_in", "whi_ready", "wlo_ready", "mT_ready", "mhi_ready", "mlo_ready", "acc_ready", "gated", "x1_ready"))
        wv = a["w_o"][0].rearrange("(k p) n -> p k n", p=P)
        PAIRS = NT // 2

        def skewed(eng, ahead, main, behind):
            def pair(i, static):
                first, last, second = (static == 0), (static == PAIRS - 1), (static == 1)
                cond = 0 if first else 1
                ahead(i, 1, cond, first)
                main(i, 0, cond, first)
                if not first:
                    behind(i - 1, 1, 0 if second else 1, second)
                if not last:
                    ahead(i + 1, 0, 1, False)
                main(i, 1, cond, first)
                behind(i, 0, cond, first)
            ahead(0, 0, 0, True)
            pair(0, 0)
            pair(1, 1)
            with eng.Fori(2, PAIRS - 1) as i:
                pair(i, None)
            pair(PAIRS - 1, PAIRS - 1)
            behind(PAIRS - 1, 1, 1, False)

        def nothing(i, j, cond, first):
            pass

        with nc.Block() as block:

            @block.sync
            def _(sp):
                for j in range(2):
                    sp.dma_start(mix[:, j], scratch["mix"][j * P:(j + 1) * P, :]).then_inc(mix_in[j], 16)
                    sp.dma_start(st.x[:, j], a["x_prompt"][0, j * P:(j + 1) * P, :]).then_inc(x_in[j], 16)
                for c in range(2):
                    sp.dma_start(gate[:, c], scratch["mod"][c:c + 1, 2 * D:3 * D].broadcast_to([P, D])).then_inc(gate_in, 16)

                def tile(i, j, last):
                    t = 2 * i + j
                    if not last:
                        sp.wait_ge(mT_ready, t + 1)
                        sp.dma_start(mix[:, j], scratch["mix"][tile_rows(t + 2), :]).then_inc(mix_in[j], 16)
                    sp.wait_ge(x1_ready, t + 1)
                    sp.dma_start(scratch["x1"][tile_rows(t), :], st.x[:, j]).then_inc(x1_out[j], 16)
                    if not last:
                        sp.wait_ge(st.xn_ready, t + 1)
                        sp.wait_ge(st.ssq_ready, t + 1)
                        sp.wait_ge(x1_out[j], 16 * i + 16)
                        sp.dma_start(st.x[:, j], a["x_sample"][0, bass.ds((t + 2 - NTP) * P, P), :]).then_inc(x_in[j], 16)
                with sp.Fori(0, PAIRS - 1) as i:
                    for j in range(2):
                        tile(i, j, False)
                for j in range(2):
                    tile(PAIRS - 1, j, True)
                for j in range(2):
                    sp.wait_ge(x1_out[j], 16 * PAIRS)

            @block.scalar
            def _(act):
                def split(n):
                    act.wait_ge(w_in[n % 2], 16 * (n // 2 + 1))
                    act.activation(whi[:, :, n * WC:(n + 1) * WC], raw[:, n % 2], ACT.Copy).then_inc(whi_ready, 1)
                for n in range(2):
                    act.dma_start(raw[:, n], wv[:, :, n * WC:(n + 1) * WC]).then_inc(w_in[n], 16)
                for n in range(NW):
                    split(n)
                    if n + 2 < NW:
                        act.wait_ge(wlo_ready, n + 1)
                        act.dma_start(raw[:, n % 2], wv[:, :, (n + 2) * WC:(n + 3) * WC]).then_inc(w_in[n % 2], 16)

                def turn(i, j, cond, first):
                    t = 2 * i + j
                    act.wait_ge(mT_ready, t + 1)
                    if not first:
                        act.wait_ge(acc_ready, t - 1)
                    act.activation(mhi[j][:, :, :], mT[:, :, :], ACT.Copy).then_inc(mhi_ready, 1)

                def square(i, j, cond, first):
                    st.act_square(act, i, j, x1_ready, 2 * i + j + 1, first)

                def high(i, j, cond, first):
                    st.act_hi(act, i, j)
                skewed(act, turn, square, high)

            @block.gpsimd
            def _(pool):
                for n in range(NW):
                    pool.wait_ge(whi_ready, n + 1)
                    at = slice(n * WC, (n + 1) * WC)
                    pool.tensor_tensor(wlo[:, :, at], raw[:, n % 2], hi_view(whi)[:, :, at], ALU.subtract).then_inc(wlo_ready, 1)

                def rstd(i, j, cond, first):
                    st.pool_rstd(pool, i, j)

                def low(i, j, cond, first):
                    st.pool_lo(pool, i, j)
                skewed(pool, nothing, rstd, low)

            @block.vector
            def _(dve):
                def turn(i, j, cond, first):
                    t = 2 * i + j
                    dve.wait_ge(mhi_ready, t + 1)
                    if not first:
                        dve.wait_ge(acc_ready, t - 1)
                    dve.tensor_tensor(mlo[j][:, :, :], mT[:, :, :], hi_view(mhi[j]), ALU.subtract).then_inc(mlo_ready, 1)

                def residual(i, j, cond, first):
                    t = 2 * i + j
                    dve.wait_ge(acc_ready, t + 1)
                    if not first:
                        dve.wait_ge(st.xT_ready, t - 1)
                    dve.tensor_tensor(st.xn[:, j], acc[:, j].rearrange("p a b -> p (a b)"), gate[:, cond], ALU.mult).then_inc(gated, 1)
                    dve.wait_ge(gated, t + 1)
                    dve.wait_ge(x_in[j], 16 * i + 16)
                    dve.tensor_tensor(st.x[:, j], st.x[:, j], st.xn[:, j], ALU.add).then_inc(x1_ready, 1)
                    st.dve_xn(dve, i, j, first)

                def modulate(i, j, cond, first):
                    st.dve_modulate(dve, i, j, cond, first)
                dve.wait_ge(gate_in, 32)
                skewed(dve, turn, residual, modulate)

            @block.tensor
            def _(pe):
                def turn(i, j, cond, first):
                    t = 2 * i + j
                    pe.wait_ge(mix_in[j], 16 * i + 16)
                    if not (first and j == 0):
                        pe.wait_ge(mlo_ready, t)
                    for k in range(KD):
                        mm = pe.transpose(mT[:, k], mix[:, j, k * P:(k + 1) * P], keep["ident"])
                    mm.then_inc(mT_ready, 1)

                def products(i, j, cond, first):
                    t = 2 * i + j
                    pe.wait_ge(mlo_ready, t + 1)
                    if not first:
                        pe.wait_ge(gated, t - 1)
                    for half in range(2):
                        if first and j == 0:
                            pe.wait_ge(wlo_ready, NW // 2 * (half + 1))
                        at = slice(half * HALF, (half + 1) * HALF)
                        for k in range(KD):
                            out = acc[:, j, half]
                            pe.matmul(out, mhi[j][:, k], whi[:, k, at], start=(k == 0), stop=False)
                            pe.matmul(out, mhi[j][:, k], wlo[:, k, at], start=False, stop=False)
                            mm = pe.matmul(out, mlo[j][:, k], whi[:, k, at], start=False, stop=(k == KD - 1))
                    mm.then_inc(acc_ready, 1)

                def norm_turn(i, j, cond, first):
                    st.pe_transpose(pe, i, j, first)
                skewed(pe, turn, products, norm_turn)


def feed_forward(nc, a, scratch, hi, lo, outs):
    NF = DFF // P
    BLOCKS = ((0, HALF), (HALF, 2 * HALF), (2 * HALF, T))
    NB = len(BLOCKS)
    RING = 5
    with ExitStack() as ctx:
        s = Space(nc, ctx, "ff")
        acc = s.sb("acc", [P, NT, D])
        raw1 = s.sb("raw1", [P, 2, KD, P])
        raw2 = s.sb("raw2", [P, 2, D])
        w1hi, w1lo = ([s.sb(f"w1{n}{j}", [P, KD, P], F32R) for j in range(2)] for n in ("hi", "lo"))
        w2hi, w2lo = ([s.sb(f"w2{n}{j}", [P, D], F32R) for j in range(2)] for n in ("hi", "lo"))
        uhi, ulo = ([s.sb(f"u{n}{j}", [P, T], F32R) for j in range(2)] for n in ("hi", "lo"))
        relu = s.sb("relu", [P, 2, HALF])
        sq = s.sb("sq", [P, 2, HALF])
        up = s.ps("up", [P, NB, HALF])
        down = s.ps("down", [P, RING, HALF])
        w1_in = [s.sem(f"w1_in{j}") for j in range(2)]
        w2_in = [s.sem(f"w2_in{j}") for j in range(2)]
        (zeroed, w1hi_ready, w1lo_ready, w2hi_ready, w2lo_ready, up_ready, relu_ready, sq_ready, uhi_ready, ulo_ready,
         down_ready, added, gate_in, x1_in, gated, out_ready, stored) = (s.sem(n) for n in (
             "zeroed", "w1hi_ready", "w1lo_ready", "w2hi_ready", "w2lo_ready", "up_ready", "relu_ready", "sq_ready",
             "uhi_ready", "ulo_ready", "down_ready", "added", "gate_in", "x1_in", "gated", "out_ready", "stored"))
        w1v = a["w_ff1"][0].rearrange("(k p) n -> p k n", p=P)
        PER = 2 * NT
        gate = [relu[:, :, :].rearrange("p a b -> p (a b)"), sq[:, :, :].rearrange("p a b -> p (a b)")]
        x1 = [raw1[:, 0].rearrange("p k n -> p (k n)"), raw1[:, 1].rearrange("p k n -> p (k n)"), raw2[:, 0], raw2[:, 1]]

        def chunks(eng, body):
            with eng.Fori(0, NF // 2) as i:
                for j in range(2):
                    body(i, j)

        def store_tile(sp, t):
            sp.wait_ge(out_ready, t + 1)
            out = outs[0][0, t * P:(t + 1) * P, :] if t < NTP else outs[1][0, (t - NTP) * P:(t - NTP + 1) * P, :]
            sp.dma_start(out, acc[:, t]).then_inc(stored, 16)

        with nc.Block() as block:

            @block.sync
            def _(sp):
                def load(i, j):
                    c = 2 * i + j
                    sp.dma_start(raw1[:, j], w1v[:, :, bass.ds(c * P, P)]).then_inc(w1_in[j], 16)
                    sp.dma_start(raw2[:, j], a["w_ff2"][0, bass.ds(c * P, P), :]).then_inc(w2_in[j], 16)
                for j in range(2):
                    load(0, j)
                with sp.Fori(1, NF // 2) as i:
                    for j in range(2):
                        sp.wait_ge(w1lo_ready, 2 * i + j - 1)
                        sp.wait_ge(w2lo_ready, 2 * i + j - 1)
                        load(i, j)
                sp.wait_ge(ulo_ready, NB * NF)
                for cond in range(2):
                    sp.dma_start(gate[cond], scratch["mod"][cond:cond + 1, 5 * D:6 * D].broadcast_to([P, D])).then_inc(gate_in, 16)
                sp.wait_ge(w2lo_ready, NF)
                for t in range(NT):
                    if t >= len(x1):
                        sp.wait_ge(out_ready, t - len(x1) + 1)
                    sp.dma_start(x1[t % len(x1)], scratch["x1"][t * P:(t + 1) * P, :]).then_inc(x1_in, 16)
                    sp.wait_ge(x1_in, 16 * (t + 1))
                    if t >= 2:
                        store_tile(sp, t - 2)
                for t in range(NT - 2, NT):
                    store_tile(sp, t)
                sp.wait_ge(stored, 16 * NT)

            @block.scalar
            def _(act):
                def split(i, j, first):
                    c = 2 * i + j
                    act.wait_ge(w1_in[j], 16 * i + 16)
                    if not first:
                        act.wait_ge(up_ready, NB * (c - 1))
                    act.activation(w1hi[j][:, :, :], raw1[:, j], ACT.Copy).then_inc(w1hi_ready, 1)
                    act.wait_ge(w2_in[j], 16 * i + 16)
                    if not first:
                        act.wait_ge(down_ready, PER * (c - 1))
                    act.activation(w2hi[j][:, :], raw2[:, j], ACT.Copy).then_inc(w2hi_ready, 1)

                def hidden(i, j, first):
                    c = 2 * i + j
                    for b, (t0, t1) in enumerate(BLOCKS):
                        n = NB * c + b
                        m = (NB * j + b) % 2
                        w = t1 - t0
                        act.wait_ge(up_ready, n + 1)
                        if not (first and NB * j + b < 2):
                            act.wait_ge(sq_ready, n - 1)
                        act.activation(relu[:, m, 0:w], up[:, b, 0:w], ACT.Relu).then_inc(relu_ready, 1)
                        act.wait_ge(sq_ready, n + 1)
                        if not first:
                            act.wait_ge(down_ready, PER * (c - 1))
                        act.activation(uhi[j][:, t0:t1], sq[:, m, 0:w], ACT.Copy).then_inc(uhi_ready, 1)
                def body(i, first):
                    hidden(i, 1, first)
                    split(i + 1, 0, False)
                    hidden(i + 1, 0, False)
                    split(i + 1, 1, False)
                for j in range(2):
                    split(0, j, True)
                hidden(0, 0, True)
                body(0, True)
                with act.Fori(1, NF // 2 - 1) as i:
                    body(i, False)
                hidden(NF // 2 - 1, 1, False)

            @block.gpsimd
            def _(pool):
                def split(i, j):
                    c = 2 * i + j
                    pool.wait_ge(w1hi_ready, c + 1)
                    pool.tensor_tensor(w1lo[j][:, :, :], raw1[:, j], hi_view(w1hi[j]), ALU.subtract).then_inc(w1lo_ready, 1)
                    pool.wait_ge(w2hi_ready, c + 1)
                    pool.tensor_tensor(w2lo[j][:, :], raw2[:, j], w2hi[j][:, :].bitcast(F32), ALU.subtract).then_inc(w2lo_ready, 1)

                def hidden(i, j):
                    c = 2 * i + j
                    for b, (t0, t1) in enumerate(BLOCKS):
                        pool.wait_ge(uhi_ready, NB * c + b + 1)
                        pool.tensor_tensor(ulo[j][:, t0:t1], sq[:, (NB * j + b) % 2, 0:t1 - t0], uhi[j][:, t0:t1].bitcast(F32),
                                           ALU.subtract).then_inc(ulo_ready, 1)
                for j in range(2):
                    split(0, j)
                hidden(0, 0)
                with pool.Fori(0, NF // 2 - 1) as i:
                    hidden(i, 1)
                    split(i + 1, 0)
                    hidden(i + 1, 0)
                    split(i + 1, 1)
                hidden(NF // 2 - 1, 1)
                pool.wait_ge(gate_in, 32)
                for t in range(NT):
                    pool.wait_ge(x1_in, 16 * (t + 1))
                    pool.wait_ge(gated, 2 * (t + 1))
                    pool.tensor_tensor(acc[:, t], acc[:, t], x1[t % len(x1)], ALU.add).then_inc(out_ready, 1)

            @block.vector
            def _(dve):
                for t in range(NT):
                    dve.memset(acc[:, t], 0.0).then_inc(zeroed, 1)

                def square(c, b, j, first):
                    t0, t1 = BLOCKS[b]
                    n = NB * c + b
                    m = (NB * j + b) % 2
                    w = t1 - t0
                    dve.wait_ge(relu_ready, n + 1)
                    if not (first and NB * j + b < 2):
                        dve.wait_ge(ulo_ready, n - 1)
                    dve.tensor_tensor(sq[:, m, 0:w], relu[:, m, 0:w], relu[:, m, 0:w], ALU.mult).then_inc(sq_ready, 1)

                def add(c, t, half, first):
                    n = 2 * t + half
                    dve.wait_ge(down_ready, PER * c + n + 1)
                    at = slice(half * HALF, (half + 1) * HALF)
                    if not first:
                        dve.wait_ge(added, PER * (c - 1) + n + 1)
                    dve.tensor_tensor(acc[:, t, at], acc[:, t, at], down[:, n % RING], ALU.add).then_inc(added, 1)

                def body(i, j, first):
                    c = 2 * i + j
                    for t in range(NT):
                        for half in range(2):
                            if t in (0, 2, 4) and half == 0:
                                square(c + 1, t // 2, 1 - j, first and j == 0)
                            add(c, t, half, first and j == 0)
                for b in range(NB):
                    square(0, b, 0, True)
                dve.wait_ge(zeroed, NT)
                for j in range(2):
                    body(0, j, True)
                with dve.Fori(1, NF // 2 - 1) as i:
                    for j in range(2):
                        body(i, j, False)
                body(NF // 2 - 1, 0, False)
                c = NF - 1
                dve.wait_ge(gate_in, 32)
                for t in range(NT):
                    for half in range(2):
                        add(c, t, half, False)
                        at = slice(half * HALF, (half + 1) * HALF)
                        dve.wait_ge(added, PER * c + 2 * t + half + 1)
                        dve.tensor_tensor(acc[:, t, at], acc[:, t, at], gate[0 if t < NTP else 1][:, at], ALU.mult).then_inc(gated, 1)

            @block.tensor
            def _(pe):
                def first_product(c, i, j, first):
                    pe.wait_ge(w1lo_ready, c + 1)
                    for b, (t0, t1) in enumerate(BLOCKS):
                        if not first:
                            pe.wait_ge(relu_ready, NB * (c - 1) + b + 1)
                        out = up[:, b, 0:t1 - t0]
                        for k in range(KD):
                            pe.matmul(out, w1hi[j][:, k, :], hi[:, k, t0:t1], start=(k == 0), stop=False)
                            pe.matmul(out, w1hi[j][:, k, :], lo[:, k, t0:t1], start=False, stop=False)
                            mm = pe.matmul(out, w1lo[j][:, k, :], hi[:, k, t0:t1], start=False, stop=(k == KD - 1))
                        mm.then_inc(up_ready, 1)

                def second_product(c, j, first):
                    pe.wait_ge(w2lo_ready, c + 1)
                    for t in range(NT):
                        if t in (0, 4, 8):
                            pe.wait_ge(ulo_ready, NB * c + t // 4 + 1)
                        for half in range(2):
                            n = 2 * t + half
                            at = slice(half * HALF, (half + 1) * HALF)
                            if not (first and n < RING):
                                pe.wait_ge(added, PER * c + n - RING + 1)
                            out = down[:, n % RING]
                            x_hi, x_lo = (x[j][:, t * P:(t + 1) * P] for x in (uhi, ulo))
                            pe.matmul(out, x_hi, w2hi[j][:, at], start=True, stop=False)
                            pe.matmul(out, x_hi, w2lo[j][:, at], start=False, stop=False)
                            pe.matmul(out, x_lo, w2hi[j][:, at], start=False, stop=True).then_inc(down_ready, 1)

                first_product(0, 0, 0, True)
                first_product(1, 0, 1, False)
                second_product(0, 0, True)
                first_product(2, 1, 0, False)
                second_product(1, 1, False)
                with pe.Fori(1, NF // 2 - 1) as i:
                    first_product(2 * i + 1, i, 1, False)
                    second_product(2 * i, 0, False)
                    first_product(2 * i + 2, i + 1, 0, False)
                    second_product(2 * i + 1, 1, False)
                first_product(NF - 1, NF // 2 - 1, 1, False)
                second_product(NF - 2, 0, False)
                second_product(NF - 1, 1, False)




def build(nc, a, outs):
    scratch = {
        "mod": nc.dram_tensor("mod_rows", (2, 6 * D), F32, kind="Internal").ap(),
        "proj": nc.dram_tensor("proj", (T, DIN), F32, kind="Internal").ap(),
        "o": nc.dram_tensor("gla_out", (2, T, GW), F32, kind="Internal").ap(),
        "mix": nc.dram_tensor("mix", (T, D), F32, kind="Internal").ap(),
        "x1": nc.dram_tensor("x1", (T, D), F32, kind="Internal").ap(),
    }
    with ExitStack() as ctx:
        s = Space(nc, ctx, "keep")
        mats = s.sb("mats", [P, 5 * P + 8])
        keep = {
            "mats": mats,
            "ident": mats[:, 0:P],
            "cum": [mats[:, P * (1 + d):P * (2 + d)] for d in range(2)],
            "causal": [mats[:, P * (3 + d):P * (4 + d)] for d in range(2)],
            "vec": [mats[:, 5 * P + 4 * d:5 * P + 4 * d + 4] for d in range(2)],
            "minus_half": s.sb("minus_half", [P, 16]),
            "eps_d": s.sb("eps_d", [P, 16]),
            "eps_h": s.sb("eps_h", [P, 16]),
            "shift": s.sb("shift", [P, 2, KD, 2]),
            "scale": s.sb("scale", [P, 2, KD, 2]),
        }
        modulation(nc, keep, a, scratch)
        with ExitStack() as inner:
            s1 = Space(nc, inner, "h1")
            hi = s1.sb("hi", [P, KD, T], F32R)
            lo = s1.sb("lo", [P, KD, T], F32R)
            norm_first(nc, keep, a, hi, lo)
            project(nc, a, hi, lo, scratch)
        gla(nc, keep, a, scratch, outs)
        attention(nc, keep, a, scratch, outs)
        with ExitStack() as inner:
            s2 = Space(nc, inner, "h2")
            hi = s2.sb("hi", [P, KD, T], F32R)
            lo = s2.sb("lo", [P, KD, T], F32R)
            merge(nc, keep, a, scratch, hi, lo)
            feed_forward(nc, a, scratch, hi, lo, outs)


INPUTS = ("x_prompt", "x_sample", "c", "cache_k", "cache_v", "state_gla_fwd", "state_gla_bwd", "c_ctx", "w_ada", "b_ada",
          "norm_mix", "norm_ff", "w_in", "w_gk_fwd", "b_gk_fwd", "w_gk_bwd", "b_gk_bwd", "gla_norm", "q_norm", "k_norm",
          "sink", "w_o", "w_ff1", "w_ff2")
OUTPUTS = ((1, TP, D), (1, TS, D), (1, 1, KV, TP, DH), (1, 1, KV, TP, DH), (1, 1, H, DH, DH), (1, 1, H, DH, DH))


def kernel(**inputs):
    import concourse.bacc as bacc
    from concourse.bass_utils import run_bass_kernel_spmd

    nc = bacc.Bacc("TRN2", target_bir_lowering=False, num_devices=1)
    arrays = {name: np.ascontiguousarray(inputs[name]) for name in INPUTS}
    arrays["mats"], arrays["window"], arrays["rope"] = constants()
    args = {n: nc.dram_tensor(f"in_{n}", x.shape, mybir.dt.from_np(x.dtype), kind="ExternalInput").ap()
            for n, x in arrays.items()}
    outs = [nc.dram_tensor(f"out_{i}", shape, F32, kind="ExternalOutput").ap() for i, shape in enumerate(OUTPUTS)]
    build(nc, args, outs)
    r = run_bass_kernel_spmd(nc, [{f"in_{n}": x for n, x in arrays.items()}], core_ids=[0])
    return tuple(r.results[0][f"out_{i}"] for i in range(len(OUTPUTS)))
```

```python
from contextlib import ExitStack

import numpy as np

import concourse.bass as bass
from concourse import mybir

F32 = mybir.dt.float32
F32R = mybir.dt.float32r
BF16 = mybir.dt.bfloat16
ALU = mybir.AluOpType
ACT = mybir.ActivationFunctionType
AX_X = mybir.AxisListType.X

P = 128
D = 1024
KD = D // P
TP, TS = 256, 1024
T = TP + TS
NT, NTP = T // P, TP // P
PAST = 512
H = 8
DH = 64
KV = 2
GW = H * DH
RANK = 16
DIN = 4 * GW + 2 * RANK + GW + 2 * KV * DH
C_GG, C_LR, C_SQ = 3 * GW, 4 * GW, 4 * GW + 2 * RANK
DFF = 4 * D
EPS = 1e-6
NEG = -1e30
GRID_W = 64
THETA = 10000.0
GATE_TEMP = 16.0
CLAMP = 42.0
HALF = 512


def constants():
    j = np.arange(P)[:, None]
    i = np.arange(P)[None, :]
    mid = P // 2
    cum_f = ((j <= i).astype(np.float32) - (j < mid)) / GATE_TEMP
    cum_b = ((j >= i).astype(np.float32) - (j >= mid)) / GATE_TEMP
    vec_f = np.zeros((P, 4), np.float32)
    vec_f[:mid, 0] = 1 / GATE_TEMP
    vec_f[:, 1] = 1 / GATE_TEMP
    vec_f[mid:, 2] = 1 / GATE_TEMP
    vec_b = vec_f.copy()
    vec_b[:, 0], vec_b[:, 2] = vec_f[:, 2], vec_f[:, 0]
    keep_f = (j <= i).astype(np.float32)
    keep_b = (j >= i).astype(np.float32)
    ident = np.eye(P, dtype=np.float32)
    mats = np.concatenate([ident, cum_f, cum_b, keep_f, keep_b, vec_f, vec_b], 1).astype(np.float32)
    tiles = TS // P
    left = np.where(i >= j, 0.0, NEG)
    right = np.where(i <= j, 0.0, NEG)
    none = np.full((P, P), NEG)
    left_all = np.concatenate([none] + [left] * (tiles - 1), 1)
    right_all = np.concatenate([right] * (tiles - 1) + [none], 1)
    window = np.concatenate([left_all, right_all], 1).astype(np.float32)
    half = DH // 4
    freqs = (THETA ** (-np.arange(half, dtype=np.float32) / half)).astype(np.float32)
    t = np.arange(TS)
    row = (t // GRID_W).astype(np.float32)[:, None] * freqs
    col = (t % GRID_W).astype(np.float32)[:, None] * freqs
    cos = np.concatenate([np.cos(row), np.cos(row), np.cos(col), np.cos(col)], 1)
    sin = np.concatenate([-np.sin(row), np.sin(row), -np.sin(col), np.sin(col)], 1)
    cos = np.concatenate([np.ones((TP, DH)), cos], 0).astype(np.float32)
    sin = np.concatenate([np.zeros((TP, DH)), sin], 0).astype(np.float32)
    rope = np.stack([cos, sin], 1)
    return mats, window, rope


class Space:

    def __init__(self, nc, ctx, prefix):
        self.nc, self.ctx, self.prefix, self.sems = nc, ctx, prefix, []
        ctx.callback(self.clear)

    def sb(self, name, shape, dt=F32):
        return self.ctx.enter_context(self.nc.sbuf_tensor(f"{self.prefix}_{name}", shape, dt))

    def ps(self, name, shape, dt=F32):
        return self.ctx.enter_context(self.nc.psum_tensor(f"{self.prefix}_{name}", shape, dt))

    def sem(self, name):
        self.sems.append(self.nc.alloc_semaphore(f"{self.prefix}_{name}"))
        return self.sems[-1]

    def clear(self):
        if self.sems:
            self.nc.clear_and_free_semaphores(self.sems)
            self.nc.all_engine_barrier()


def tile_rows(t):
    return bass.ds(t * P, P)


class NormStage:

    def __init__(self, s, keep, which, hi, lo, slots=2):
        self.slots = slots
        self.keep, self.which, self.hi, self.lo = keep, which, hi, lo
        self.x = s.sb("x", [P, 2, D])
        self.ssq = s.sb("ssq", [P, 2])
        self.ms = s.sb("ms", [P, 2])
        self.rstd = s.sb("rstd", [P, 2])
        self.xn = s.sb("xn", [P, 2, D])
        self.h = s.sb("h", [P, slots, KD, P])
        self.xT = s.ps("xT", [P, slots, KD, P])
        self.ssq_ready, self.ms_ready = s.sem("ssq_ready"), s.sem("ms_ready")
        self.rstd_ready, self.xn_ready = s.sem("rstd_ready"), s.sem("xn_ready")
        self.xT_ready, self.h_ready = s.sem("xT_ready"), s.sem("h_ready")
        self.hi_ready, self.lo_ready = s.sem("hi_ready"), s.sem("lo_ready")

    def act_square(self, act, i, j, ready, value, first):
        act.wait_ge(ready, value)
        if not first:
            act.wait_ge(self.xT_ready, 2 * i + j - 1)
        act.activation(self.xn[:, j], self.x[:, j], ACT.Square, accum_out=self.ssq[:, j:j + 1]).then_inc(self.ssq_ready, 1)

    def pool_rstd(self, pool, i, j):
        t = 2 * i + j
        pool.wait_ge(self.ssq_ready, t + 1)
        pool.tensor_tensor(self.ms[:, j:j + 1], self.ssq[:, j:j + 1], self.keep["eps_d"][:, 0:1], ALU.add).then_inc(self.ms_ready, 1)
        pool.wait_ge(self.ms_ready, t + 1)
        pool.tensor_tensor(self.rstd[:, j:j + 1], self.ms[:, j:j + 1], self.keep["minus_half"][:, 0:1], ALU.pow).then_inc(self.rstd_ready, 1)

    def dve_xn(self, dve, i, j, first):
        t = 2 * i + j
        dve.wait_ge(self.rstd_ready, t + 1)
        if not first:
            dve.wait_ge(self.xT_ready, t - 1)
        dve.tensor_scalar(self.xn[:, j], self.x[:, j], self.rstd[:, j:j + 1], D ** 0.5, ALU.mult, ALU.mult).then_inc(self.xn_ready, 1)

    def pe_transpose(self, pe, i, j, first):
        t = 2 * i + j
        m = j % self.slots
        pe.wait_ge(self.xn_ready, t + 1)
        if not (first and j < self.slots):
            pe.wait_ge(self.h_ready, t + 1 - self.slots)
        for k in range(KD):
            tr = pe.transpose(self.xT[:, m, k], self.xn[:, j, k * P:(k + 1) * P], self.keep["ident"])
        tr.then_inc(self.xT_ready, 1)

    def dve_modulate(self, dve, i, j, cond, first):
        t = 2 * i + j
        m = j % self.slots
        dve.wait_ge(self.xT_ready, t + 1)
        if not (first and j < self.slots):
            dve.wait_ge(self.lo_ready, t + 1 - self.slots)
        for k in range(KD):
            op = dve.tensor_scalar(self.h[:, m, k], self.xT[:, m, k], self.keep["scale"][:, self.which, k, cond:cond + 1],
                                   self.keep["shift"][:, self.which, k, cond:cond + 1], ALU.mult, ALU.add)
        op.then_inc(self.h_ready, 1)

    def act_hi(self, act, i, j):
        t = 2 * i + j
        act.wait_ge(self.h_ready, t + 1)
        act.activation(self.hi[:, :, tile_rows(t)], self.h[:, j % self.slots], ACT.Copy).then_inc(self.hi_ready, 1)

    def pool_lo(self, pool, i, j):
        t = 2 * i + j
        pool.wait_ge(self.hi_ready, t + 1)
        pool.tensor_tensor(self.lo[:, :, tile_rows(t)], self.h[:, j % self.slots], hi_view(self.hi)[:, :, tile_rows(t)],
                           ALU.subtract).then_inc(self.lo_ready, 1)


def hi_view(hi):
    return hi[:, :, :].bitcast(F32)


def pairs(engine, body):
    body(0, 0, True)
    with engine.Fori(1, NT // 2) as i:
        body(i, 1, False)


def modulate_and_norm(nc, keep, a, raw, hi, lo, scratch):
    COLS = HALF
    NCH = 6 * D // COLS
    BEFORE = 2 * D // COLS
    PAIRS = NT // 2
    assert NCH == BEFORE + 2 * (PAIRS - 1)
    PARTS = ((0, 1), (3, 4))
    with ExitStack() as ctx:
        s = Space(nc, ctx, "n1")
        st = NormStage(s, keep, 0, hi, lo)
        w = s.sb("w", [P, 2, KD, COLS])
        cond = s.sb("cond", [P, 2, KD])
        e = s.sb("e", [P, 2, KD])
        e1 = s.sb("e1", [P, 2, KD])
        rec = s.sb("rec", [P, 2, KD])
        silu = s.sb("silu", [P, KD, 2])
        rows = s.sb("rows", [2, 6 * D])
        gain = s.sb("gain", [P, 2, KD])
        acc = s.ps("acc", [2, 2, COLS])
        cols = s.ps("cols", [P, 2, 2, KD, 2])
        x_in = [s.sem(f"x_in{j}") for j in range(2)]
        w_in = [s.sem(f"w_in{j}") for j in range(2)]
        (const_ready, cond_in, small_in, e_ready, e1_ready, rec_ready, silu_ready, acc_ready, rows_ready, cols_ready, mod_ready,
         scaled, rows_out, raw_in) = (s.sem(n) for n in (
             "const_ready", "cond_in", "small_in", "e_ready", "e1_ready", "rec_ready", "silu_ready", "acc_ready", "rows_ready",
             "cols_ready", "mod_ready", "scaled", "rows_out", "raw_in"))
        wv = a["w_ada"][0].rearrange("(k p) n -> p k n", p=P)
        with nc.Block() as block:

            @block.sync
            def _(sp):
                sp.dma_start(cond[:, 0, :], a["c_ctx"].rearrange("(k p) -> p k", p=P), allow_slow_non_contiguous=True).then_inc(cond_in, 16)
                sp.dma_start(cond[:, 1, :], a["c"][0].rearrange("(k p) -> p k", p=P), allow_slow_non_contiguous=True).then_inc(cond_in, 16)

                def load(c, j, first):
                    if not first:
                        sp.wait_ge(acc_ready, c - 1)
                    sp.dma_start(w[:, j], wv[:, :, bass.ds(c * COLS, COLS)]).then_inc(w_in[j], 16)
                for j in range(2):
                    load(j, j, True)
                sp.dma_start(rows[:, :], a["b_ada"].broadcast_to([2, 6 * D])).then_inc(small_in, 16)
                sp.dma_start(gain[:, 0, :], a["norm_mix"][0].rearrange("(k p) -> p k", p=P), allow_slow_non_contiguous=True).then_inc(small_in, 16)
                sp.dma_start(gain[:, 1, :], a["norm_ff"][0].rearrange("(k p) -> p k", p=P), allow_slow_non_contiguous=True).then_inc(small_in, 16)
                sp.dma_start(keep["mats"][:, :], a["mats"]).then_inc(small_in, 16)
                for j in range(2):
                    sp.dma_start(st.x[:, j], a["x_prompt"][0, j * P:(j + 1) * P, :]).then_inc(x_in[j], 16)
                for c in range(2, BEFORE + 2):
                    load(c, c % 2, False)

                def body(i, last):
                    for j in range(2):
                        sp.wait_ge(st.xn_ready, 2 * i + j - 1)
                        sp.dma_start(st.x[:, j], a["x_sample"][0, bass.ds((2 * i + j - NTP) * P, P), :]).then_inc(x_in[j], 16)
                    for j in range(2):
                        if not last:
                            load(2 * i + j + BEFORE, j, False)
                with sp.Fori(1, PAIRS - 1) as i:
                    body(i, False)
                body(PAIRS - 1, True)
                for j in range(2):
                    load_group(sp, a, raw, j, j).then_inc(raw_in, 16)
                sp.wait_ge(rows_ready, NCH)
                sp.dma_start(scratch["mod"], rows[:, :]).then_inc(rows_out, 16)
                sp.wait_ge(rows_out, 16)
                sp.wait_ge(raw_in, 32)

            @block.scalar
            def _(act):
                act.wait_ge(cond_in, 2 * 16)
                act.activation(e[:, :, :], cond[:, :, :], ACT.Exp, scale=-1.0).then_inc(e_ready, 1)

                def body(i, cond, first):
                    for j in range(2):
                        st.act_square(act, i, j, x_in[j], 16 * i + 16, first)
                    for j in range(2):
                        st.act_hi(act, i, j)
                pairs(act, body)

            @block.gpsimd
            def _(pool):
                pool.memset(keep["minus_half"][:, :], -0.5).then_inc(const_ready, 1)
                pool.memset(keep["eps_d"][:, :], D * EPS).then_inc(const_ready, 1)
                pool.memset(keep["eps_h"][:, :], DH * EPS).then_inc(const_ready, 1)
                pool.wait_ge(const_ready, 3)

                def body(i, cond, first):
                    for j in range(2):
                        st.pool_rstd(pool, i, j)
                    for j in range(2):
                        st.pool_lo(pool, i, j)
                pairs(pool, body)

            @block.vector
            def _(dve):
                dve.wait_ge(e_ready, 1)
                dve.tensor_scalar(e1[:, :, :], e[:, :, :], 1.0, None, ALU.add).then_inc(e1_ready, 1)
                dve.wait_ge(e1_ready, 1)
                dve.reciprocal(rec[:, :, :], e1[:, :, :]).then_inc(rec_ready, 1)
                dve.wait_ge(rec_ready, 1)
                dve.tensor_tensor(silu[:, :, :], cond[:, :, :].rearrange("p c k -> p k c"),
                                  rec[:, :, :].rearrange("p c k -> p k c"), ALU.mult).then_inc(silu_ready, 1)

                def add_bias(c, j):
                    dve.wait_ge(acc_ready, c + 1)
                    at = bass.ds(c * COLS, COLS)
                    dve.tensor_tensor(rows[:, at], acc[:, j], rows[:, at], ALU.add).then_inc(rows_ready, 1)

                def columns(n):
                    dve.wait_ge(cols_ready, n + 1)
                    dve.tensor_copy(keep["shift"][:, n], cols[:, n, 0]).then_inc(mod_ready, 1)
                    dve.tensor_scalar(keep["scale"][:, n], cols[:, n, 1], 1.0, None, ALU.add).then_inc(mod_ready, 1)
                    dve.wait_ge(mod_ready, 2 * n + 2)
                    for c in range(2):
                        dve.tensor_tensor(keep["scale"][:, n, :, c], keep["scale"][:, n, :, c], gain[:, n, :],
                                          ALU.mult).then_inc(scaled, 1)

                dve.wait_ge(small_in, 4 * 16)
                for c in range(2):
                    add_bias(c, c)
                for j in range(2):
                    st.dve_xn(dve, 0, j, True)
                for c in range(2, BEFORE):
                    add_bias(c, c % 2)
                columns(0)
                dve.wait_ge(scaled, 2)
                for j in range(2):
                    st.dve_modulate(dve, 0, j, 0, True)
                with dve.Fori(1, PAIRS) as i:
                    for j in range(2):
                        st.dve_xn(dve, i, j, False)
                    for j in range(2):
                        add_bias(2 * i + j + BEFORE - 2, j)
                    for j in range(2):
                        st.dve_modulate(dve, i, j, 1, False)
                columns(1)

            @block.tensor
            def _(pe):
                def product(c, i, j, first):
                    pe.wait_ge(w_in[j], 16 * i + 16)
                    if not first:
                        pe.wait_ge(rows_ready, c - 1)
                    for k in range(KD):
                        mm = pe.matmul(acc[:, j], silu[:, k, :], w[:, j, k, :], start=(k == 0), stop=(k == KD - 1))
                    mm.then_inc(acc_ready, 1)

                def columns(n):
                    for m, part in enumerate(PARTS[n]):
                        for k in range(KD):
                            at = part * D + k * P
                            tr = pe.transpose(cols[:, n, m, k, :], rows[0:2, at:at + P], keep["ident"][0:2, 0:2])
                    tr.then_inc(cols_ready, 1)

                def body(i, first, last):
                    for j in range(2):
                        st.pe_transpose(pe, i, j, first)
                    if not last:
                        for j in range(2):
                            product(2 * i + j + BEFORE, i + BEFORE // 2, j, False)

                pe.wait_ge(silu_ready, 1)
                for c in range(BEFORE):
                    product(c, c // 2, c % 2, c < 2)
                pe.wait_ge(small_in, 4 * 16)
                pe.wait_ge(rows_ready, BEFORE)
                columns(0)
                body(0, True, False)
                with pe.Fori(1, PAIRS - 1) as i:
                    body(i, False, False)
                body(PAIRS - 1, False, True)
                pe.wait_ge(rows_ready, NCH)
                columns(1)


NG = 8
COLS_IN = DIN // NG


def group(g):
    return bass.ds(g * -COLS_IN + (NG - 1) * COLS_IN, COLS_IN)


def load_group(eng, a, raw, g, j):
    return eng.dma_start(raw[:, j], a["w_in"][0].rearrange("(k p) n -> p k n", p=P)[:, :, group(g)])


class HeadsPrep:
    NX = H + KV
    WX = NX * DH

    def __init__(self, s, keep, a, scratch, outs):
        self.keep, self.a, self.scratch, self.outs = keep, a, scratch, outs
        WX, NX = self.WX, self.NX
        self.x, self.xg, self.xr = s.sb("x", [P, 2, WX + KV * DH]), s.sb("xg", [P, 2, WX]), s.sb("xr", [P, 2, WX])
        self.sq, self.xn, self.xc, self.xs = (s.sb(n, [P, WX]) for n in ("sq", "xn", "xc", "xs"))
        self.ssq, self.ms, self.rstd = (s.sb(n, [P, NX]) for n in ("ssq", "ms", "rstd"))
        self.gain = s.sb("gain", [P, NX, DH])
        self.rope = s.sb("rope", [P, NT, 2 * DH])
        (self.const_in, self.sq_ready, self.ssq_ready, self.ms_ready, self.rstd_ready, self.xn_ready, self.xg_ready,
         self.xc_ready, self.xs_ready, self.xr_ready, self.kv_out) = (s.sem(n) for n in (
             "const_in", "sq_ready", "ssq_ready", "ms_ready", "rstd_ready", "xn_ready", "xg_ready", "xc_ready", "xs_ready",
             "xr_ready", "kv_out"))
        self.x_in = [s.sem(f"x_in{j}") for j in range(2)]
        self.xr_out = [s.sem(f"xr_out{j}") for j in range(2)]
        self.CONSTS = 16 * (NX + 1)
        self.KV_OUT = 16 * 2 * KV * NTP

    @staticmethod
    def heads(y):
        return y.rearrange("p (h d) -> p h d", d=DH)

    @staticmethod
    def axes(y):
        return y.rearrange("p (h a b f) -> p h a b f", a=2, b=2, f=DH // 4)

    def sp_constants(self, sp):
        for h in range(self.NX):
            sp.dma_start(self.gain[:, h], self.a["q_norm" if h < H else "k_norm"].broadcast_to([P, DH])).then_inc(self.const_in, 16)
        sp.dma_start(self.rope[:, :, :], self.a["rope"].rearrange("(t p) c d -> p t (c d)", p=P)).then_inc(self.const_in, 16)

    def sp_load(self, sp, t):
        if t >= 2:
            sp.wait_ge(self.xn_ready, t - 1)
            sp.wait_ge(self.sq_ready, t - 1)
        if 2 <= t < 2 + NTP:
            sp.wait_ge(self.kv_out, self.KV_OUT // NTP * (t - 1))
        sp.dma_start(self.x[:, t % 2], self.scratch["proj"][t * P:(t + 1) * P, C_SQ:DIN]).then_inc(self.x_in[t % 2], 16)

    def sp_store(self, sp, t):
        if t < NTP:
            sp.wait_ge(self.xg_ready, t + 1)
            for kv in range(KV):
                at = GW + kv * DH
                sp.dma_start(self.outs[2][0, 0, kv, t * P:(t + 1) * P, :], self.xg[:, t, at:at + DH]).then_inc(self.kv_out, 16)
                at = self.WX + kv * DH
                sp.dma_start(self.outs[3][0, 0, kv, t * P:(t + 1) * P, :], self.x[:, t, at:at + DH]).then_inc(self.kv_out, 16)
        sp.wait_ge(self.xr_ready, t + 1)
        sp.dma_start(self.scratch["qk"][t * P:(t + 1) * P, :], self.xr[:, t % 2]).then_inc(self.xr_out[t % 2], 16)

    def pool(self, pool, t):
        j = t % 2
        pool.wait_ge(self.x_in[j], 16 * (t // 2 + 1))
        if t == 0:
            pool.wait_ge(self.const_in, self.CONSTS)
        else:
            pool.wait_ge(self.ssq_ready, t)
        pool.tensor_tensor(self.sq[:, :], self.x[:, j, 0:self.WX], self.x[:, j, 0:self.WX], ALU.mult).then_inc(self.sq_ready, 1)
        pool.wait_ge(self.ssq_ready, t + 1)
        pool.tensor_tensor(self.ms[:, :], self.ssq[:, :], self.keep["eps_h"][:, 0:self.NX], ALU.add).then_inc(self.ms_ready, 1)
        pool.wait_ge(self.ms_ready, t + 1)
        if t:
            pool.wait_ge(self.xn_ready, t)
        pool.tensor_tensor(self.rstd[:, :], self.ms[:, :], self.keep["minus_half"][:, 0:self.NX], ALU.pow).then_inc(self.rstd_ready, 1)
        pool.wait_ge(self.xn_ready, t + 1)
        if t == 2:
            pool.wait_ge(self.kv_out, self.KV_OUT)
        if t >= 2:
            pool.wait_ge(self.xc_ready, t - 1)
        pool.tensor_tensor(self.xg[:, j], self.xn[:, :], self.gain[:, :, :].rearrange("p h d -> p (h d)"), ALU.mult).then_inc(self.xg_ready, 1)
        pool.wait_ge(self.xg_ready, t + 1)
        if t:
            pool.wait_ge(self.xr_ready, t)
        sin = self.axes(self.rope[:, t, DH:2 * DH])
        for b in range(2):
            pool.tensor_tensor(self.axes(self.xs[:, :])[:, :, :, b], self.axes(self.xg[:, j])[:, :, :, 1 - b],
                               sin[:, :, :, b].broadcast_to([P, self.NX, 2, DH // 4]), ALU.mult).then_inc(self.xs_ready, 1)

    def dve_sum(self, dve, t):
        dve.wait_ge(self.sq_ready, t + 1)
        if t:
            dve.wait_ge(self.ms_ready, t)
        dve.tensor_reduce(self.ssq[:, :], self.heads(self.sq[:, :]), AX_X, ALU.add).then_inc(self.ssq_ready, 1)

    def dve_rotate(self, dve, t):
        j, NX = t % 2, self.NX
        dve.wait_ge(self.rstd_ready, t + 1)
        if t:
            dve.wait_ge(self.xg_ready, t)
        dve.scalar_tensor_tensor(self.heads(self.xn[:, :]), self.heads(self.x[:, j, 0:self.WX]), DH ** 0.5,
                                 self.rstd[:, :].unsqueeze(2).broadcast_to([P, NX, DH]), ALU.mult, ALU.mult).then_inc(self.xn_ready, 1)
        dve.wait_ge(self.xg_ready, t + 1)
        if t:
            dve.wait_ge(self.xr_ready, t)
        dve.tensor_tensor(self.heads(self.xc[:, :]), self.heads(self.xg[:, j]),
                          self.rope[:, t:t + 1, 0:DH].broadcast_to([P, NX, DH]), ALU.mult).then_inc(self.xc_ready, 1)
        dve.wait_ge(self.xc_ready, t + 1)
        dve.wait_ge(self.xs_ready, 2 * t + 2)
        if t >= 2:
            dve.wait_ge(self.xr_out[j], 16 * (t // 2))
        dve.tensor_tensor(self.xr[:, j], self.xc[:, :], self.xs[:, :], ALU.add).then_inc(self.xr_ready, 1)


def project(nc, keep, a, raw, hi, lo, scratch, outs):
    COLS = COLS_IN
    RING = 4
    assert COLS * NG == DIN and COLS <= HALF and (2 * NT) % RING == 0
    with ExitStack() as ctx:
        s = Space(nc, ctx, "prj")
        whi = [s.sb(f"whi{j}", [P, KD, COLS], F32R) for j in range(2)]
        wlo = [s.sb(f"wlo{j}", [P, KD, COLS], F32R) for j in range(2)]
        stage = s.sb("stage", [P, RING, COLS])
        acc = s.ps("acc", [P, RING, HALF])
        w_in = [s.sem(f"w_in{j}") for j in range(2)]
        whi_ready, wlo_ready, acc_ready = s.sem("whi_ready"), s.sem("wlo_ready"), s.sem("acc_ready")
        first_lo_ready = s.sem("first_lo_ready")
        staged = [s.sem("staged_dve"), s.sem("staged_act")]
        stored = [s.sem(f"stored{b}") for b in range(RING)]
        prep = HeadsPrep(s, keep, a, scratch, outs)
        PAIRS = NG // 2
        HALF_STORES = 16 * (PAIRS // 2) * 2 * NT // RING
        PER_PAIR = NT // (PAIRS // 2)
        assert PAIRS == 4 and NG // 2 * COLS <= C_SQ and 2 * NT == 4 * PER_PAIR

        with nc.Block() as block:

            @block.sync
            def _(sp):

                prep.sp_constants(sp)

                def body(i, first, last, heads):
                    for j in range(2):
                        g = 2 * i + j
                        if not last:
                            if first and j == 0:
                                sp.wait_ge(first_lo_ready, 1)
                            else:
                                sp.wait_ge(wlo_ready, g)
                            load_group(sp, a, raw, g + 2, j).then_inc(w_in[j], 16)
                        for t in range(NT):
                            n = NT * j + t
                            sp.wait_ge(staged[n % 2], NT * i + n // 2 + 1)
                            sp.dma_start(scratch["proj"][t * P:(t + 1) * P, group(g)],
                                         stage[:, n % RING]).then_inc(stored[n % RING], 16)
                            if heads and n % 4 == 3:
                                m = PER_PAIR * (i - PAIRS // 2) + n // 4
                                prep.sp_store(sp, m)
                                if m + 2 < NT:
                                    prep.sp_load(sp, m + 2)
                body(0, True, False, False)
                for i in range(1, PAIRS // 2):
                    body(i, False, False, False)
                for b in range(RING):
                    sp.wait_ge(stored[b], HALF_STORES)
                for t in range(2):
                    prep.sp_load(sp, t)
                body(PAIRS // 2, False, False, True)
                body(PAIRS - 1, False, True, True)
                for b in range(RING):
                    sp.wait_ge(stored[b], 16 * NG * NT // RING)
                for j in range(2):
                    sp.wait_ge(prep.xr_out[j], 16 * NT // 2)

            def evacuate(eng, copy, parity, i, first, heads):
                for n in range(parity, 2 * NT, 2):
                    eng.wait_ge(acc_ready, 2 * NT * i + n + 1)
                    if not (first and n < RING):
                        eng.wait_ge(stored[n % RING], 16 * (2 * NT // RING * i + n // RING))
                    copy(stage[:, n % RING], acc[:, n % RING, 0:COLS]).then_inc(staged[parity], 1)
                    if heads:
                        t = PER_PAIR * (i - PAIRS // 2) + n // 4
                        if n % 4 == 0:
                            prep.dve_sum(eng, t)
                        else:
                            prep.dve_rotate(eng, t)

            @block.scalar
            def _(act):
                def split(i, j, first):
                    g = 2 * i + j
                    if not first:
                        act.wait_ge(w_in[j], 16 * i)
                        act.wait_ge(acc_ready, NT * (g - 1))
                    act.activation(whi[j][:, :, :], raw[:, j], ACT.Copy).then_inc(whi_ready, 1)

                def copy(out, in_):
                    return act.activation(out, in_, ACT.Copy)
                for j in range(2):
                    split(0, j, True)

                def body(i, first, last):
                    for j in range(2):
                        for n in range(NT * j + (1 - (NT * j) % 2), NT * (j + 1), 2):
                            act.wait_ge(acc_ready, 2 * NT * i + n + 1)
                            if not (first and n < RING):
                                act.wait_ge(stored[n % RING], 16 * (2 * NT // RING * i + n // RING))
                            copy(stage[:, n % RING], acc[:, n % RING, 0:COLS]).then_inc(staged[1], 1)
                        if not last:
                            split(i + 1, j, False)
                body(0, True, False)
                with act.Fori(1, NG // 2 - 1) as i:
                    body(i, False, False)
                body(NG // 2 - 1, False, True)

            @block.gpsimd
            def _(pool):
                def split(g, j):
                    pool.wait_ge(whi_ready, g + 1)
                    pool.tensor_tensor(wlo[j][:, :, :], raw[:, j], hi_view(whi[j]), ALU.subtract).then_inc(wlo_ready, 1)
                split(1, 1)
                with pool.Fori(1, PAIRS - 1) as i:
                    for j in range(2):
                        split(2 * i + j, j)
                for t in range(NT):
                    if t == PER_PAIR // 2:
                        split(NG - 2, 0)
                    if t == PER_PAIR:
                        split(NG - 1, 1)
                    prep.pool(pool, t)

            @block.vector
            def _(dve):
                dve.wait_ge(whi_ready, 1)
                dve.tensor_tensor(wlo[0][:, :, :], raw[:, 0], hi_view(whi[0]), ALU.subtract).then_inc(first_lo_ready, 1)
                evacuate(dve, dve.tensor_copy, 0, 0, True, False)
                for i in range(1, PAIRS):
                    evacuate(dve, dve.tensor_copy, 0, i, False, i >= PAIRS // 2)

            @block.tensor
            def _(pe):
                def body(i, first):
                    for j in range(2):
                        if first and j == 0:
                            pe.wait_ge(first_lo_ready, 1)
                        else:
                            pe.wait_ge(wlo_ready, 2 * i + j)
                        for t in range(NT):
                            n = NT * j + t
                            if not (first and n < RING):
                                pe.wait_ge(staged[n % 2], NT * i + n // 2 - 1)
                            for k in range(KD):
                                x_hi, x_lo = (x[:, k, t * P:(t + 1) * P] for x in (hi, lo))
                                pe.matmul(acc[:, n % RING, 0:COLS], x_hi, whi[j][:, k, :], start=(k == 0), stop=False)
                                pe.matmul(acc[:, n % RING, 0:COLS], x_hi, wlo[j][:, k, :], start=False, stop=False)
                                mm = pe.matmul(acc[:, n % RING, 0:COLS], x_lo, whi[j][:, k, :], start=False, stop=(k == KD - 1))
                            mm.then_inc(acc_ready, 1)
                body(0, True)
                with pe.Fori(1, NG // 2) as i:
                    body(i, False)


def gla(nc, keep, a, scratch, outs):
    with ExitStack() as ctx:
        s = Space(nc, ctx, "gla")
        qkv = s.sb("qkv", [P, NT, 3 * GW])
        glr = s.sb("glr", [P, NT, 2 * RANK])
        lrT = s.sb("lrT", [2 * RANK + 1, T])
        wgk = s.sb("wgk", [2 * RANK + 1, 2, GW])
        ln = s.sb("ln", [P, 2, NT, GW])
        g = s.sb("g", [P, 2, GW])
        bc = s.sb("bc", [P, 2, GW])
        up = s.sb("up", [P, 2, GW])
        down = s.sb("down", [P, 2, GW])
        qe = s.sb("qe", [P, 2, GW])
        ke = s.sb("ke", [P, 2, GW])
        qT = s.sb("qT", [P, 2, H // 2, P])
        kT = s.sb("kT", [P, 2, H // 2, P])
        at = s.sb("at", [P, 2, H, P])
        dec = s.sb("dec", [P, 2, H // 2, 4])
        state = [s.sb("state_p", [P, 2, H // 2, DH]), s.sb("state_s", [P, 2, H // 2, DH])]
        mid = s.sb("mid", [P, 2, H // 2, 2, DH])
        kept = s.sb("kept", [P, 2, H // 2, DH])
        new = s.sb("new", [P, 2, H // 2, DH])
        o = s.sb("o", [P, 2, NT, GW])
        ps = [s.ps(f"ps{d}", [P, 4, HALF]) for d in range(2)]
        (min_ready, logit_ready, mag_ready, ex_ready, ln_ready, g_ready, bc_ready, clamp_ready, up_ready, down_ready,
         qe_ready, ke_ready, tr_ready, qT_ready, kT_ready, score_ready, at_ready, dec_ready, mid_ready, o_ready,
         o_kept, ds_ready, kept_ready, new_ready, state_ready) = (s.sem(n) for n in (
             "min_ready", "logit_ready", "mag_ready", "ex_ready", "ln_ready", "g_ready", "bc_ready", "clamp_ready",
             "up_ready", "down_ready", "qe_ready", "ke_ready", "tr_ready", "qT_ready", "kT_ready", "score_ready",
             "at_ready", "dec_ready", "mid_ready", "o_ready", "o_kept", "ds_ready", "kept_ready", "new_ready",
             "state_ready"))
        loaded, glr_in, zeroed, weights_in, lrT_ready, lrT_kept, stored = (s.sem(n) for n in (
            "loaded", "glr_in", "zeroed", "weights_in", "lrT_ready", "lrT_kept", "stored"))

        def steps(eng, body):
            body(0, 0, True, False)
            body(1, 0, False, False)
            with eng.Fori(2, NT - 1) as i:
                body(i, 1, False, False)
            body(NT - 1, 1, False, True)

        def tiles_of(eng, i, part):
            if part == 0:
                return i, NTP - 1 - i
            return eng.snap(i + 0), eng.snap(i * -1 + (NTP + NT - 1))

        gates = [(i, d, (i, NTP - 1 - i)[d] if i < NTP else (i, NTP + NT - 1 - i)[d]) for i in range(NT) for d in range(2)]

        def logits(n):
            return ps[n % 2][:, n // 2 % 4]

        with nc.Block() as block:

            @block.sync
            def _(sp):
                sp.dma_start(glr[:, :, :], scratch["proj"][:, C_LR:C_SQ].rearrange("(t p) n -> p t n", p=P)).then_inc(glr_in, 16)
                sp.wait_ge(zeroed, 1)
                for d, (w, b) in enumerate((("w_gk_fwd", "b_gk_fwd"), ("w_gk_bwd", "b_gk_bwd"))):
                    sp.dma_start(wgk[d * RANK:(d + 1) * RANK, d, :], a[w][0]).then_inc(weights_in, 16)
                    sp.dma_start(wgk[2 * RANK:2 * RANK + 1, d, :], a[b]).then_inc(weights_in, 16)
                for half in range(2):
                    t0 = half * NT // 2
                    sp.dma_start(qkv[:, t0:t0 + NT // 2, :],
                                 scratch["proj"][t0 * P:(t0 + NT // 2) * P, 0:3 * GW].rearrange("(t p) n -> p t n", p=P)
                                 ).then_inc(loaded, 16)
                for d, name in enumerate(("state_gla_fwd", "state_gla_bwd")):
                    for half in range(2):
                        sp.dma_start(state[1][half * DH:(half + 1) * DH, d],
                                     a[name][0, 0].rearrange("(b c) k v -> c k b v", c=2)[half]).then_inc(loaded, 16)

                def store(i, part):
                    tile = tiles_of(sp, i, part)
                    for d in range(2):
                        sp.wait_ge(o_kept, 2 * i + d + 1)
                        sp.dma_start(scratch["o"][d, tile_rows(tile[d]), :],
                                     o[:, d, bass.ds(tile[d], 1)].rearrange("p t n -> p (t n)")).then_inc(stored, 16)
                for i in range(NTP):
                    store(i, 0)
                sp.wait_ge(state_ready, 2 * NTP)
                for d in range(2):
                    for half in range(2):
                        sp.dma_start(outs[4 + d][0, 0].rearrange("(b c) k v -> c k b v", c=2)[half],
                                     state[0][half * DH:(half + 1) * DH, d]).then_inc(stored, 16)
                with sp.Fori(NTP, NT) as i:
                    store(i, 1)
                sp.wait_ge(stored, 16 * (4 + 2 * NT))

            @block.gpsimd
            def _(pool):
                pool.wait_ge(min_ready, 2 * NT)
                pool.wait_ge(loaded, 6 * 16)

                def gate(i, d, tile, first):
                    u = 2 * i + d
                    pool.wait_ge(ln_ready, u + 1)
                    if not first:
                        pool.wait_ge(bc_ready, u - 1)
                    at = bass.ds(tile, 1)
                    pool.tensor_tensor(g[:, d], o[:, d, at].rearrange("p t n -> p (t n)"), ln[:, d, at].rearrange("p t n -> p (t n)"),
                                       ALU.subtract).then_inc(g_ready, 1)

                def body(i, part, first, following):
                    tile = tiles_of(pool, i, part)
                    for d in range(2):
                        u = 2 * i + d
                        pool.wait_ge(down_ready, u + 1)
                        if not first:
                            pool.wait_ge(ds_ready, u - 1)
                        pool.tensor_tensor(ke[:, d], down[:, d], qkv[:, bass.ds(tile[d], 1), GW:2 * GW].rearrange("p t n -> p (t n)"),
                                           ALU.mult).then_inc(ke_ready, 1)
                        if following:
                            gate(i + 1, d, following[d], False)
                for d in range(2):
                    gate(0, d, tiles_of(pool, 0, 0)[d], True)
                body(0, 0, True, tiles_of(pool, 1, 0))
                body(1, 0, False, (NTP, NT - 1))
                with pool.Fori(NTP, NT - 1) as i:
                    body(i, 1, False, tiles_of(pool, i + 1, 1))
                body(NT - 1, 1, False, None)

            @block.scalar
            def _(act):
                for n, (i, d, t) in enumerate(gates):
                    act.wait_ge(logit_ready, n + 1)
                    act.activation(ln[:, d, t], logits(n), ACT.Abs).then_inc(mag_ready, 1)
                    act.wait_ge(mag_ready, n + 1)
                    act.activation(ln[:, d, t], ln[:, d, t], ACT.Exp, scale=-1.0).then_inc(ex_ready, 1)
                for n, (i, d, t) in enumerate(gates):
                    act.wait_ge(ex_ready, n + 1)
                    act.activation(ln[:, d, t], ln[:, d, t], ACT.Ln, bias=1.0).then_inc(ln_ready, 1)

                def body(i, part, first, last):
                    for d in range(2):
                        u = 2 * i + d
                        act.wait_ge(clamp_ready, u + 1)
                        if not first:
                            act.wait_ge(qe_ready, u - 1)
                            act.wait_ge(ke_ready, u - 1)
                        act.activation(up[:, d], bc[:, d], ACT.Exp).then_inc(up_ready, 1)
                        act.activation(down[:, d], bc[:, d], ACT.Exp, scale=-1.0).then_inc(down_ready, 1)
                        if not first:
                            act.wait_ge(state_ready, u - 1)
                        act.activation(dec[:, d], ps[d][:, 1, 0:2 * H].rearrange("p (b c) -> p b c", c=4), ACT.Exp).then_inc(dec_ready, 1)
                    for d in range(2):
                        u = 2 * i + d
                        act.wait_ge(tr_ready, u + 1)
                        act.activation(qT[:, d], ps[d][:, 1].rearrange("p (b c) -> p b c", c=P), ACT.Copy).then_inc(qT_ready, 1)
                steps(act, body)

            @block.vector
            def _(dve):
                dve.memset(wgk[:, :, :], 0.0).then_inc(zeroed, 1)
                dve.memset(lrT[2 * RANK:2 * RANK + 1, :], 1.0).then_inc(zeroed, 1)
                dve.memset(state[0][:, :, :, :], 0.0).then_inc(zeroed, 1)
                dve.memset(mid[:, :, :, :, :], 0.0).then_inc(zeroed, 1)
                for n in range(3):
                    w = min(4, NT - 4 * n) * P
                    dve.wait_ge(lrT_ready, 1)
                    dve.tensor_copy(lrT[0:2 * RANK, 4 * n * P:4 * n * P + w], ps[0][0:2 * RANK, n, 0:w]).then_inc(lrT_kept, 1)
                for n, (i, d, t) in enumerate(gates):
                    dve.wait_ge(mag_ready, n + 1)
                    dve.tensor_scalar(o[:, d, t], logits(n), 0.0, None, ALU.min).then_inc(min_ready, 1)
                dve.wait_ge(loaded, 6 * 16)
                dve.wait_ge(zeroed, 4)

                def clamp(i, d, first):
                    u = 2 * i + d
                    dve.wait_ge(bc_ready, u + 1)
                    if not first:
                        dve.wait_ge(down_ready, u - 1)
                    dve.tensor_scalar(bc[:, d], ps[d][:, 0], CLAMP, -CLAMP, ALU.min, ALU.max).then_inc(clamp_ready, 1)

                def body(i, part, first, last):
                    tile = tiles_of(dve, i, part)
                    for d in range(2):
                        u = 2 * i + d
                        dve.wait_ge(up_ready, u + 1)
                        if not first:
                            dve.wait_ge(tr_ready, u - 1)
                        dve.scalar_tensor_tensor(qe[:, d], up[:, d], DH ** -0.5,
                                                 qkv[:, bass.ds(tile[d], 1), 0:GW].rearrange("p t n -> p (t n)"),
                                                 ALU.mult, ALU.mult).then_inc(qe_ready, 1)
                        dve.wait_ge(dec_ready, u + 1)
                        if not first:
                            dve.wait_ge(state_ready, u - 1)
                            dve.wait_ge(o_ready, u - 1)
                        for half in range(2):
                            rows = slice(half * DH, (half + 1) * DH)
                            dve.tensor_tensor(mid[rows, d, :, half], state[part][rows, d],
                                              dec[rows, d, :, 0:1].broadcast_to([DH, H // 2, DH]), ALU.mult).then_inc(mid_ready, 1)
                    for d in range(2):
                        u = 2 * i + d
                        dve.wait_ge(tr_ready, u + 1)
                        dve.tensor_copy(kT[:, d], ps[d][:, 2].rearrange("p (b c) -> p b c", c=P)).then_inc(kT_ready, 1)
                    for d in range(2):
                        u = 2 * i + d
                        dve.tensor_tensor(kept[:, d], state[part][:, d], dec[:, d, :, 1:2].broadcast_to([P, H // 2, DH]),
                                          ALU.mult).then_inc(kept_ready, 1)
                        dve.wait_ge(ds_ready, u + 1)
                        for half in range(2):
                            rows = slice(half * DH, (half + 1) * DH)
                            upd = ps[d][rows, 0].rearrange("p (b c) -> p b c", c=P)[:, :, half * DH:(half + 1) * DH]
                            dve.tensor_tensor(new[rows, d], upd, dec[rows, d, :, 2:3].broadcast_to([DH, H // 2, DH]),
                                              ALU.mult).then_inc(new_ready, 1)
                        dve.wait_ge(new_ready, 2 * u + 2)
                        dve.wait_ge(kept_ready, u + 1)
                        dve.wait_ge(mid_ready, 2 * u + 2)
                        dve.tensor_tensor(state[part][:, d], kept[:, d], new[:, d], ALU.add).then_inc(state_ready, 1)
                        dve.wait_ge(score_ready, u + 1)
                        if not first:
                            dve.wait_ge(o_ready, u - 1)
                        dve.tensor_tensor(at[:, d], ps[d][:, 1:3].rearrange("p b (c n) -> p (b c) n", n=P),
                                          keep["causal"][d].unsqueeze(1).broadcast_to([P, H, P]), ALU.mult).then_inc(at_ready, 1)
                    for d in range(2):
                        u = 2 * i + d
                        dve.wait_ge(o_ready, u + 1)
                        dve.tensor_copy(o[:, d, bass.ds(tile[d], 1), :].rearrange("p t n -> p (t n)"),
                                        ps[d][:, 3]).then_inc(o_kept, 1)
                        if not last:
                            clamp(i + 1, d, False)
                for d in range(2):
                    clamp(0, d, True)
                steps(dve, body)

            @block.tensor
            def _(pe):
                pe.wait_ge(glr_in, 16)
                for t in range(NT):
                    tr = pe.transpose(ps[0][0:2 * RANK, t // 4, (t % 4) * P:(t % 4 + 1) * P], glr[:, t, :], keep["ident"])
                tr.then_inc(lrT_ready, 1)
                pe.wait_ge(weights_in, 4 * 16)
                pe.wait_ge(lrT_kept, 3)

                for n, (i, d, t) in enumerate(gates):
                    if n >= 8:
                        pe.wait_ge(min_ready, n - 7)
                    pe.matmul(logits(n), lrT[:, t * P:(t + 1) * P], wgk[:, d, :], start=True, stop=True).then_inc(logit_ready, 1)
                pe.wait_ge(min_ready, 2 * NT)
                pe.wait_ge(loaded, 6 * 16)

                def decays(i, d, first):
                    u = 2 * i + d
                    pe.wait_ge(g_ready, u + 1)
                    if not first:
                        pe.wait_ge(state_ready, u - 1)
                        pe.wait_ge(at_ready, u - 1)
                    pe.matmul(ps[d][:, 0], keep["cum"][d], g[:, d], start=True, stop=True)
                    for b in range(H // 2):
                        mm = pe.matmul(ps[d][:, 1, 4 * b:4 * b + 4], g[:, d, b * P:(b + 1) * P], keep["vec"][d],
                                       start=True, stop=True)
                    mm.then_inc(bc_ready, 1)

                def body(i, part, first, last):
                    tile = tiles_of(pe, i, part)
                    for d in range(2):
                        u = 2 * i + d
                        pe.wait_ge(qe_ready, u + 1)
                        pe.wait_ge(ke_ready, u + 1)
                        pe.wait_ge(dec_ready, u + 1)
                        if not first:
                            pe.wait_ge(at_ready, u - 1)
                        for bank, x in ((1, qe), (2, ke)):
                            for b in range(H // 2):
                                tr = pe.transpose(ps[d][:, bank, b * P:(b + 1) * P], x[:, d, b * P:(b + 1) * P], keep["ident"])
                        tr.then_inc(tr_ready, 1)
                        for b in range(H // 2):
                            mm = pe.matmul(ps[d][:, 0, b * P:(b + 1) * P], ke[:, d, b * P:(b + 1) * P],
                                           qkv[:, bass.ds(tile[d], 1), 2 * GW + b * P:2 * GW + (b + 1) * P].rearrange("p t n -> p (t n)"),
                                           start=True, stop=True)
                        mm.then_inc(ds_ready, 1)
                    for d in range(2):
                        u = 2 * i + d
                        pe.wait_ge(qT_ready, u + 1)
                        pe.wait_ge(kT_ready, u + 1)
                        for h in range(H):
                            rows = slice((h % 2) * DH, (h % 2 + 1) * DH)
                            mm = pe.matmul(ps[d][:, 1 + h % 2, (h // 2) * P:(h // 2 + 1) * P], kT[rows, d, h // 2], qT[rows, d, h // 2],
                                           start=True, stop=True)
                        mm.then_inc(score_ready, 1)
                    for d in range(2):
                        u = 2 * i + d
                        pe.wait_ge(at_ready, u + 1)
                        pe.wait_ge(mid_ready, 2 * u + 2)
                        if not first:
                            pe.wait_ge(o_kept, u - 1)
                        for b in range(H // 2):
                            pe.matmul(ps[d][:, 3, b * P:(b + 1) * P], qT[:, d, b], mid[:, d, b].rearrange("p c n -> p (c n)"),
                                      start=True, stop=False)
                            for half in range(2):
                                c = b * P + half * DH
                                mm = pe.matmul(ps[d][:, 3, c:c + DH], at[:, d, half * (H // 2) + b],
                                               qkv[:, bass.ds(tile[d], 1), 2 * GW + c:2 * GW + c + DH].rearrange("p t n -> p (t n)"),
                                               start=False, stop=(half == 1))
                        mm.then_inc(o_ready, 1)
                        if not last:
                            decays(i + 1, d, False)
                for d in range(2):
                    decays(0, d, True)
                steps(pe, body)


class GlaOutput:
    def __init__(self, s, keep, a, scratch, out, stored):
        self.out, self.stored = out, stored
        self.keep, self.a, self.scratch = keep, a, scratch
        self.of, self.ob, self.gg, self.o, self.sq, self.tanh, self.factor, self.si, self.on, self.og = (
            s.sb("glo_" + n, [P, 2, GW]) for n in ("of", "ob", "gg", "o", "sq", "tanh", "factor", "si", "on", "og"))
        self.norm = s.sb("glo_norm", [P, DH])
        self.root = s.sb("glo_root", [P, DH])
        self.one = s.sb("glo_one", [P, GW])
        self.gain = s.sb("glo_gain", [P, DH])
        self.ssq, self.ms, self.rstd = (s.sb("glo_" + n, [P, 2, H]) for n in ("ssq", "ms", "rstd"))
        (self.o_ready, self.sq_ready, self.ssq_ready, self.ms_ready, self.rstd_ready, self.tanh_ready, self.factor_ready,
         self.si_ready, self.on_ready, self.og_ready, self.out_ready, self.norm_in, self.root_ready,
         self.gain_ready) = (s.sem("glo_" + n) for n in (
             "o_ready", "sq_ready", "ssq_ready", "ms_ready", "rstd_ready", "tanh_ready", "factor_ready", "si_ready",
             "on_ready", "og_ready", "out_ready", "norm_in", "root_ready", "gain_ready"))
        self.loaded = [s.sem(f"glo_loaded{j}") for j in range(2)]

    def sp_gain(self, sp):
        sp.dma_start(self.norm[:, :], self.a["gla_norm"].broadcast_to([P, DH])).then_inc(self.norm_in, 16)

    def sp_load(self, sp, t, j):
        sp.dma_start(self.of[:, j], self.scratch["o"][0, tile_rows(t), :]).then_inc(self.loaded[j], 16)
        sp.dma_start(self.ob[:, j], self.scratch["o"][1, tile_rows(t), :]).then_inc(self.loaded[j], 16)
        sp.dma_start(self.gg[:, j], self.scratch["proj"][tile_rows(t), C_GG:C_LR]).then_inc(self.loaded[j], 16)

    def pool_gain(self, pool):
        pool.memset(self.root[:, :], DH ** 0.5 / 2).then_inc(self.root_ready, 1)
        pool.memset(self.one[:, :], 1.0).then_inc(self.root_ready, 1)
        pool.wait_ge(self.root_ready, 2)
        pool.wait_ge(self.norm_in, 16)
        pool.tensor_tensor(self.gain[:, :], self.norm[:, :], self.root[:, :], ALU.mult).then_inc(self.gain_ready, 1)
        pool.wait_ge(self.gain_ready, 1)

    def pool(self, pool, i, j, first):
        t = 2 * i + j

        def heads(x):
            return x.rearrange("p (h d) -> p h d", d=DH)
        pool.wait_ge(self.loaded[j], 48 * i + 48)
        pool.tensor_tensor(self.o[:, j], self.of[:, j], self.ob[:, j], ALU.add).then_inc(self.o_ready, 1)
        pool.wait_ge(self.o_ready, t + 1)
        pool.tensor_tensor(self.sq[:, j], self.o[:, j], self.o[:, j], ALU.mult).then_inc(self.sq_ready, 1)
        pool.wait_ge(self.ssq_ready, t + 1)
        pool.tensor_tensor(self.ms[:, j], self.ssq[:, j], self.keep["eps_h"][:, 0:H], ALU.add).then_inc(self.ms_ready, 1)
        pool.wait_ge(self.ms_ready, t + 1)
        pool.tensor_tensor(self.rstd[:, j], self.ms[:, j], self.keep["minus_half"][:, 0:H], ALU.pow).then_inc(self.rstd_ready, 1)
        pool.wait_ge(self.rstd_ready, t + 1)
        pool.tensor_tensor(heads(self.on[:, j]), heads(self.o[:, j]), self.rstd[:, j].unsqueeze(2).broadcast_to([P, H, DH]),
                           ALU.mult).then_inc(self.on_ready, 1)
        pool.wait_ge(self.on_ready, t + 1)
        pool.tensor_tensor(heads(self.og[:, j]), heads(self.on[:, j]), self.gain[:, :].unsqueeze(1).broadcast_to([P, H, DH]),
                           ALU.mult).then_inc(self.og_ready, 1)
        pool.wait_ge(self.tanh_ready, t + 1)
        pool.tensor_tensor(self.factor[:, j], self.tanh[:, j], self.one[:, :], ALU.add).then_inc(self.factor_ready, 1)
        pool.wait_ge(self.factor_ready, t + 1)
        pool.tensor_tensor(self.si[:, j], self.gg[:, j], self.factor[:, j], ALU.mult).then_inc(self.si_ready, 1)
        pool.wait_ge(self.si_ready, t + 1)
        pool.wait_ge(self.og_ready, t + 1)
        if not first:
            pool.wait_ge(self.stored[j], 16 * i)
        pool.tensor_tensor(self.out[:, j], self.og[:, j], self.si[:, j], ALU.mult).then_inc(self.out_ready, 1)

    def act(self, act, i, j, first):
        act.wait_ge(self.loaded[j], 48 * i + 48)
        if not first:
            act.wait_ge(self.factor_ready, 2 * i + j - 1)
        act.activation(self.tanh[:, j], self.gg[:, j], ACT.Tanh, scale=0.5).then_inc(self.tanh_ready, 1)

    def dve(self, dve, i, j, first):
        t = 2 * i + j
        dve.wait_ge(self.sq_ready, t + 1)
        if not first:
            dve.wait_ge(self.ms_ready, t - 1)
        dve.tensor_reduce(self.ssq[:, j], self.sq[:, j].rearrange("p (h d) -> p h d", d=DH), AX_X, ALU.add).then_inc(self.ssq_ready, 1)


class OutputWeights:
    WC = D // (TS // P)

    def __init__(self, s, a, whi, wlo):
        self.whi, self.wlo = whi, wlo
        self.raw = s.sb("wo_raw", [P, 2, KD, self.WC])
        self.w_in = [s.sem(f"wo_in{j}") for j in range(2)]
        self.whi_ready, self.wlo_ready = s.sem("wo_hi_ready"), s.sem("wo_lo_ready")
        self.view = a["w_o"][0].rearrange("(k p) n -> p k n", p=P)

    def columns(self, n):
        return bass.ds(n * self.WC, self.WC)

    def sp_load(self, sp, n, j):
        sp.dma_start(self.raw[:, j], self.view[:, :, self.columns(n)]).then_inc(self.w_in[j], 16)

    def act(self, act, i, j):
        act.wait_ge(self.w_in[j], 16 * i + 16)
        act.activation(self.whi[:, :, self.columns(2 * i + j)], self.raw[:, j], ACT.Copy).then_inc(self.whi_ready, 1)

    def pool(self, pool, i, j):
        pool.wait_ge(self.whi_ready, 2 * i + j + 1)
        at = self.columns(2 * i + j)
        pool.tensor_tensor(self.wlo[:, :, at], self.raw[:, j], hi_view(self.whi)[:, :, at], ALU.subtract).then_inc(self.wlo_ready, 1)


def attention(nc, keep, a, scratch, whi, wlo):
    NL, NC = 3, PAST // P
    PAD = NTP
    SLOTS = NT + 2
    with ExitStack() as ctx:
        s = Space(nc, ctx, "att")
        kT = s.sb("kT", [P, KV, SLOTS * P], F32R)
        kcT = s.sb("kcT", [P, KV, PAST], F32R)
        v = s.sb("v", [P, SLOTS, KV * DH])
        vc = s.sb("vc", [P, NC, KV, DH])
        sink = s.sb("sink", [P, H])
        nsink = s.sb("nsink", [P, H])
        win = s.sb("win", [P, 2 * TS], BF16)
        identb = s.sb("identb", [P, P], BF16)

        with ExitStack() as inner:
            s1 = Space(nc, inner, "keys")
            winf = s1.sb("winf", [P, 2 * TS])
            k = s1.sb("k", [P, NT, KV, 2, DH])
            kc = s1.sb("kc", [P, NC, KV, 2, DH])
            PER = HALF // P
            NK, NKC = NT * KV // PER, NC * KV // PER
            khi = s1.sb("khi", [P, NK + NKC, HALF], F32R)
            tr = s1.ps("tr", [P, NK + NKC, HALF])
            k_in, v_in, tables_in, padded, tables, tr_ready, hi_ready, lo_ready = (s1.sem(n) for n in (
                "k_in", "v_in", "tables_in", "padded", "tables", "tr_ready", "hi_ready", "lo_ready"))
            assert NK * PER == NT * KV and NKC == KV and NTP * KV == PER

            def bank(n, rows):
                if n >= NK:
                    return kcT[rows, n - NK], tr[rows, n], khi[rows, n]
                slot = 2 * n + (1 if n else 0)
                view = "p (t k n) -> p k t n"
                return (kT[rows, :, slot * P:(slot + 2) * P].rearrange("p k (t n) -> p k t n", n=P),
                        tr[rows, n].rearrange(view, k=KV, n=P), khi[rows, n].rearrange(view, k=KV, n=P))

            with nc.Block() as block:

                @block.sync
                def _(sp):
                    for c in range(2):
                        for kv in range(KV):
                            sp.dma_start(k[:, :, kv, c], scratch["qk"][:, GW + kv * DH:GW + (kv + 1) * DH].rearrange("(t p) d -> p t d", p=P)
                                         ).then_inc(k_in, 16)
                            sp.dma_start(kc[:, :, kv, c], a["cache_k"][0, 0, kv].rearrange("(b p) d -> p b d", p=P)).then_inc(k_in, 16)
                    sp.dma_start(winf[:, :], a["window"]).then_inc(tables_in, 16)
                    sp.dma_start(sink[:, :], a["sink"].broadcast_to([P, H])).then_inc(tables_in, 16)
                    for kv in range(KV):
                        sp.dma_start(vc[:, :, kv, :], a["cache_v"][0, 0, kv].rearrange("(b p) d -> p b d", p=P)).then_inc(v_in, 16)
                    pv = scratch["proj"][:, DIN - KV * DH:DIN].rearrange("(t p) d -> p t d", p=P)
                    sp.dma_start(v[:, 0:NTP], pv[:, 0:NTP]).then_inc(v_in, 16)
                    sp.dma_start(v[:, NTP + 1:SLOTS - 1], pv[:, NTP:NT]).then_inc(v_in, 16)
                    sp.wait_ge(v_in, 16 * (KV + 2))

                @block.vector
                def _(dve):
                    for slot in (PAD, SLOTS - 1):
                        dve.tensor_scalar(kT[:, :, slot * P:(slot + 1) * P], keep["ident"].unsqueeze(1).broadcast_to([P, KV, P]),
                                          0.0, None, ALU.mult).then_inc(padded, 1)
                        dve.memset(v[:, slot], 0.0).then_inc(padded, 1)
                    dve.tensor_copy(identb[:, :], keep["ident"]).then_inc(tables, 1)
                    for n in range(NK + NKC):
                        dve.wait_ge(hi_ready, 2 * n + 2)
                        low, x, high = bank(n, slice(DH, P))
                        dve.tensor_tensor(low, x, high.bitcast(F32), ALU.subtract).then_inc(lo_ready, 1)
                    dve.wait_ge(tables_in, 32)
                    dve.tensor_scalar(nsink[:, :], sink[:, :], -1.0, None, ALU.mult).then_inc(tables, 1)
                    dve.tensor_copy(win[:, :], winf[:, :]).then_inc(tables, 1)

                @block.scalar
                def _(act):
                    for n in range(NK + NKC):
                        act.wait_ge(tr_ready, n + 1)
                        high, x, _ = bank(n, slice(0, DH))
                        act.activation(high, x, ACT.Copy).then_inc(hi_ready, 1)
                        _, x, beside = bank(n, slice(DH, P))
                        act.activation(beside, x, ACT.Copy).then_inc(hi_ready, 1)

                @block.tensor
                def _(pe):
                    pe.wait_ge(k_in, 16 * 4 * KV)
                    for n in range(NK + NKC):
                        for m in range(PER):
                            b = n * PER + m
                            src = k[:, b // KV, b % KV] if n < NK else kc[:, m, n - NK]
                            mm = pe.transpose(tr[:, n, m * P:(m + 1) * P], src.rearrange("p c d -> p (c d)"), keep["ident"])
                        mm.then_inc(tr_ready, 1)

        with ExitStack() as inner:
            s2 = Space(nc, inner, "soft")
            qh, ql = ([s2.sb(f"{n}{j}", [P, H, P], F32R) for j in range(2)] for n in ("qh", "ql"))
            xq = s2.sb("xq", [P, 2, H, 2, DH])
            prob = s2.sb("prob", [P, 2, (NC + NL) * P])
            pT = s2.sb("pT", [P, 2, 8, P])
            top = s2.sb("top", [P, 2, H])
            bias = s2.sb("bias", [P, 2, H])
            total = s2.sb("total", [P, 2, H])
            sb_in, sb_out, den, inv = (s2.sb(n, [P, 2, H]) for n in ("sb_in", "sb_out", "den", "inv"))
            mix = s2.sb("mix", [P, 2, 2 * GW])
            score = s2.ps("score", [P, 2, 2 * HALF])
            pTp = s2.ps("pTp", [P, 8, P])
            op = s2.ps("op", [P, 2, HALF])
            (qt_ready, qh_ready, ql_ready, s_ready, top_ready, bias_ready, p_ready, pTp_ready, pTa_ready, pTd_ready, pv_ready, sin_ready, sout_ready,
             den_ready, inv_ready, o_ready) = (s2.sem(n) for n in (
                 "qt_ready", "qh_ready", "ql_ready", "s_ready", "top_ready", "bias_ready", "p_ready", "pTp_ready", "pTa_ready", "pTd_ready", "pv_ready",
                 "sin_ready", "sout_ready", "den_ready", "inv_ready", "o_ready"))
            stored = [s2.sem(f"stored{j}") for j in range(2)]
            xq_in = [s2.sem(f"xq_in{j}") for j in range(2)]
            glo = GlaOutput(s2, keep, a, scratch, mix[:, :, 0:GW], stored)
            wo = OutputWeights(s2, a, whi, wlo)
            UNITS = 2 * H

            LAST = NT // 2 - 1
            TURN = (3, 5)
            HQ = H // 2

            def tile_pairs(eng, body):
                body(0, 0, False, False)
                with eng.Fori(0, LAST - 1) as i:
                    body(i + 1, i, True, False)
                body(LAST, LAST - 1, True, True)

            def turn_queries(pe, t, j, r, i, first):
                if r == 0:
                    pe.wait_ge(xq_in[j], 32 * i + 32)
                    if not first:
                        pe.wait_ge(o_ready, t - 1)
                else:
                    pe.wait_ge(ql_ready, 2 * t + 1)
                for m in range(HQ):
                    mm = pe.transpose(op[:, j, m * P:(m + 1) * P], xq[:, j, HQ * r + m].rearrange("p c d -> p (c d)"), keep["ident"])
                mm.then_inc(qt_ready, 1)

            def high_queries(act, t, j, r, first):
                act.wait_ge(qt_ready, 2 * t + r + 1)
                if not first:
                    act.wait_ge(s_ready, H * (t - 1))
                act.activation(qh[j][:, HQ * r:HQ * (r + 1)], op[:, j].rearrange("p (h n) -> p h n", n=P), ACT.Copy).then_inc(qh_ready, 1)

            def low_queries(dve, t, j, r, first):
                dve.wait_ge(qh_ready, 2 * t + r + 1)
                if not first:
                    dve.wait_ge(s_ready, H * (t - 1))
                dve.tensor_tensor(ql[j][:, HQ * r:HQ * (r + 1)], op[:, j].rearrange("p (h n) -> p h n", n=P),
                                  qh[j][:, HQ * r:HQ * (r + 1)].bitcast(F32), ALU.subtract).then_inc(ql_ready, 1)

            def next_step(i, j, h, sample):
                t, _, slot = next_tile(i, j)
                return t, slot, TURN.index(h - 1), not sample and j == 0

            def next_tile(i, j):
                return 2 * i + j + 1, i + j, 1 - j

            def softmax_span(sample):
                return slice(0, (NC + NL) * P) if sample else slice(HALF, HALF + NTP * P)

            def blocks(sample):
                if sample:
                    return [(b * P, b) for b in range(NC + NL)]
                return [(HALF, 0), (HALF + P, NC)]

            def evac_slots(sample, engine):
                if sample:
                    return (slice(0, NC), slice(NC, NC + NL))[engine]
                return (slice(0, 1), slice(NC, NC + 1))[engine]

            with nc.Block() as block:

                @block.sync
                def _(sp):
                    glo.sp_gain(sp)
                    def load_queries(t, j):
                        for c in range(2):
                            sp.dma_start(xq[:, j, :, c], scratch["qk"][tile_rows(t), 0:GW].rearrange("p (h d) -> p h d", d=DH)).then_inc(xq_in[j], 16)
                    for j in range(2):
                        load_queries(j, j)
                    for j in range(2):
                        glo.sp_load(sp, j, j)
                    for j in range(2):
                        wo.sp_load(sp, j, j)

                    def body(i, sample, last):
                        for j in range(2):
                            t = 2 * i + j
                            if not last:
                                sp.wait_ge(qt_ready, 2 * t + 2)
                                load_queries(t + 2, j)
                            sp.wait_ge(glo.out_ready, t + 1)
                            sp.wait_ge(o_ready, t + 1)
                            sp.dma_start(scratch["mix"][tile_rows(t), :], mix[:, j]).then_inc(stored[j], 16)
                            if sample and not last:
                                wo.sp_load(sp, t + 2 - NTP, j)
                            if not last:
                                glo.sp_load(sp, t + 2, j)
                    body(0, False, False)
                    with sp.Fori(1, LAST) as i:
                        body(i, True, False)
                    body(LAST, True, True)
                    for j in range(2):
                        sp.wait_ge(stored[j], 16 * NT // 2)

                @block.gpsimd
                def _(pool):
                    glo.pool_gain(pool)

                    def body(i, si, sample, last):
                        for j in range(2):
                            if sample:
                                wo.pool(pool, si, j)
                                pool.wait_ge(wo.wlo_ready, 2 * si + j + 1)
                            glo.pool(pool, i, j, not sample)
                    tile_pairs(pool, body)

                @block.tensor
                def _(pe):
                    def body(i, si, sample, last):
                        def scores(n):
                            j, h = n // H, n % H
                            kv = h // (H // KV)
                            if h == 0:
                                pe.wait_ge(ql_ready, 2 * (2 * i + j) + 2)
                            if sample or n >= 2:
                                pe.wait_ge(p_ready, UNITS * i + n - 1)
                            if sample:
                                st = 2 * si + j
                                keys = kT[:, kv, bass.ds((PAD + st) * P, NL * P)]
                                loc = score[:, n % 2, HALF:HALF + NL * P]
                                for part, q in enumerate((qh[j], ql[j])):
                                    pe.matmul(score[:, n % 2, 0:PAST], q[:, h], kcT[:, kv], start=(part == 0), stop=(part == 1))
                                    pe.matmul(loc, q[:, h], keys, start=(part == 0), stop=False)
                                pe.matmul(loc[:, 0:P], identb[:, :], win[:, bass.ds(st * P, P)], start=False, stop=False)
                                mm = pe.matmul(loc[:, 2 * P:3 * P], identb[:, :], win[:, bass.ds(TS + st * P, P)], start=False, stop=True)
                            else:
                                for part, q in enumerate((qh[j], ql[j])):
                                    mm = pe.matmul(score[:, n % 2, HALF:HALF + TP], q[:, h], kT[:, kv, 0:TP],
                                                   start=(part == 0), stop=(part == 1))
                            mm.then_inc(s_ready, 1)

                        def turn(n):
                            pe.wait_ge(p_ready, UNITS * i + n + 1)
                            if sample or n >= 1:
                                pe.wait_ge(pTa_ready, UNITS * i + n)
                                pe.wait_ge(pTd_ready, UNITS * i + n)
                            for col, slot in blocks(sample):
                                mm = pe.transpose(pTp[:, slot], prob[:, n % 2, col:col + P] if sample else prob[:, n % 2, col - HALF:col - HALF + P],
                                                  keep["ident"])
                            mm.then_inc(pTp_ready, 1)

                        def values(n):
                            j, h = n // H, n % H
                            kv = h // (H // KV)
                            pe.wait_ge(pTa_ready, UNITS * i + n + 1)
                            pe.wait_ge(pTd_ready, UNITS * i + n + 1)
                            every = blocks(sample)
                            for m, (col, slot) in enumerate(every):
                                if sample and slot < NC:
                                    rhs = vc[:, slot, kv]
                                else:
                                    first = PAD + 2 * si + j if sample else 0
                                    off = slot - NC if sample else m
                                    rhs = v[:, bass.ds(first + off, 1), kv * DH:(kv + 1) * DH].rearrange("p t d -> p (t d)")
                                mm = pe.matmul(op[:, j, h * DH:(h + 1) * DH], pT[:, n % 2, slot], rhs,
                                               start=(m == 0), stop=(m == len(every) - 1))
                            mm.then_inc(pv_ready, 1)

                        scores(0)
                        for n in range(UNITS):
                            if n + 1 < UNITS:
                                scores(n + 1)
                            turn(n)
                            if n:
                                values(n - 1)
                            if n % H in TURN and not (last and n >= H):
                                t, ti, slot = next_tile(i, n // H)
                                turn_queries(pe, t, slot, TURN.index(n % H), ti, not sample and n < H)
                        values(UNITS - 1)
                    for r in range(2):
                        turn_queries(pe, 0, 0, r, 0, True)
                    tile_pairs(pe, body)

                @block.scalar
                def _(act):
                    def body(i, si, sample, last):
                        span = softmax_span(sample)

                        def evac(n):
                            act.wait_ge(pTp_ready, UNITS * i + n + 1)
                            if sample or n >= 2:
                                act.wait_ge(pv_ready, UNITS * i + n - 1)
                            sl = evac_slots(sample, 0)
                            act.activation(pT[:, n % 2, sl], pTp[:, sl], ACT.Copy).then_inc(pTa_ready, 1)

                        def sink_term(j):
                            act.wait_ge(sin_ready, 2 * i + j + 1)
                            act.activation(sb_out[:, j], sb_in[:, j], ACT.Exp).then_inc(sout_ready, 1)

                        for n in range(UNITS):
                            j, h = n // H, n % H
                            act.wait_ge(bias_ready, UNITS * i + n + 1)
                            if sample or n >= 2:
                                act.wait_ge(pTp_ready, UNITS * i + n - 1)
                            if h == 0 and sample:
                                act.wait_ge(den_ready, 2 * i + j - 1)
                            act.activation(prob[:, n % 2, 0:span.stop - span.start], score[:, n % 2, span], ACT.Exp,
                                           bias=bias[:, j, h:h + 1], scale=DH ** -0.5, accum_out=total[:, j, h:h + 1]).then_inc(p_ready, 1)
                            if n:
                                evac(n - 1)
                            if h == 0:
                                glo.act(act, i, j, not sample)
                            if h == 1 and sample:
                                wo.act(act, si, j)
                            if h - 1 in TURN and not (last and j == 1):
                                high_queries(act, *next_step(i, j, h, sample))
                            if n == H + 1:
                                sink_term(0)
                        evac(UNITS - 1)
                        sink_term(1)
                    for r in range(2):
                        high_queries(act, 0, 0, r, True)
                    tile_pairs(act, body)

                @block.vector
                def _(dve):
                    def body(i, si, sample, last):
                        span = softmax_span(sample)

                        def evac(n):
                            dve.wait_ge(pTp_ready, UNITS * i + n + 1)
                            if sample or n >= 2:
                                dve.wait_ge(pv_ready, UNITS * i + n - 1)
                            sl = evac_slots(sample, 1)
                            dve.tensor_copy(pT[:, n % 2, sl], pTp[:, sl]).then_inc(pTd_ready, 1)

                        def sink_in(j):
                            dve.wait_ge(bias_ready, UNITS * i + H * j + H)
                            dve.tensor_tensor(sb_in[:, j], sink[:, :], bias[:, j], ALU.add).then_inc(sin_ready, 1)

                        def finish(j):
                            dve.wait_ge(sout_ready, 2 * i + j + 1)
                            dve.wait_ge(p_ready, UNITS * i + H * j + H)
                            dve.tensor_tensor(den[:, j], sb_out[:, j], total[:, j], ALU.add).then_inc(den_ready, 1)
                            dve.wait_ge(den_ready, 2 * i + j + 1)
                            dve.reciprocal(inv[:, j], den[:, j]).then_inc(inv_ready, 1)
                            dve.wait_ge(inv_ready, 2 * i + j + 1)
                            dve.wait_ge(pv_ready, UNITS * i + H * j + H)
                            if sample:
                                dve.wait_ge(stored[j], 16 * i)
                            dve.tensor_tensor(mix[:, j, GW:2 * GW].rearrange("p (h d) -> p h d", d=DH), op[:, j].rearrange("p (h d) -> p h d", d=DH),
                                              inv[:, j].unsqueeze(2).broadcast_to([P, H, DH]), ALU.mult).then_inc(o_ready, 1)

                        for n in range(UNITS):
                            j, h = n // H, n % H
                            dve.wait_ge(s_ready, UNITS * i + n + 1)
                            dve.tensor_reduce(top[:, j, h:h + 1], score[:, n % 2, span], AX_X, ALU.max).then_inc(top_ready, 1)
                            dve.wait_ge(top_ready, UNITS * i + n + 1)
                            if h == 0 and sample:
                                dve.wait_ge(sin_ready, 2 * i + j - 1)
                            dve.tensor_scalar(bias[:, j, h:h + 1], top[:, j, h:h + 1], -DH ** -0.5, nsink[:, h:h + 1], ALU.mult, ALU.min).then_inc(bias_ready, 1)
                            if n:
                                evac(n - 1)
                            if h == 5:
                                glo.dve(dve, i, j, not sample)
                            if h - 1 in TURN and not (last and j == 1):
                                low_queries(dve, *next_step(i, j, h, sample))
                            if n == H:
                                sink_in(0)
                            if n == H + 2:
                                finish(0)
                        evac(UNITS - 1)
                        sink_in(1)
                        finish(1)
                    for r in range(2):
                        low_queries(dve, 0, 0, r, True)
                    tile_pairs(dve, body)


def merge(nc, keep, a, scratch, whi, wlo, hi, lo):
    with ExitStack() as ctx:
        s = Space(nc, ctx, "mrg")
        st = NormStage(s, keep, 1, hi, lo, slots=1)
        mix = s.sb("mix", [P, 2, D])
        mhi = [s.sb(f"mhi{j}", [P, KD, P], F32R) for j in range(2)]
        mlo = [s.sb(f"mlo{j}", [P, KD, P], F32R) for j in range(2)]
        gate = s.sb("gate", [P, 2, D])
        mT = s.ps("mT", [P, KD, P])
        acc = s.ps("acc", [P, 2, 2, HALF])
        x_in = [s.sem(f"x_in{j}") for j in range(2)]
        mix_in = [s.sem(f"mix_in{j}") for j in range(2)]
        x1_out = [s.sem(f"x1_out{j}") for j in range(2)]
        (gate_in, mT_ready, mhi_ready, mlo_ready, acc_ready, gated, x1_ready) = (s.sem(n) for n in (
            "gate_in", "mT_ready", "mhi_ready", "mlo_ready", "acc_ready", "gated", "x1_ready"))
        PAIRS = NT // 2

        def skewed(eng, ahead, main, behind):
            def pair(i, static):
                first, last, second = (static == 0), (static == PAIRS - 1), (static == 1)
                cond = 0 if first else 1
                ahead(i, 1, cond, first)
                main(i, 0, cond, first)
                if not first:
                    behind(i - 1, 1, 0 if second else 1, second)
                if not last:
                    ahead(i + 1, 0, 1, False)
                main(i, 1, cond, first)
                behind(i, 0, cond, first)
            ahead(0, 0, 0, True)
            pair(0, 0)
            pair(1, 1)
            with eng.Fori(2, PAIRS - 1) as i:
                pair(i, None)
            pair(PAIRS - 1, PAIRS - 1)
            behind(PAIRS - 1, 1, 1, False)

        def nothing(i, j, cond, first):
            pass

        with nc.Block() as block:

            @block.sync
            def _(sp):
                for j in range(2):
                    sp.dma_start(mix[:, j], scratch["mix"][j * P:(j + 1) * P, :]).then_inc(mix_in[j], 16)
                    sp.dma_start(st.x[:, j], a["x_prompt"][0, j * P:(j + 1) * P, :]).then_inc(x_in[j], 16)
                for c in range(2):
                    sp.dma_start(gate[:, c], scratch["mod"][c:c + 1, 2 * D:3 * D].broadcast_to([P, D])).then_inc(gate_in, 16)

                def tile(i, j, last):
                    t = 2 * i + j
                    if not last:
                        sp.wait_ge(mT_ready, t + 1)
                        sp.dma_start(mix[:, j], scratch["mix"][tile_rows(t + 2), :]).then_inc(mix_in[j], 16)
                    sp.wait_ge(x1_ready, t + 1)
                    sp.dma_start(scratch["x1"][tile_rows(t), :], st.x[:, j]).then_inc(x1_out[j], 16)
                    if not last:
                        sp.wait_ge(st.xn_ready, t + 1)
                        sp.wait_ge(st.ssq_ready, t + 1)
                        sp.wait_ge(x1_out[j], 16 * i + 16)
                        sp.dma_start(st.x[:, j], a["x_sample"][0, bass.ds((t + 2 - NTP) * P, P), :]).then_inc(x_in[j], 16)
                with sp.Fori(0, PAIRS - 1) as i:
                    for j in range(2):
                        tile(i, j, False)
                for j in range(2):
                    tile(PAIRS - 1, j, True)
                for j in range(2):
                    sp.wait_ge(x1_out[j], 16 * PAIRS)

            @block.scalar
            def _(act):
                def turn(i, j, cond, first):
                    t = 2 * i + j
                    act.wait_ge(mT_ready, t + 1)
                    if not first:
                        act.wait_ge(acc_ready, t - 1)
                    act.activation(mhi[j][:, :, :], mT[:, :, :], ACT.Copy).then_inc(mhi_ready, 1)

                def square(i, j, cond, first):
                    st.act_square(act, i, j, x1_ready, 2 * i + j + 1, first)

                def high(i, j, cond, first):
                    st.act_hi(act, i, j)
                skewed(act, turn, square, high)

            @block.gpsimd
            def _(pool):
                def rstd(i, j, cond, first):
                    st.pool_rstd(pool, i, j)

                def low(i, j, cond, first):
                    st.pool_lo(pool, i, j)
                skewed(pool, nothing, rstd, low)

            @block.vector
            def _(dve):
                def turn(i, j, cond, first):
                    t = 2 * i + j
                    dve.wait_ge(mhi_ready, t + 1)
                    if not first:
                        dve.wait_ge(acc_ready, t - 1)
                    dve.tensor_tensor(mlo[j][:, :, :], mT[:, :, :], hi_view(mhi[j]), ALU.subtract).then_inc(mlo_ready, 1)

                def residual(i, j, cond, first):
                    t = 2 * i + j
                    dve.wait_ge(acc_ready, t + 1)
                    if not first:
                        dve.wait_ge(st.xT_ready, t - 1)
                    dve.tensor_tensor(st.xn[:, j], acc[:, j].rearrange("p a b -> p (a b)"), gate[:, cond], ALU.mult).then_inc(gated, 1)
                    dve.wait_ge(gated, t + 1)
                    dve.wait_ge(x_in[j], 16 * i + 16)
                    dve.tensor_tensor(st.x[:, j], st.x[:, j], st.xn[:, j], ALU.add).then_inc(x1_ready, 1)
                    st.dve_xn(dve, i, j, first)

                def modulate(i, j, cond, first):
                    st.dve_modulate(dve, i, j, cond, first)
                dve.wait_ge(gate_in, 32)
                skewed(dve, turn, residual, modulate)

            @block.tensor
            def _(pe):
                def turn(i, j, cond, first):
                    t = 2 * i + j
                    pe.wait_ge(mix_in[j], 16 * i + 16)
                    if not (first and j == 0):
                        pe.wait_ge(mlo_ready, t)
                    for k in range(KD):
                        mm = pe.transpose(mT[:, k], mix[:, j, k * P:(k + 1) * P], keep["ident"])
                    mm.then_inc(mT_ready, 1)

                def products(i, j, cond, first):
                    t = 2 * i + j
                    pe.wait_ge(mlo_ready, t + 1)
                    if not first:
                        pe.wait_ge(gated, t - 1)
                    for half in range(2):
                        at = slice(half * HALF, (half + 1) * HALF)
                        for k in range(KD):
                            out = acc[:, j, half]
                            pe.matmul(out, mhi[j][:, k], whi[:, k, at], start=(k == 0), stop=False)
                            pe.matmul(out, mhi[j][:, k], wlo[:, k, at], start=False, stop=False)
                            mm = pe.matmul(out, mlo[j][:, k], whi[:, k, at], start=False, stop=(k == KD - 1))
                    mm.then_inc(acc_ready, 1)

                def norm_turn(i, j, cond, first):
                    st.pe_transpose(pe, i, j, first)
                skewed(pe, turn, products, norm_turn)


def feed_forward(nc, a, scratch, room_a, room_b, hi, lo, outs):
    NF = DFF // P
    BLOCKS = ((0, HALF), (HALF, 2 * HALF), (2 * HALF, T))
    NB = len(BLOCKS)
    RING = 5
    with ExitStack() as ctx:
        s = Space(nc, ctx, "ff")
        acc = s.sb("acc", [P, NT, D])
        raw1 = s.sb("raw1", [P, 2, KD, P])
        raw2 = s.sb("raw2", [P, 2, D])
        w1hi, w1lo = ([room_a[:, m + j].rearrange("p (k n) -> p k n", n=P) for j in range(2)] for m in (0, 2))
        w2hi, w2lo = ([room_a[:, m + j] for j in range(2)] for m in (4, 6))
        flat = room_b[:, :, :].rearrange("p k n -> p (k n)")
        uhi, ulo = ([flat[:, (m + j) * T:(m + j + 1) * T] for j in range(2)] for m in (0, 2))
        relu = s.sb("relu", [P, 2, HALF])
        sq = relu
        up = s.ps("up", [P, NB, HALF])
        down = s.ps("down", [P, RING, HALF])
        w1_in = [s.sem(f"w1_in{j}") for j in range(2)]
        w2_in = [s.sem(f"w2_in{j}") for j in range(2)]
        (zeroed, w1hi_ready, w1lo_ready, w2hi_ready, w2lo_ready, up_ready, relu_ready, sq_ready, uhi_ready, ulo_ready,
         down_ready, added, gate_in, gated, out_ready, stored) = (s.sem(n) for n in (
             "zeroed", "w1hi_ready", "w1lo_ready", "w2hi_ready", "w2lo_ready", "up_ready", "relu_ready", "sq_ready",
             "uhi_ready", "ulo_ready", "down_ready", "added", "gate_in", "gated", "out_ready", "stored"))
        w1v = a["w_ff1"][0].rearrange("(k p) n -> p k n", p=P)
        PER = 2 * NT
        gate = [relu[:, :, :].rearrange("p a b -> p (a b)"), raw1[:, 0].rearrange("p k n -> p (k n)")]
        x1 = [raw1[:, 1].rearrange("p k n -> p (k n)"), raw2[:, 0], raw2[:, 1]]
        x1_in = [s.sem(f"x1_in{m}") for m in range(len(x1))]

        def chunks(eng, body):
            with eng.Fori(0, NF // 2) as i:
                for j in range(2):
                    body(i, j)

        def store_tile(sp, t):
            sp.wait_ge(out_ready, t + 1)
            out = outs[0][0, t * P:(t + 1) * P, :] if t < NTP else outs[1][0, (t - NTP) * P:(t - NTP + 1) * P, :]
            sp.dma_start(out, acc[:, t]).then_inc(stored, 16)

        with nc.Block() as block:

            @block.sync
            def _(sp):
                def load(i, j):
                    c = 2 * i + j
                    sp.dma_start(raw1[:, j], w1v[:, :, bass.ds(c * P, P)]).then_inc(w1_in[j], 16)
                    sp.dma_start(raw2[:, j], a["w_ff2"][0, bass.ds(c * P, P), :]).then_inc(w2_in[j], 16)
                for j in range(2):
                    load(0, j)
                with sp.Fori(1, NF // 2) as i:
                    for j in range(2):
                        sp.wait_ge(w1lo_ready, 2 * i + j - 1)
                        sp.wait_ge(w2lo_ready, 2 * i + j - 1)
                        load(i, j)
                sp.wait_ge(ulo_ready, NB * NF)
                sp.wait_ge(w2lo_ready, NF)
                for cond in range(2):
                    sp.dma_start(gate[cond], scratch["mod"][cond:cond + 1, 5 * D:6 * D].broadcast_to([P, D])).then_inc(gate_in, 16)
                for t in range(NT):
                    if t >= len(x1):
                        store_tile(sp, t - len(x1))
                    sp.dma_start(x1[t % len(x1)], scratch["x1"][t * P:(t + 1) * P, :]).then_inc(x1_in[t % len(x1)], 16)
                for t in range(NT - len(x1), NT):
                    store_tile(sp, t)
                sp.wait_ge(stored, 16 * NT)

            @block.scalar
            def _(act):
                def split(i, j, first):
                    c = 2 * i + j
                    act.wait_ge(w1_in[j], 16 * i + 16)
                    if not first:
                        act.wait_ge(up_ready, NB * (c - 1))
                    act.activation(w1hi[j], raw1[:, j], ACT.Copy).then_inc(w1hi_ready, 1)
                    act.wait_ge(w2_in[j], 16 * i + 16)
                    if not first:
                        act.wait_ge(down_ready, PER * (c - 1))
                    act.activation(w2hi[j], raw2[:, j], ACT.Copy).then_inc(w2hi_ready, 1)

                def hidden(i, j, first):
                    c = 2 * i + j
                    for b, (t0, t1) in enumerate(BLOCKS):
                        n = NB * c + b
                        m = (NB * j + b) % 2
                        w = t1 - t0
                        act.wait_ge(up_ready, n + 1)
                        if not (first and NB * j + b < 2):
                            act.wait_ge(ulo_ready, n - 1)
                        act.activation(relu[:, m, 0:w], up[:, b, 0:w], ACT.Relu).then_inc(relu_ready, 1)
                        act.wait_ge(sq_ready, n + 1)
                        if not first:
                            act.wait_ge(down_ready, PER * (c - 1))
                        act.activation(uhi[j][:, t0:t1], sq[:, m, 0:w], ACT.Copy).then_inc(uhi_ready, 1)
                def body(i, first):
                    hidden(i, 1, first)
                    split(i + 1, 0, False)
                    hidden(i + 1, 0, False)
                    split(i + 1, 1, False)
                for j in range(2):
                    split(0, j, True)
                hidden(0, 0, True)
                body(0, True)
                with act.Fori(1, NF // 2 - 1) as i:
                    body(i, False)
                hidden(NF // 2 - 1, 1, False)

            @block.gpsimd
            def _(pool):
                def split(i, j):
                    c = 2 * i + j
                    pool.wait_ge(w1hi_ready, c + 1)
                    pool.tensor_tensor(w1lo[j], raw1[:, j], w1hi[j].bitcast(F32), ALU.subtract).then_inc(w1lo_ready, 1)
                    pool.wait_ge(w2hi_ready, c + 1)
                    pool.tensor_tensor(w2lo[j], raw2[:, j], w2hi[j].bitcast(F32), ALU.subtract).then_inc(w2lo_ready, 1)

                def hidden(i, j):
                    c = 2 * i + j
                    for b, (t0, t1) in enumerate(BLOCKS):
                        pool.wait_ge(uhi_ready, NB * c + b + 1)
                        pool.tensor_tensor(ulo[j][:, t0:t1], sq[:, (NB * j + b) % 2, 0:t1 - t0], uhi[j][:, t0:t1].bitcast(F32),
                                           ALU.subtract).then_inc(ulo_ready, 1)
                for j in range(2):
                    split(0, j)
                hidden(0, 0)
                with pool.Fori(0, NF // 2 - 1) as i:
                    hidden(i, 1)
                    split(i + 1, 0)
                    hidden(i + 1, 0)
                    split(i + 1, 1)
                hidden(NF // 2 - 1, 1)
                pool.wait_ge(gate_in, 32)
                for t in range(NT):
                    pool.wait_ge(x1_in[t % len(x1)], 16 * (t // len(x1) + 1))
                    pool.wait_ge(gated, 2 * (t + 1))
                    pool.tensor_tensor(acc[:, t], acc[:, t], x1[t % len(x1)], ALU.add).then_inc(out_ready, 1)

            @block.vector
            def _(dve):
                for t in range(NT):
                    dve.memset(acc[:, t], 0.0).then_inc(zeroed, 1)

                def square(c, b, j, first):
                    t0, t1 = BLOCKS[b]
                    n = NB * c + b
                    m = (NB * j + b) % 2
                    w = t1 - t0
                    dve.wait_ge(relu_ready, n + 1)
                    dve.tensor_tensor(sq[:, m, 0:w], relu[:, m, 0:w], relu[:, m, 0:w], ALU.mult).then_inc(sq_ready, 1)

                def add(c, t, half, first):
                    n = 2 * t + half
                    dve.wait_ge(down_ready, PER * c + n + 1)
                    at = slice(half * HALF, (half + 1) * HALF)
                    if not first:
                        dve.wait_ge(added, PER * (c - 1) + n + 1)
                    dve.tensor_tensor(acc[:, t, at], acc[:, t, at], down[:, n % RING], ALU.add).then_inc(added, 1)

                def body(i, j, first):
                    c = 2 * i + j
                    for t in range(NT):
                        for half in range(2):
                            if t in (0, 2, 4) and half == 0:
                                square(c + 1, t // 2, 1 - j, first and j == 0)
                            add(c, t, half, first and j == 0)
                for b in range(NB):
                    square(0, b, 0, True)
                dve.wait_ge(zeroed, NT)
                for j in range(2):
                    body(0, j, True)
                with dve.Fori(1, NF // 2 - 1) as i:
                    for j in range(2):
                        body(i, j, False)
                body(NF // 2 - 1, 0, False)
                c = NF - 1
                dve.wait_ge(gate_in, 32)
                for t in range(NT):
                    for half in range(2):
                        add(c, t, half, False)
                        at = slice(half * HALF, (half + 1) * HALF)
                        dve.wait_ge(added, PER * c + 2 * t + half + 1)
                        dve.tensor_tensor(acc[:, t, at], acc[:, t, at], gate[0 if t < NTP else 1][:, at], ALU.mult).then_inc(gated, 1)

            @block.tensor
            def _(pe):
                def first_product(c, i, j, first):
                    pe.wait_ge(w1lo_ready, c + 1)
                    for b, (t0, t1) in enumerate(BLOCKS):
                        if not first:
                            pe.wait_ge(relu_ready, NB * (c - 1) + b + 1)
                        out = up[:, b, 0:t1 - t0]
                        for k in range(KD):
                            pe.matmul(out, w1hi[j][:, k, :], hi[:, k, t0:t1], start=(k == 0), stop=False)
                            pe.matmul(out, w1hi[j][:, k, :], lo[:, k, t0:t1], start=False, stop=False)
                            mm = pe.matmul(out, w1lo[j][:, k, :], hi[:, k, t0:t1], start=False, stop=(k == KD - 1))
                        mm.then_inc(up_ready, 1)

                def second_product(c, j, first):
                    pe.wait_ge(w2lo_ready, c + 1)
                    for t in range(NT):
                        if t in (0, 4, 8):
                            pe.wait_ge(ulo_ready, NB * c + t // 4 + 1)
                        for half in range(2):
                            n = 2 * t + half
                            at = slice(half * HALF, (half + 1) * HALF)
                            if not (first and n < RING):
                                pe.wait_ge(added, PER * c + n - RING + 1)
                            out = down[:, n % RING]
                            x_hi, x_lo = (x[j][:, t * P:(t + 1) * P] for x in (uhi, ulo))
                            pe.matmul(out, x_hi, w2hi[j][:, at], start=True, stop=False)
                            pe.matmul(out, x_hi, w2lo[j][:, at], start=False, stop=False)
                            pe.matmul(out, x_lo, w2hi[j][:, at], start=False, stop=True).then_inc(down_ready, 1)

                first_product(0, 0, 0, True)
                first_product(1, 0, 1, False)
                second_product(0, 0, True)
                first_product(2, 1, 0, False)
                second_product(1, 1, False)
                with pe.Fori(1, NF // 2 - 1) as i:
                    first_product(2 * i + 1, i, 1, False)
                    second_product(2 * i, 0, False)
                    first_product(2 * i + 2, i + 1, 0, False)
                    second_product(2 * i + 1, 1, False)
                first_product(NF - 1, NF // 2 - 1, 1, False)
                second_product(NF - 2, 0, False)
                second_product(NF - 1, 1, False)




def build(nc, a, outs):
    scratch = {
        "mod": nc.dram_tensor("mod_rows", (2, 6 * D), F32, kind="Internal").ap(),
        "proj": nc.dram_tensor("proj", (T, DIN), F32, kind="Internal").ap(),
        "qk": nc.dram_tensor("qk", (T, GW + KV * DH), F32, kind="Internal").ap(),
        "o": nc.dram_tensor("gla_out", (2, T, GW), F32, kind="Internal").ap(),
        "mix": nc.dram_tensor("mix", (T, D), F32, kind="Internal").ap(),
        "x1": nc.dram_tensor("x1", (T, D), F32, kind="Internal").ap(),
    }
    with ExitStack() as ctx:
        s = Space(nc, ctx, "keep")
        mats = s.sb("mats", [P, 5 * P + 8])
        keep = {
            "mats": mats,
            "ident": mats[:, 0:P],
            "cum": [mats[:, P * (1 + d):P * (2 + d)] for d in range(2)],
            "causal": [mats[:, P * (3 + d):P * (4 + d)] for d in range(2)],
            "vec": [mats[:, 5 * P + 4 * d:5 * P + 4 * d + 4] for d in range(2)],
            "minus_half": s.sb("minus_half", [P, 16]),
            "eps_d": s.sb("eps_d", [P, 16]),
            "eps_h": s.sb("eps_h", [P, 16]),
            "shift": s.sb("shift", [P, 2, KD, 2]),
            "scale": s.sb("scale", [P, 2, KD, 2]),
        }
        with ExitStack() as inner:
            s1 = Space(nc, inner, "h1")
            hi = s1.sb("hi", [P, KD, T], F32R)
            lo = s1.sb("lo", [P, KD, T], F32R)
            raw = s1.sb("raw", [P, 2, KD, COLS_IN])
            modulate_and_norm(nc, keep, a, raw, hi, lo, scratch)
            project(nc, keep, a, raw, hi, lo, scratch, outs)
        gla(nc, keep, a, scratch, outs)
        with ExitStack() as inner:
            s2 = Space(nc, inner, "h2")
            whi, wlo = s2.sb("whi", [P, KD, D], F32R), s2.sb("wlo", [P, KD, D], F32R)
            attention(nc, keep, a, scratch, whi, wlo)
            hi = s2.sb("hi", [P, KD, T], F32R)
            lo = s2.sb("lo", [P, KD, T], F32R)
            merge(nc, keep, a, scratch, whi, wlo, hi, lo)
            feed_forward(nc, a, scratch, whi, wlo, hi, lo, outs)


INPUTS = ("x_prompt", "x_sample", "c", "cache_k", "cache_v", "state_gla_fwd", "state_gla_bwd", "c_ctx", "w_ada", "b_ada",
          "norm_mix", "norm_ff", "w_in", "w_gk_fwd", "b_gk_fwd", "w_gk_bwd", "b_gk_bwd", "gla_norm", "q_norm", "k_norm",
          "sink", "w_o", "w_ff1", "w_ff2")
OUTPUTS = ((1, TP, D), (1, TS, D), (1, 1, KV, TP, DH), (1, 1, KV, TP, DH), (1, 1, H, DH, DH), (1, 1, H, DH, DH))


def kernel(**inputs):
    import concourse.bacc as bacc
    from concourse.bass_utils import run_bass_kernel_spmd

    nc = bacc.Bacc("TRN2", target_bir_lowering=False, num_devices=1)
    arrays = {name: np.ascontiguousarray(inputs[name]) for name in INPUTS}
    arrays["mats"], arrays["window"], arrays["rope"] = constants()
    args = {n: nc.dram_tensor(f"in_{n}", x.shape, mybir.dt.from_np(x.dtype), kind="ExternalInput").ap()
            for n, x in arrays.items()}
    outs = [nc.dram_tensor(f"out_{i}", shape, F32, kind="ExternalOutput").ap() for i, shape in enumerate(OUTPUTS)]
    build(nc, args, outs)
    r = run_bass_kernel_spmd(nc, [{f"in_{n}": x for n, x in arrays.items()}], core_ids=[0])
    return tuple(r.results[0][f"out_{i}"] for i in range(len(OUTPUTS)))
```
